# Optimizing a Trainium2 kernel written in Bass

```python
import math
import jax, jax.numpy as jnp
from jax import lax
import numpy as np

D_MODEL = 1024
BATCH = 1
SEQ = 1024
DEPTH = 1

CHUNK = 64
Q_BLOCK = 128
EPS = 1e-6

DA_HEADS = 4
DA_HEAD_DIM = 64
DA_V_DIM = 2 * DA_HEAD_DIM
DA_QK = DA_HEADS * 2 * DA_HEAD_DIM
DA_WIDTH = DA_HEADS * DA_V_DIM

GDN_HEADS = 4
GDN_K_DIM = 128
GDN_V_DIM = 128
GDN_QK = GDN_HEADS * GDN_K_DIM
GDN_WIDTH = GDN_HEADS * GDN_V_DIM
CONV_WIDTH = 4

N_BRANCHES = 2
D_IN = 2 * DA_QK + 2 * DA_WIDTH + 2 * GDN_QK + 2 * GDN_WIDTH + 2 * GDN_HEADS + N_BRANCHES * D_MODEL

kernel_name = "hybrid_diffattn_gdn_gated_merge"

def rms_norm(x, w):
    xf = x.astype(jnp.float32)
    y = xf * lax.rsqrt(jnp.mean(xf * xf, axis=-1, keepdims=True) + EPS)
    return (y * w.astype(jnp.float32)).astype(x.dtype)

def l2_norm(x):
    return x * lax.rsqrt(jnp.sum(x * x, axis=-1, keepdims=True) + EPS)

def lambda_init_for(layer):
    return 0.8 - 0.6 * math.exp(-0.3 * layer)

def diff_attention(q, k, v, q_gain, k_gain, lam_qk, out_gain, lambda_init):
    B, S, _ = q.shape
    nb = S // Q_BLOCK
    q = rms_norm(q.reshape(B, S, DA_HEADS, 2, DA_HEAD_DIM), q_gain)
    k = rms_norm(k.reshape(B, S, DA_HEADS, 2, DA_HEAD_DIM), k_gain)
    lam_f = lam_qk.astype(jnp.float32)
    lam = (jnp.exp(jnp.sum(lam_f[0] * lam_f[1])) - jnp.exp(jnp.sum(lam_f[2] * lam_f[3]))
           + lambda_init)
    qb = q.reshape(B, nb, Q_BLOCK, DA_HEADS, 2, DA_HEAD_DIM).transpose(1, 0, 3, 4, 2, 5)
    kf = k.transpose(0, 2, 3, 1, 4).astype(jnp.float32)
    vf = v.reshape(B, S, DA_HEADS, DA_V_DIM).transpose(0, 2, 1, 3).astype(jnp.float32)
    key_chunk = jnp.arange(S) // CHUNK
    scale = DA_HEAD_DIM ** -0.5

    def block(args):
        q_blk, blk = args
        q_chunk = (blk * Q_BLOCK + jnp.arange(Q_BLOCK)) // CHUNK
        mask = key_chunk[None, :] <= q_chunk[:, None]
        s = jnp.einsum('bhmqd,bhmkd->bhmqk', q_blk.astype(jnp.float32), kf) * scale
        p = jax.nn.softmax(jnp.where(mask, s, -jnp.inf), axis=-1)
        p = p[:, :, 0] - lam * p[:, :, 1]
        return jnp.einsum('bhqk,bhkd->bhqd', p, vf)

    o = lax.map(block, (qb, jnp.arange(nb)))
    o = o.transpose(1, 0, 3, 2, 4).reshape(B, S, DA_HEADS, DA_V_DIM)
    o = rms_norm(o, out_gain) * (1.0 - lambda_init)
    return o.reshape(B, S, DA_WIDTH).astype(v.dtype)

def short_conv(x, w):
    C = x.shape[-1]
    y = lax.conv_general_dilated(x, w[:, None, :].astype(x.dtype), window_strides=(1,),
                                 padding=[(CONV_WIDTH - 1, 0)],
                                 dimension_numbers=('NWC', 'WIO', 'NWC'),
                                 feature_group_count=C)
    return jax.nn.silu(y)

def gated_delta_rule(q, k, v, g, beta):
    B, H, S, dk = q.shape
    dv = v.shape[-1]
    n = S // CHUNK
    q = q * dk ** -0.5

    def rs(t):
        return t.reshape(B, H, n, CHUNK, *t.shape[3:])

    q, k, v, g, beta = rs(q), rs(k), rs(v), rs(g), rs(beta)
    g = jnp.cumsum(g, axis=-1)
    tri_incl = jnp.tril(jnp.ones((CHUNK, CHUNK), dtype=bool))
    tri_strict = jnp.tril(jnp.ones((CHUNK, CHUNK), dtype=bool), -1)
    gamma = jnp.exp(jnp.where(tri_incl, g[..., :, None] - g[..., None, :], -jnp.inf))
    k_beta = k * beta[..., None]
    v_beta = v * beta[..., None]
    a_strict = jnp.where(tri_strict, jnp.einsum('bhnid,bhnjd->bhnij', k_beta, k) * gamma, 0.0)
    eye = jnp.eye(CHUNK, dtype=q.dtype)
    rhs = jnp.concatenate([v_beta, k_beta * jnp.exp(g)[..., None]], axis=-1)
    sol = lax.linalg.triangular_solve(a_strict + eye, rhs, left_side=True, lower=True)
    u = sol[..., :dv]
    w = sol[..., dv:]
    a_intra = jnp.where(tri_incl, jnp.einsum('bhnid,bhnjd->bhnij', q, k) * gamma, 0.0)
    q_dec = q * jnp.exp(g)[..., None]
    k_tail = k * jnp.exp(g[..., -1:] - g)[..., None]
    g_last = jnp.exp(g[..., -1])

    def nf(t):
        return jnp.moveaxis(t, 2, 0)

    def step(state, inp):
        u_c, w_c, qd_c, kt_c, a_c, gl_c = inp
        v_new = u_c - jnp.einsum('bhcd,bhde->bhce', w_c, state)
        o_c = (jnp.einsum('bhcd,bhde->bhce', qd_c, state)
               + jnp.einsum('bhij,bhje->bhie', a_c, v_new))
        state = state * gl_c[..., None, None] + jnp.einsum('bhcd,bhce->bhde', kt_c, v_new)
        return state, o_c

    s0 = jnp.zeros((B, H, dk, dv), dtype=q.dtype)
    _, o = lax.scan(step, s0, (nf(u), nf(w), nf(q_dec), nf(k_tail), nf(a_intra), nf(g_last)))
    return o.transpose(1, 2, 0, 3, 4).reshape(B, H, S, dv)

def gated_deltanet(q, k, v, a, b, conv_w, a_log, dt_bias):
    B, S, _ = q.shape
    qkv = short_conv(jnp.concatenate([q, k, v], axis=-1), conv_w).astype(jnp.float32)
    q, k, v = jnp.split(qkv, [GDN_QK, 2 * GDN_QK], axis=-1)
    q = l2_norm(q.reshape(B, S, GDN_HEADS, GDN_K_DIM)).transpose(0, 2, 1, 3)
    k = l2_norm(k.reshape(B, S, GDN_HEADS, GDN_K_DIM)).transpose(0, 2, 1, 3)
    v = v.reshape(B, S, GDN_HEADS, GDN_V_DIM).transpose(0, 2, 1, 3)
    af = a.astype(jnp.float32)
    g = -jnp.exp(a_log.astype(jnp.float32)) * jax.nn.softplus(af + dt_bias.astype(jnp.float32))
    beta = jax.nn.sigmoid(b.astype(jnp.float32))
    o = gated_delta_rule(q, k, v, g.transpose(0, 2, 1), beta.transpose(0, 2, 1))
    return o.transpose(0, 2, 1, 3)

def setup_inputs(seed: int = 0) -> dict:
    key = jax.random.key(seed)
    ks = jax.random.split(key, 16)
    f32 = jnp.float32
    x = jax.random.normal(ks[0], (BATCH, SEQ, D_MODEL), f32)
    norm_w = 1.0 + 0.02 * jax.random.normal(ks[1], (DEPTH, D_MODEL), f32)
    w_in = jax.random.normal(ks[2], (DEPTH, D_MODEL, D_IN), f32) * D_MODEL ** -0.5
    da_q_gain = 1.0 + 0.02 * jax.random.normal(ks[3], (DEPTH, DA_HEAD_DIM), f32)
    da_k_gain = 1.0 + 0.02 * jax.random.normal(ks[4], (DEPTH, DA_HEAD_DIM), f32)
    da_lambda = 0.1 * jax.random.normal(ks[5], (DEPTH, 4, DA_HEAD_DIM), f32)
    da_out_gain = 1.0 + 0.02 * jax.random.normal(ks[6], (DEPTH, DA_V_DIM), f32)
    gdn_conv_w = jax.random.normal(ks[7], (DEPTH, CONV_WIDTH, 2 * GDN_QK + GDN_WIDTH), f32) * CONV_WIDTH ** -0.5
    gdn_a_log = jnp.log(jax.random.uniform(ks[8], (DEPTH, GDN_HEADS), f32, 1.0, 16.0))
    dt = jnp.exp(jax.random.uniform(ks[9], (DEPTH, GDN_HEADS), f32, math.log(1e-3), math.log(1e-1)))
    gdn_dt_bias = dt + jnp.log(-jnp.expm1(-dt))
    gdn_norm_w = 1.0 + 0.02 * jax.random.normal(ks[10], (DEPTH, GDN_V_DIM), f32)
    w_up_da = jax.random.normal(ks[11], (DEPTH, DA_WIDTH, D_MODEL), f32) * DA_WIDTH ** -0.5
    w_up_gdn = jax.random.normal(ks[12], (DEPTH, GDN_WIDTH, D_MODEL), f32) * GDN_WIDTH ** -0.5
    w_out = jax.random.normal(ks[13], (DEPTH, D_MODEL, D_MODEL), f32) * D_MODEL ** -0.5
    return {"x": x, "norm_w": norm_w, "w_in": w_in, "da_q_gain": da_q_gain,
            "da_k_gain": da_k_gain, "da_lambda": da_lambda, "da_out_gain": da_out_gain,
            "gdn_conv_w": gdn_conv_w, "gdn_a_log": gdn_a_log, "gdn_dt_bias": gdn_dt_bias,
            "gdn_norm_w": gdn_norm_w, "w_up_da": w_up_da, "w_up_gdn": w_up_gdn, "w_out": w_out}

def reference(x, norm_w, w_in, da_q_gain, da_k_gain, da_lambda, da_out_gain,
              gdn_conv_w, gdn_a_log, gdn_dt_bias, gdn_norm_w, w_up_da, w_up_gdn, w_out):
    B, S, _ = x.shape
    sizes = [DA_QK, DA_QK, DA_WIDTH, DA_WIDTH, GDN_QK, GDN_QK, GDN_WIDTH, GDN_WIDTH,
             GDN_HEADS, GDN_HEADS, N_BRANCHES * D_MODEL]
    split_points = [int(s) for s in np.cumsum(sizes)[:-1]]
    for l in range(DEPTH):
        lambda_init = lambda_init_for(l)
        h = rms_norm(x, norm_w[l])
        proj = jnp.einsum('bsd,de->bse', h, w_in[l])
        qa, ka, va, za, qb, kb, vb, zb, ab, bb, gate = jnp.split(proj, split_points, axis=-1)
        ya = diff_attention(qa, ka, va, da_q_gain[l], da_k_gain[l], da_lambda[l],
                            da_out_gain[l], lambda_init) * jax.nn.silu(za)
        ob = gated_deltanet(qb, kb, vb, ab, bb, gdn_conv_w[l], gdn_a_log[l], gdn_dt_bias[l])
        ob = rms_norm(ob, gdn_norm_w[l]).astype(x.dtype)
        yb = ob.reshape(B, S, GDN_WIDTH) * jax.nn.silu(zb)
        gates = jax.nn.sigmoid(gate.reshape(B, S, N_BRANCHES, D_MODEL))
        merged = (gates[:, :, 0] * jnp.einsum('bsw,wd->bsd', ya, w_up_da[l])
                  + gates[:, :, 1] * jnp.einsum('bsw,wd->bsd', yb, w_up_gdn[l]))
        x = x + jnp.einsum('bsd,de->bse', merged, w_out[l]).astype(x.dtype)
    return x


_drawn_inputs = setup_inputs


def setup_inputs(seed=0):
    import zlib

    import numpy as np

    out = dict(_drawn_inputs(seed))
    spreads = {}
    factors = {'norm_w': 3.653,
     'da_q_gain': 8.0,
     'da_k_gain': 8.0,
     'da_lambda': 3.821,
     'da_out_gain': 8.0,
     'gdn_norm_w': 8.0}
    for name, (base, spread) in spreads.items():
        noise = np.random.default_rng([zlib.crc32(name.encode()), seed]).standard_normal(out[name].shape)
        drawn = base * np.exp(spread * noise) if base else spread * noise
        out[name] = __import__('jax').numpy.asarray(drawn.astype(out[name].dtype))
    for name, factor in factors.items():
        out[name] = (out[name] * factor).astype(out[name].dtype)
    return out
```

```python
import math
from contextlib import ExitStack

import concourse.bass as bass
from concourse import mybir

F32 = mybir.dt.float32
F32R = mybir.dt.float32r
ALU = mybir.AluOpType
ACT = mybir.ActivationFunctionType
AX = mybir.AxisListType

P = 128
SEQ, DM = 1024, 1024
NT = SEQ // P
NK = DM // P
HALF = 512
CHUNK = 64
HEADS = 4
HD = 128
SUB = 64
TAPS = 4
EPS = 1e-6
LAMBDA_INIT = 0.8 - 0.6 * math.exp(-0.3 * 0)
WIDTH = HEADS * HD
COL_QA, COL_KA, COL_VA, COL_ZA = 0, WIDTH, 2 * WIDTH, 3 * WIDTH
COL_QB = 4 * WIDTH
COL_AB = 8 * WIDTH
COL_GATE = COL_AB + 2 * HEADS
LEVELS = 6
NEG = -1.0e30


class Signal:

    def __init__(self, sem, per=1, lead=0):
        self.sem, self.per, self.lead = sem, per, lead

    def at(self, step, k=None):
        return step * self.per + (self.lead + (self.per if k is None else k))


def hybrid_block(nc, x, norm_w, w_in, da_q_gain, da_k_gain, da_lambda, da_out_gain, conv_w,
                 gdn_a_log, gdn_dt_bias, gdn_norm_w, w_up_da, w_up_gdn, w_out, out):
    ctx = ExitStack()
    with ctx:
        def sig(name, per=1, lead=0):
            return Signal(ctx.enter_context(nc.semaphore(name)), per, lead)

        def sb(scope, name, shape, dt=F32):
            return scope.enter_context(nc.sbuf_tensor(name, shape, dt))

        def wait(eng, signal, step=0, k=None):
            eng.wait_ge(signal.sem, signal.at(step, k))

        x_t = x[0].rearrange("(t p) d -> p t d", p=P)
        out_t = out[0].rearrange("(t p) d -> p t d", p=P)
        w_in_k = w_in[0].rearrange("(k p) n -> p k n", p=P)
        w_out_k = w_out[0].rearrange("(k p) n -> p k n", p=P)
        w_up_k = [w[0].rearrange("(k p) n -> p k n", p=P) for w in (w_up_da, w_up_gdn)]

        h_hi = sb(ctx, "h_hi", [P, NK, SEQ], F32R)
        h_lo = sb(ctx, "h_lo", [P, NK, SEQ], F32R)
        w_raw = sb(ctx, "w_raw", [P, 2, HALF])
        w_hi = sb(ctx, "w_hi", [P, 2, HALF], F32R)
        w_lo = sb(ctx, "w_lo", [P, 2, HALF], F32R)
        zv = sb(ctx, "zv", [P, 12, SEQ])
        ident = sb(ctx, "ident", [P, P])
        tri = sb(ctx, "tri", [P, P])
        block_ones = sb(ctx, "block_ones", [P, P])
        vec_rows = sb(ctx, "vec_rows", [64, P])
        vec = sb(ctx, "vec", [P, 64])
        half_conv = sb(ctx, "half_conv", [P, 12, TAPS])
        gain_b = sb(ctx, "gain_b", [P, 1])
        gain_a = sb(ctx, "gain_a", [P, 1])
        gain_qk = sb(ctx, "gain_qk", [P, 1])
        neg_lam = sb(ctx, "neg_lam", [P, 1])
        mask_lhs = sb(ctx, "mask_lhs", [P, P])
        neg_rows = sb(ctx, "neg_rows", [P, CHUNK])
        ones1 = sb(ctx, "ones1", [P, 1])
        token_scalars = sb(ctx, "token_scalars", [P, NT, 8, HEADS])
        masks = sb(ctx, "masks", [P, LEVELS, P])
        a_dt = sb(ctx, "a_dt", [P, 2, HEADS])
        neg_half = sb(ctx, "neg_half", [P, 64])
        PS = ctx.enter_context(nc.psum_tensor("PS", [P, 8, HALF], F32))

        scope = ExitStack()
        x_in = sb(scope, "x_in", [P, 4, DM])
        xs = sb(scope, "xs", [P, 2, DM])
        h32 = sb(scope, "h32", [P, 2, NK, P])
        row_sq = sb(scope, "row_sq", [P, 4])
        row_ms = sb(scope, "row_ms", [P, 4])
        row_r = sb(scope, "row_r", [P, 4])
        sq_junk = sb(scope, "sq_junk", [P, 2, DM])
        lam_rows = sb(scope, "lam_rows", [P, 4, SUB])
        lam_junk = sb(scope, "lam_junk", [P, SUB])
        lam_s = sb(scope, "lam_s", [P, 4])
        scope.close()

        scope_ab = ExitStack()
        conv_out = sb(scope_ab, "conv_out", [P, 12, SEQ])
        scope = ExitStack()
        pre = sb(scope, "pre", [P, TAPS - 1 + SEQ])
        acc = sb(scope, "acc", [P, SEQ])
        th = sb(scope, "th", [P, SEQ])
        cw = sb(scope, "cw", [P, TAPS])
        ab_rows = sb(scope, "ab_rows", [8, SEQ])
        ab = sb(scope, "ab", [P, NT, 8])
        sq8 = sb(scope, "sq8", [P, 2, 8, P])
        log1p = sb(scope, "log1p", [P, 8, NT, HEADS])
        qk_ms = sb(scope, "qk_ms", [P, NT, 8])
        qk_r = sb(scope, "qk_r", [P, NT, 8])
        scope.close()
        scope = ExitStack()
        ct = sb(scope, "ct", [P, 8, P])
        ts = sb(scope, "ts", [P, 8, HEADS])
        gam = sb(scope, "gam", [P, HEADS, P])
        qd = sb(scope, "qd", [P, HEADS, P])
        egl = sb(scope, "egl", [P, 2, HEADS])
        gm = sb(scope, "gm", [P, HEADS, P])
        U = sb(scope, "U", [P, HEADS, P])
        um = sb(scope, "um", [P, 2, HEADS, P])
        V = sb(scope, "V", [P, HEADS, P])
        X = sb(scope, "X", [P, HEADS, P])
        Y = sb(scope, "Y", [P, HEADS, P])
        k_tail = sb(scope, "k_tail", [P, HEADS, P])
        k_exp = sb(scope, "k_exp", [P, HEADS, P])
        v_beta = sb(scope, "v_beta", [P, HEADS, P])
        S = sb(scope, "S", [P, HEADS, P])
        Sg = sb(scope, "Sg", [P, HEADS, P])
        o_ss = sb(scope, "o_ss", [P, HEADS])
        o_ms = sb(scope, "o_ms", [P, HEADS])
        o_r = sb(scope, "o_r", [P, HEADS])
        o_f = sb(scope, "o_f", [P, HEADS])
        scope.close()
        scope_ab.close()
        v_new, on_b, nwT = gam, U, X

        scope = ExitStack()
        qk_raw = sb(scope, "qk_raw", [P, 2, SEQ])
        qk_sq = sb(scope, "qk_sq", [P, 2, SEQ])
        qT = sb(scope, "qT", [P, SEQ])
        kT = sb(scope, "kT", [P, SEQ])
        v_st = sb(scope, "v_st", [P, SEQ])
        k_tok = sb(scope, "k_tok", [P, NT, 2, SUB])
        v_tok = sb(scope, "v_tok", [P, NT, P])
        z_th = sb(scope, "z_th", [P, SEQ])
        prob = sb(scope, "prob", [P, 2, SEQ])
        prob_c = sb(scope, "prob_c", [P, SEQ])
        probT = sb(scope, "probT", [P, NT, P])
        on_a = sb(scope, "on_a", [P, P])
        o_junk = sb(scope, "o_junk", [P, P])
        r_ms = sb(scope, "r_ms", [P, 2, NT, 2])
        r_qk = sb(scope, "r_qk", [P, 2, NT, 2])
        mx = sb(scope, "mx", [P, 2])
        nm = sb(scope, "nm", [P, 2])
        l_sum = sb(scope, "l_sum", [P, 2])
        at_s = sb(scope, "at_s", [P, 12])
        scope.close()

        scope = ExitStack()
        y_hi = sb(scope, "y_hi", [P, 8, SEQ], F32R)
        y_lo = sb(scope, "y_lo", [P, 8, SEQ], F32R)
        gate = sb(scope, "gate", [P, 2, SEQ])
        scope.close()
        scope = ExitStack()
        x_res = sb(scope, "x_res", [P, NT, DM])
        out_sb = sb(scope, "out_sb", [P, NT, DM])
        scope.close()
        m32 = zv[:, 0:8, :]

        vec_loaded = sig("vec_loaded")
        lam_loaded = sig("lam_loaded")
        ab_loaded = sig("ab_loaded")
        x_loaded = [sig(f"x_loaded{b}", 16) for b in range(4)]
        consts_ready = sig("consts_ready")
        masks_ready = sig("masks_ready")
        pows_ready = sig("pows_ready")
        vec_T = sig("vec_T")
        vec_ready = sig("vec_ready")
        lam_sums = sig("lam_sums")
        lam_exp = sig("lam_exp")
        lam_ready = sig("lam_ready")
        row_ms_ready = sig("row_ms_ready", 2)
        row_r_ready = sig("row_r_ready")
        xs_ready = sig("xs_ready", lead=4)
        xT_ready = sig("xT_ready", lead=2)
        h32_ready = sig("h32_ready", lead=2)
        h_hi_ready = sig("h_hi_ready")
        h_lo_ready = sig("h_lo_ready", lead=2)
        w_loaded = [sig(f"w_loaded{b}", 16) for b in range(2)]
        w_hi_ready = sig("w_hi_ready")
        w_lo_ready = sig("w_lo_ready", lead=2)
        w_used = sig("w_used", lead=2)
        proj_half0 = sig("proj_half0")
        proj_out = sig("proj_out", 2, lead=2)
        conv_w_ready = sig("conv_w_ready")
        conv_acc = sig("conv_acc", TAPS, lead=TAPS)
        conv_th = sig("conv_th", lead=1)
        conv_done = sig("conv_done", lead=1)
        z_th_ready = sig("z_th_ready")
        z_silu = sig("z_silu", lead=1)
        ab_T = sig("ab_T")
        a2_dve = sig("a2_dve")
        a2_act = sig("a2_act")
        a2_cum = sig("a2_cum")
        sq8_ready = sig("sq8_ready")
        qk_ss = sig("qk_ss", lead=2)
        qk_pow = sig("qk_pow")
        tile_in = sig("tile_in", 2)
        ts_ready = sig("ts_ready")
        kv_T = sig("kv_T", 2)
        kk_qk = sig("kk_qk", 2, lead=2)
        g_b = sig("g_b", 2, lead=2)
        diff_ready = sig("diff_ready", 4)
        gam_ready = sig("gam_ready")
        eg_ready = sig("eg_ready", 2)
        kv_scaled = sig("kv_scaled", 3)
        gm_ready = sig("gm_ready", 4)
        u_ready = sig("u_ready", 2)
        at_ready = sig("at_ready")
        qd_ready = sig("qd_ready", lead=1)
        um_ready = sig("um_ready", LEVELS)
        v0_ready = sig("v0_ready")
        x0_T = sig("x0_T")
        x0_ready = sig("x0_ready")
        y_mm = sig("y_mm", LEVELS - 1)
        y_ready = sig("y_ready", LEVELS - 1, lead=1)
        x_mm = sig("x_mm", LEVELS - 2)
        v_mm = sig("v_mm", LEVELS - 1, lead=1)
        x_ready = sig("x_ready", LEVELS - 2, lead=1)
        v_ready = sig("v_ready", LEVELS - 1)
        w_mm = sig("w_mm", 2)
        nw_ready = sig("nw_ready", lead=1)
        vnew_mm = sig("vnew_mm", 2)
        vnew_ready = sig("vnew_ready", 2, lead=2)
        o_mm = sig("o_mm", 2, lead=2)
        s_mm = sig("s_mm", 2, lead=2)
        sg_ready = sig("sg_ready", 2, lead=2)
        s_ready = sig("s_ready", 2, lead=1)
        o_ss_ready = sig("o_ss_ready", 4)
        o_ms_ready = sig("o_ms_ready", 3)
        o_pow = sig("o_pow")
        on_ready = sig("on_ready", 2, lead=2)
        on_T = sig("on_T", lead=1)
        yb_ready = sig("yb_ready", lead=1)
        c_sq = sig("c_sq", 2)
        c_q = sig("c_q")
        c_v = sig("c_v")
        c_stat = sig("c_stat")
        c_ms = sig("c_ms", 2)
        c_r = sig("c_r")
        c_kT1 = sig("c_kT1", lead=1)
        c_vT = sig("c_vT")
        c_ktok = sig("c_ktok")
        c_vtok = sig("c_vtok", lead=1)
        c_kT2 = sig("c_kT2")
        c_kT = sig("c_kT")
        c_zth = sig("c_zth")
        c_z = sig("c_z", lead=1)
        c_s = sig("c_s", 2)
        c_mx = sig("c_mx", 3)
        c_p = sig("c_p", 2, lead=2)
        c_coef = sig("c_coef", 4)
        c_pc = sig("c_pc", lead=1)
        c_pT = sig("c_pT", lead=1)
        c_pT_sb = sig("c_pT_sb", lead=1)
        c_o = sig("c_o", lead=1)
        c_oss = sig("c_oss")
        c_oms = sig("c_oms", 2)
        c_opow = sig("c_opow")
        c_on = sig("c_on", lead=1)
        c_oT = sig("c_oT")
        c_y = sig("c_y", lead=1)
        yhi_ready = sig("yhi_ready")
        ylo_ready = sig("ylo_ready")
        d_up = sig("d_up", 2)
        d_gated = sig("d_gated", 6, lead=6)
        m_hi_ready = sig("m_hi_ready")
        m_lo_ready = sig("m_lo_ready")
        x_res_loaded = sig("x_res_loaded", 16)
        out_mm = sig("out_mm", NT - 1)
        out_sum = sig("out_sum", NT, lead=NT)
        stored = sig("stored", 16)

        G_ZB, G_AB, G_FILL, G_QK = 12, 16, 17, 17 + NT
        G_END = G_QK + 2 * HEADS
        PAIR_D = G_END
        PAIR_E = PAIR_D + 3 * NK
        pre_zero = sig("pre_zero")
        passed = sig("passed")

        def settle(eng):
            eng.sem_inc(passed.sem, 1)

        s_zero = sig("s_zero")
        A2_ABS, A2_G, A2_DECAY, A2_QK_MS = 4, 24, 28, 29
        N_CONSTS = 15 + 3 * LEVELS
        TAKE_AT = {2: (0, 0), 3: (0, 1), 7: (1, 0), 8: (1, 1)}
        SPLIT_AT = {1: (0, 0), 3: (0, 1), 6: (1, 0), 8: (1, 1)}
        VEC_ROWS = [(0, conv_w[0].rearrange("w (c p) -> (w c) p", p=P)), (48, norm_w[0].rearrange("(k p) -> k p", p=P)),
                    (56, gdn_norm_w), (57, da_out_gain), (58, da_q_gain), (59, da_k_gain)]
        x_rows = x[0]
        zv_flat = zv[:, :, :].rearrange("p c n -> p (c n)")
        conv_flat = conv_out[:, :, :].rearrange("p c n -> p (c n)")
        half_conv_flat = half_conv[:, :, :].rearrange("p c w -> p (c w)")
        ts_flat = token_scalars[:, :, :, :].rearrange("p t a h -> p (t a h)")

        def bank4(b):
            return PS[:, b, :].rearrange("p (h n) -> p h n", h=HEADS)

        def banks(b):
            return PS[:, b:b + 2, :].rearrange("p a n -> p (a n)")

        o_sq = Y
        block = ctx.enter_context(nc.Block())

        @block.sync
        def _(sp):
            def load_slab(pair, b, src):
                wait(sp, w_lo_ready, pair * 2 + (b - 2))
                settle(sp)
                dst = w_raw[:, b, :]
                if len(src.shape) == 3:
                    dst = dst.rearrange("p (k n) -> p k n", k=src.shape[1])
                sp.dma_start(dst, src).then_inc(w_loaded[b].sem, 16)

            def load_tile(pair, col):
                for b in range(2):
                    load_slab(pair, b, w_in_k[:, 4 * b:4 * b + 4, bass.ds(col, P)])

            with sp.Fori(0, NT // 4) as i:
                for b in range(4):
                    wait(sp, xs_ready, i * 4 + (b - 4))
                    settle(sp)
                    sp.dma_start(x_in[:, b, :], x_rows[bass.ds((i * 4 + b) * P, P), :]).then_inc(x_loaded[b].sem, 16)
            with sp.Fori(0, G_AB) as j:
                load_tile(j, j * P + COL_QB)
            load_tile(G_AB, COL_AB)
            with sp.Fori(0, NT) as t:
                load_tile(t + G_FILL, t * P + COL_VA)
            with sp.Fori(0, HEADS) as h:
                load_tile(h * 2 + G_QK, h * P + COL_QA)
                load_tile(h * 2 + (G_QK + 1), h * P + COL_KA)
            with sp.Fori(0, NK) as n:
                for i in range(2):
                    load_tile(n * 3 + (PAIR_D + i), n * P + (COL_GATE + i * DM))
                for i in range(2):
                    load_slab(n * 3 + (PAIR_D + 2), i, w_up_k[i][:, :, bass.ds(n * P, P)])
            for c in range(2):
                for k in range(NK):
                    load_slab(PAIR_E + c * NK // 2 + k // 2, k % 2, w_out_k[:, k, c * HALF:(c + 1) * HALF])
                    if c == 0 and k == 1:
                        wait(sp, w_used, PAIR_E * 2 - 1)
                        sp.dma_start(x_res[:, :, :], x_t).then_inc(x_res_loaded.sem, 16)
                    if c == 1:
                        wait(sp, out_sum, 0, k + 1)
                        sp.dma_start(out_t[:, k, 0:HALF], out_sb[:, k, 0:HALF]).then_inc(stored.sem, 16)
            for t in range(NT):
                wait(sp, out_sum, 1, t + 1)
                sp.dma_start(out_t[:, t, HALF:DM], out_sb[:, t, HALF:DM]).then_inc(stored.sem, 16)
            wait(sp, stored, 2 * NT - 1)

        @block.gpsimd
        def _(pool):
            made = [0]

            def link(ins):
                made[0] += 1
                ins.then_inc(consts_ready.sem, 1)
                pool.wait_ge(consts_ready.sem, made[0])

            pool.sem_inc(w_lo_ready.sem, w_lo_ready.lead)
            pool.sem_inc(h_lo_ready.sem, h_lo_ready.lead)
            pool.sem_inc(sg_ready.sem, sg_ready.lead)
            link(pool.memset(ident[:, :], 0.0))
            link(pool.affine_select(out=ident[:, :], in_=ident[:, :], compare_op=ALU.not_equal, fill=1.0,
                                    base=0, pattern=[[-1, P]], channel_multiplier=1))
            link(pool.memset(neg_half[:, :], -0.5))
            link(pool.memset(ones1[:, :], 1.0))
            link(pool.memset(tri[:, :], 1.0))
            link(pool.affine_select(out=tri[:, :], in_=tri[:, :], compare_op=ALU.is_ge, fill=0.0,
                                    base=0, pattern=[[1, P]], channel_multiplier=-1))
            link(pool.memset(tri[0:CHUNK, CHUNK:P], 0.0))
            link(pool.memset(block_ones[:, :], 0.0))
            link(pool.memset(block_ones[0:CHUNK, 0:CHUNK], 1.0))
            link(pool.memset(block_ones[CHUNK:P, CHUNK:P], 1.0))
            link(pool.memset(mask_lhs[:, :], 0.0))
            link(pool.memset(mask_lhs[0:1, 0:CHUNK], 1.0))
            link(pool.memset(mask_lhs[CHUNK:CHUNK + 1, 0:CHUNK], 1.0))
            link(pool.memset(neg_rows[:, :], NEG))
            link(pool.memset(masks[:, :, :], 0.0))
            for level in range(LEVELS):
                s = 1 << level
                second = masks[:, level, :].rearrange("p (b two s) -> p b two s", two=2, s=s)[:, :, 1, :]
                nb = P // (2 * s)
                link(pool.memset(second, 1.0))
                link(pool.affine_select(out=second, in_=second, compare_op=ALU.is_ge, fill=0.0,
                                        base=0, pattern=[[-2 * s, nb], [0, s]], channel_multiplier=1))
                link(pool.affine_select(out=second, in_=second, compare_op=ALU.is_ge, fill=0.0,
                                        base=s - 1, pattern=[[2 * s, nb], [0, s]], channel_multiplier=-1))
            assert made[0] == N_CONSTS

            def split_lo(pair, b):
                wait(pool, w_hi_ready, pair * 2 + b)
                pool.tensor_tensor(w_lo[:, b, :], w_raw[:, b, :], w_hi[:, b, :].bitcast(F32), ALU.subtract)\
                    .then_inc(w_lo_ready.sem, 1)

            def row_pow(i, b):
                wait(pool, row_ms_ready, i * 4 + b)
                pool.tensor_tensor(row_r[:, b:b + 1], row_ms[:, b:b + 1], neg_half[:, 0:1], ALU.pow)\
                    .then_inc(row_r_ready.sem, 1)

            def h_rest(i, b):
                wait(pool, h_hi_ready, i * 4 + b)
                cols = bass.ds((i * 4 + b) * P, P)
                settle(pool)
                pool.tensor_tensor(h_lo[:, :, cols], h32[:, b % 2, :, :], h_hi[:, :, cols].bitcast(F32), ALU.subtract)\
                    .then_inc(h_lo_ready.sem, 1)

            with pool.Fori(0, NT // 4) as i:
                row_pow(i, 0)
                row_pow(i, 1)
                for b in range(4):
                    if b < 2:
                        row_pow(i, b + 2)
                    h_rest(i, b)
            for b in range(2):
                split_lo(0, b)

            with pool.Fori(0, G_FILL) as g:
                for b in range(2):
                    split_lo(g + 1, b)

            wait(pool, conv_done, 11)
            with pool.Fori(0, NT // 2) as i:
                for b in range(2):
                    wait(pool, qk_ss, i * 2 + (b - 2))
                    settle(pool)
                    src = conv_out[:, 0:8, bass.ds((i * 2 + b) * P, P)]
                    pool.tensor_tensor(sq8[:, b, :, :], src, src, ALU.mult).then_inc(sq8_ready.sem, 1)
            pool.wait_ge(a2_dve.sem, A2_QK_MS)
            pool.tensor_tensor(qk_r[:, :, :].rearrange("p t c -> p (t c)"), qk_ms[:, :, :].rearrange("p t c -> p (t c)"),
                               neg_half[:, :], ALU.pow).then_inc(qk_pow.sem, 1)

            with pool.Fori(0, NT) as t:
                cols = bass.ds(t * P, P)
                wait(pool, kk_qk, t - 1)
                wait(pool, qd_ready, t - 1)
                settle(pool)
                pool.tensor_copy(ct[:, :, :], conv_out[:, 0:8, cols]).then_inc(tile_in.sem, 1)
                wait(pool, v_mm, t - 1)
                settle(pool)
                pool.tensor_copy(Y[:, :, :], conv_out[:, 8:12, cols]).then_inc(tile_in.sem, 1)
                for level in range(LEVELS):
                    if level == 0:
                        wait(pool, u_ready, t)
                    if level == 2:
                        wait(pool, v0_ready, t)
                    if level >= 3:
                        wait(pool, y_mm, t, level - 2)
                    pool.tensor_tensor(um[:, level % 2, :, :], U[:, :, :],
                                       masks[:, level, :].unsqueeze(1).broadcast_to([P, HEADS, P]), ALU.mult)\
                        .then_inc(um_ready.sem, 1)
                split_lo(t + G_FILL + 1, 0)
                for c in range(2):
                    if c == 0:
                        wait(pool, eg_ready, t)
                    pool.wait_ge(s_ready.sem, t * 2 + (c + 1))
                    pool.tensor_tensor(Sg[:, :, :], S[:, :, :],
                                       egl[:, c, :].unsqueeze(2).broadcast_to([P, HEADS, P]), ALU.mult)\
                        .then_inc(sg_ready.sem, 1)
                wait(pool, o_ms_ready, t)
                pool.tensor_tensor(o_r[:, :], o_ms[:, :], neg_half[:, 0:HEADS], ALU.pow).then_inc(o_pow.sem, 1)
                split_lo(t + G_FILL + 1, 1)

            split_lo(G_QK + 1, 0)
            split_lo(G_QK + 1, 1)
            split_lo(G_QK + 2, 0)
            split_lo(G_QK + 2, 1)

            def head(h, last):
                wait(pool, proj_out, h * 2 + G_QK)
                settle(pool)
                pool.tensor_copy(qT[:, :], qk_raw[:, 0, :]).then_inc(c_q.sem, 1)
                pool.tensor_tensor(qk_sq[:, 0, :], qk_raw[:, 0, :], qk_raw[:, 0, :], ALU.mult).then_inc(c_sq.sem, 1)
                wait(pool, proj_out, h * 2 + (G_QK + 1))
                pool.tensor_tensor(qk_sq[:, 1, :], qk_raw[:, 1, :], qk_raw[:, 1, :], ALU.mult).then_inc(c_sq.sem, 1)
                settle(pool)
                pool.tensor_copy(v_st[:, :], zv_flat[:, bass.ds(h * SEQ + 4 * SEQ, SEQ)]).then_inc(c_v.sem, 1)
                wait(pool, c_ms, h)
                pool.tensor_tensor(r_qk[:].rearrange("p a t s -> p (a t s)"), r_ms[:].rearrange("p a t s -> p (a t s)"),
                                   neg_half[:, 0:4 * NT], ALU.pow).then_inc(c_r.sem, 1)
                for t in range(NT):
                    wait(pool, c_oms, h * NT + t)
                    pool.tensor_tensor(at_s[:, 4:5], at_s[:, 3:4], neg_half[:, 0:1], ALU.pow).then_inc(c_opow.sem, 1)
                    if not last and t in SPLIT_AT:
                        split_lo(h * 2 + (G_QK + 3 + SPLIT_AT[t][0]), SPLIT_AT[t][1])
                if not last:
                    split_lo(h * 2 + (G_QK + 3 + SPLIT_AT[NT][0]), SPLIT_AT[NT][1])

            with pool.Fori(0, HEADS - 1) as h:
                head(h, False)
            head(HEADS - 1, True)

            with pool.Fori(0, 3 * NK) as p:
                for b in range(2):
                    split_lo(p + (PAIR_D + 1), b)
            with pool.Fori(0, NK - 1) as p:
                for b in range(2):
                    split_lo(p + (PAIR_E + 1), b)

        @block.scalar
        def _(act):
            act.sem_inc(proj_out.sem, proj_out.lead)
            act.sem_inc(conv_th.sem, conv_th.lead)
            act.sem_inc(xs_ready.sem, xs_ready.lead)
            act.sem_inc(y_ready.sem, y_ready.lead)
            act.sem_inc(nw_ready.sem, nw_ready.lead)
            act.sem_inc(vnew_ready.sem, vnew_ready.lead)
            act.sem_inc(c_p.sem, c_p.lead)
            act.sem_inc(c_pT_sb.sem, c_pT_sb.lead)
            act.sem_inc(c_vtok.sem, c_vtok.lead)
            for row, src in VEC_ROWS:
                act.dma_start(vec_rows[row:row + src.shape[0], 0:src.shape[1]], src).then_inc(vec_loaded.sem, 16)
            for row, src in ((58, da_q_gain), (59, da_k_gain)):
                act.dma_start(vec_rows[row:row + 1, SUB:P], src).then_inc(vec_loaded.sem, 16)
            act.dma_start(lam_rows[:, :, :].rearrange("p a b -> p (a b)"),
                          da_lambda.rearrange("o a b -> o (a b)").broadcast_to([P, 4 * SUB])).then_inc(lam_loaded.sem, 16)
            act.dma_start(a_dt[:, 0, :], gdn_a_log.broadcast_to([P, HEADS])).then_inc(ab_loaded.sem, 16)
            act.dma_start(a_dt[:, 1, :], gdn_dt_bias.broadcast_to([P, HEADS])).then_inc(ab_loaded.sem, 16)
            act.wait_ge(lam_sums.sem, 2)
            act.activation(lam_s[:, 2:4], lam_s[:, 0:2], ACT.Exp).then_inc(lam_exp.sem, 1)

            def split_hi(pair, b):
                wait(act, w_loaded[b], pair)
                wait(act, w_used, pair * 2 + (b - 2))
                act.activation(w_hi[:, b, :], w_raw[:, b, :], ACT.Copy).then_inc(w_hi_ready.sem, 1)

            def scale_rows(i, b):
                wait(act, row_r_ready, i * 4 + b)
                wait(act, xT_ready, i * 4 + (b - 2))
                act.activation(xs[:, b % 2, :], x_in[:, b, :], ACT.Copy, scale=row_r[:, b:b + 1]).then_inc(xs_ready.sem, 1)

            def round_h(i, b):
                wait(act, h32_ready, i * 4 + b)
                settle(act)
                act.activation(h_hi[:, :, bass.ds((i * 4 + b) * P, P)], h32[:, b % 2, :, :], ACT.Copy)\
                    .then_inc(h_hi_ready.sem, 1)

            with act.Fori(0, NT // 4) as i:
                scale_rows(i, 0)
                scale_rows(i, 1)
                for b in range(4):
                    round_h(i, b)
                    if b < 2:
                        scale_rows(i, b + 2)
            for b in range(2):
                split_hi(0, b)

            def take_bank(dst, g, pair, half, func=ACT.Copy, scale=1.0):
                if half == 0:
                    wait(act, proj_half0, g)
                else:
                    wait(act, w_used, pair * 2 + 1)
                n = dst.shape[0]
                settle(act)
                act.activation(dst, PS[0:n, half, :], func, scale=scale).then_inc(proj_out.sem, 1)

            def conv_tile(g):
                split_hi(g + 1, 0)
                wait(act, conv_acc, g - 1)
                for half in range(2):
                    at = TAPS - 1 + half * HALF
                    take_bank(pre[:, at:at + HALF], g, g, half)
                split_hi(g + 1, 1)
                wait(act, conv_acc, g)
                wait(act, conv_done, g - 1)
                act.activation(th[:, :], acc[:, :], ACT.Tanh).then_inc(conv_th.sem, 1)

            with act.Fori(0, 12) as g:
                conv_tile(g)
            with act.Fori(0, HEADS) as j:
                split_hi(j + 13, 0)
                for half in range(2):
                    take_bank(zv_flat[:, bass.ds(j * SEQ + half * HALF, HALF)], j + G_ZB, j + G_ZB, half)
                split_hi(j + 13, 1)
                wait(act, proj_out, j + G_ZB)
                act.wait_ge(z_silu.sem, j + 1)
                wait(act, conv_done, 11)
                settle(act)
                act.activation(th[:, :], zv_flat[:, bass.ds(j * SEQ, SEQ)], ACT.Tanh, scale=0.5).then_inc(z_th_ready.sem, 1)
            split_hi(G_FILL, 0)
            for half in range(2):
                take_bank(ab_rows[:, half * HALF:(half + 1) * HALF], G_AB, G_AB, half)
            split_hi(G_FILL, 1)

            act.wait_ge(ab_loaded.sem, 32)
            act.activation(a_dt[:, 0, :], a_dt[:, 0, :], ACT.Exp).then_inc(a2_act.sem, 1)
            act.wait_ge(a2_dve.sem, A2_ABS)
            act.activation(log1p[:, 2, :, :], log1p[:, 1, :, :], ACT.Exp, scale=-1.0).then_inc(a2_act.sem, 1)
            act.activation(log1p[:, 7, :, :], ab[:, :, HEADS:2 * HEADS], ACT.Exp, scale=-1.0).then_inc(a2_act.sem, 1)
            act.wait_ge(a2_dve.sem, A2_DECAY)
            act.activation(log1p[:, 0, :, :], token_scalars[:, :, 0, :], ACT.Exp).then_inc(a2_act.sem, 1)
            act.activation(log1p[:, 1, :, :], log1p[:, 3, :, :], ACT.Exp).then_inc(a2_act.sem, 1)

            with act.Fori(0, NT) as t:
                wait(act, diff_ready, t)
                act.activation(gam[:, :, :], gam[:, :, :], ACT.Exp).then_inc(gam_ready.sem, 1)
                wait(act, o_mm, t - 1)
                act.activation(qd[:, :, :], PS[:, 6, :].rearrange("p (h n) -> p h n", h=HEADS), ACT.Exp)\
                    .then_inc(eg_ready.sem, 1)
                wait(act, eg_ready, t, 1)
                wait(act, sg_ready, t - 1)
                act.activation(egl[:, :, :], qd[:, :, CHUNK - 1:P:CHUNK].rearrange("p h c -> p c h"), ACT.Copy)\
                    .then_inc(eg_ready.sem, 1)
                wait(act, x0_T, t)
                act.activation(X[:, :, :], bank4(2), ACT.Copy).then_inc(x0_ready.sem, 1)
                for level in range(1, LEVELS):
                    wait(act, y_mm, t, level)
                    if level == 1:
                        wait(act, kv_T, t)
                    if level > 1:
                        wait(act, v_mm, t, level - 1)
                    act.activation(Y[:, :, :], bank4(2), ACT.Copy).then_inc(y_ready.sem, 1)
                split_hi(t + G_FILL + 1, 0)
                wait(act, w_mm, t)
                act.activation(nwT[:, :, :], bank4(7), ACT.Copy, scale=-1.0).then_inc(nw_ready.sem, 1)
                for c in range(2):
                    rows = slice(c * CHUNK, (c + 1) * CHUNK)
                    wait(act, vnew_mm, t, c + 1)
                    act.activation(v_new[rows, :, :], bank4(5)[rows], ACT.Copy).then_inc(vnew_ready.sem, 1)
                    if c == 0:
                        take_bank(zv_flat[:, bass.ds(t * SEQ + 4 * SEQ, HALF)], t + G_FILL, t + G_FILL, 0)
                wait(act, o_mm, t)
                for h in range(HEADS):
                    if h == 0:
                        wait(act, on_ready, t - 1)
                    act.activation(o_sq[:, h, :], bank4(6)[:, h, :], ACT.Square, accum_out=o_ss[:, h:h + 1])\
                        .then_inc(o_ss_ready.sem, 1)
                take_bank(zv_flat[:, bass.ds(t * SEQ + (4 * SEQ + HALF), HALF)], t + G_FILL, t + G_FILL, 1)
                split_hi(t + G_FILL + 1, 1)

            for s in range(2):
                split_hi(G_QK + s + 1, 0)
                if s == 0:
                    wait(act, yb_ready, NT - 1)
                for half in range(2):
                    take_bank(qk_raw[:, s, half * HALF:(half + 1) * HALF], G_QK + s, G_QK + s, half)
                split_hi(G_QK + s + 1, 1)

            def head(h, last):
                act.wait_ge(c_z.sem, h + 1)
                settle(act)
                act.activation(z_th[:, :], zv_flat[:, bass.ds(h * SEQ + 8 * SEQ, SEQ)], ACT.Tanh, scale=0.5)\
                    .then_inc(c_zth.sem, 1)
                wait(act, c_vT, h)
                wait(act, c_o, h * NT - 1)
                act.activation(v_tok[:, :, :].rearrange("p t d -> p (t d)"), banks(4), ACT.Copy).then_inc(c_vtok.sem, 1)
                wait(act, c_kT2, h)
                act.activation(kT[:, :], banks(2), ACT.Copy, scale=gain_qk[:, 0:1]).then_inc(c_kT.sem, 1)

                def exps(t):
                    n = (t + 1) * P
                    st = h * NT + t
                    wait(act, c_mx, st)
                    wait(act, c_pc, st - 1)
                    for m in range(2):
                        act.activation(prob[:, m, 0:n], banks(2 + 2 * m)[:, 0:n], ACT.Exp, bias=nm[:, m:m + 1],
                                       scale=r_qk[:, 0, t, m:m + 1], accum_out=l_sum[:, m:m + 1]).then_inc(c_p.sem, 1)

                exps(0)
                for t in range(NT):
                    st = h * NT + t
                    n = (t + 1) * P
                    wait(act, c_pT, st)
                    wait(act, c_o, st - 1)
                    act.activation(probT[:, 0:t + 1, :].rearrange("p t d -> p (t d)"), banks(6)[:, 0:n], ACT.Copy)\
                        .then_inc(c_pT_sb.sem, 1)
                    if t + 1 < NT:
                        exps(t + 1)
                    wait(act, c_o, st)
                    act.activation(o_junk[:, :], PS[:, 6, 0:P], ACT.Square, accum_out=at_s[:, 0:1]).then_inc(c_oss.sem, 1)
                    if not last:
                        stream_step(h, t)
                if not last:
                    stream_step(h, NT)

            def stream_step(h, t):
                if t in TAKE_AT:
                    tile, half = TAKE_AT[t]
                    g = h * 2 + (G_QK + 2 + tile)
                    take_bank(qk_raw[:, tile, half * HALF:(half + 1) * HALF], g, g, half)
                if t in SPLIT_AT:
                    tile, b = SPLIT_AT[t]
                    split_hi(h * 2 + (G_QK + 3 + tile), b)

            with act.Fori(0, HEADS - 1) as h:
                head(h, False)
            head(HEADS - 1, True)

            wait(act, c_y, HEADS * NT - 1)
            for i in range(8):
                act.activation(y_hi[:, i, :], zv[:, (i + 8) % 12, :], ACT.Copy).then_inc(yhi_ready.sem, 1)
            with act.Fori(0, NK) as n:
                for i in range(2):
                    pair = n * 3 + (PAIR_D + i)
                    split_hi(pair + 1, 0)
                    wait(act, d_gated, n - 1, 2 + 4 * i)
                    for half in range(2):
                        take_bank(gate[:, i, half * HALF:(half + 1) * HALF], n * 2 + (G_END + i), pair, half,
                                  ACT.Tanh, 0.5)
                    split_hi(pair + 1, 1)
                split_hi(n * 3 + (PAIR_D + 3), 0)
                split_hi(n * 3 + (PAIR_D + 3), 1)

            wait(act, d_gated, NK - 1)
            for k in range(NK):
                act.activation(h_hi[:, k, :], m32[:, k, :], ACT.Copy, scale=0.5).then_inc(m_hi_ready.sem, 1)
                if k in (3, 6):
                    split_hi(PAIR_E + 1, k // 4)
            with act.Fori(1, NK - 1) as p:
                for b in range(2):
                    split_hi(p + (PAIR_E + 1), b)

        @block.tensor
        def _(pe):
            pe.sem_inc(w_used.sem, w_used.lead)
            for s_ in (xT_ready, qk_ss, kk_qk, g_b, v_mm, o_mm, s_mm, on_T, c_kT1, c_pT, c_o):
                pe.sem_inc(s_.sem, s_.lead)
            pe.wait_ge(vec_loaded.sem, 16 * (len(VEC_ROWS) + 2))
            pe.wait_ge(consts_ready.sem, N_CONSTS)
            pe.transpose(PS[:, 7, 0:60], vec_rows[0:60, :], ident[0:60, 0:60]).then_inc(vec_T.sem, 1)

            def transpose_x(i, b):
                wait(pe, xs_ready, i * 4 + b)
                wait(pe, h32_ready, i * 4 + (b - 2))
                for k in range(NK):
                    last = pe.transpose(PS[:, 2 * (b % 2) + k // 4, (k % 4) * P:(k % 4 + 1) * P],
                                        xs[:, b % 2, k * P:(k + 1) * P], ident[:, :])
                last.then_inc(xT_ready.sem, 1)

            with pe.Fori(0, NT // 4) as i:
                for b in range(4):
                    transpose_x(i, b)

            def three_passes(dst, w, lo_w, hi, lo, first, last):
                pe.matmul(dst, w, hi, start=first, stop=False)
                yield None
                pe.matmul(dst, w, lo, start=False, stop=False)
                yield None
                mm = pe.matmul(dst, lo_w, hi, start=False, stop=last)
                yield mm

            def projection(g, pair):
                for kh in range(2):
                    wait(pe, w_lo_ready, pair * 2 + kh)
                    for half in range(2):
                        if kh == 0:
                            wait(pe, proj_out, g - 1, half + 1)
                        for k in range(4):
                            cols = slice(k * P, (k + 1) * P)
                            toks = slice(half * HALF, (half + 1) * HALF)
                            steps = three_passes(PS[:, half, :], w_hi[:, kh, cols], w_lo[:, kh, cols],
                                                 h_hi[:, 4 * kh + k, toks], h_lo[:, 4 * kh + k, toks],
                                                 kh == 0 and k == 0, kh == 1 and k == 3)
                            for mm in steps:
                                if mm is not None and k == 3:
                                    if half == 1:
                                        mm.then_inc(w_used.sem, 1)
                                    elif kh == 1:
                                        mm.then_inc(proj_half0.sem, 1)
                                yield

            def whole(steps):
                for _ in steps:
                    pass

            def take(steps, n):
                for _ in range(n):
                    next(steps, None)

            wait(pe, h_lo_ready, NT - 1)
            with pe.Fori(0, G_FILL) as g:
                whole(projection(g, g))

            pe.wait_ge(proj_out.sem, proj_out.at(G_AB))
            for t in range(NT):
                last = pe.transpose(PS[:, 2, t * 8:(t + 1) * 8], ab_rows[:, t * P:(t + 1) * P], ident[0:8, 0:8])
            last.then_inc(ab_T.sem, 1)
            with pe.Fori(0, NT // 2) as i:
                for b in range(2):
                    wait(pe, sq8_ready, i * 2 + b)
                    for c in range(8):
                        last = pe.matmul(PS[:, 3, bass.ds(i * 16 + (b * 8 + c), 1)], sq8[:, b, c, :], ones1[:, :],
                                         start=True, stop=True)
                    last.then_inc(qk_ss.sem, 1)
            pe.wait_ge(a2_dve.sem, A2_G)
            g_all = token_scalars[:, :, 6, :]
            pe.matmul(PS[:, 4, 0:32], tri[:, :], g_all, start=True, stop=True)
            pe.matmul(PS[:, 4, 32:64], block_ones[:, :], g_all, start=True, stop=True, skip_group_check=True)\
                .then_inc(a2_cum.sem, 1)

            def each_head(fn, signal=None):
                for h in range(HEADS):
                    last = fn(h)
                if signal is not None:
                    last.then_inc(signal.sem, 1)

            with pe.Fori(0, NT) as t:
                fill = projection(t + G_FILL, t + G_FILL)
                wait(pe, tile_in, t, 1)
                each_head(lambda h: pe.transpose(bank4(2)[:, h, :], ct[:, 4 + h, :], ident[:, :]), kv_T)
                wait(pe, tile_in, t, 2)
                each_head(lambda h: pe.transpose(bank4(3)[:, h, :], Y[:, h, :], ident[:, :]), kv_T)
                wait(pe, yb_ready, t - 1)
                each_head(lambda h: pe.matmul(bank4(4)[:, h, :], ct[:, 4 + h, :], ct[:, 4 + h, :], start=True, stop=True), kk_qk)
                each_head(lambda h: pe.matmul(bank4(5)[:, h, :], ct[:, 4 + h, :], ct[:, h, :], start=True, stop=True), kk_qk)
                wait(pe, ts_ready, t)
                each_head(lambda h: pe.matmul(bank4(6)[:, h, :], ts[:, 6, h:h + 1].broadcast_to([P, P]), tri[:, :],
                                              start=True, stop=True), g_b)
                each_head(lambda h: pe.matmul(bank4(7)[:, h, :], ts[:, 5, h:h + 1].broadcast_to([P, P]), ident[:, :],
                                              start=True, stop=True), g_b)
                take(fill, 9)
                wait(pe, v0_ready, t)
                wait(pe, kv_scaled, t, 2)
                each_head(lambda h: pe.transpose(bank4(2)[:, h, :], V[:, h, :], ident[:, :]), x0_T)
                take(fill, 3)
                wait(pe, x0_ready, t)
                wait(pe, kv_scaled, t)
                for level in range(1, LEVELS):
                    if level > 1:
                        wait(pe, x_ready, t, level - 1)
                    wait(pe, um_ready, t, level + 1)
                    each_head(lambda h: pe.matmul(bank4(2)[:, h, :], um[:, level % 2, h, :], X[:, h, :],
                                                  start=True, stop=True), y_mm)
                    take(fill, 3)
                    wait(pe, y_ready, t, level)
                    if level > 1:
                        wait(pe, v_ready, t, level - 1)
                    if level < LEVELS - 1:
                        each_head(lambda h: pe.matmul(bank4(3)[:, h, :], V[:, h, :], Y[:, h, :], start=True, stop=True), x_mm)
                    wait(pe, u_ready, t)
                    each_head(lambda h: pe.matmul(bank4(4)[:, h, :], Y[:, h, :], V[:, h, :], start=True, stop=True), v_mm)
                    take(fill, 1)
                take(fill, 1)
                wait(pe, v_ready, t)
                wait(pe, at_ready, t)
                each_head(lambda h: pe.matmul(bank4(5)[:, h, :], V[:, h, :], v_beta[:, h, :], start=(h == 0), stop=False,
                                              skip_group_check=True), w_mm)
                each_head(lambda h: pe.matmul(bank4(7)[:, h, :], k_exp[:, h, :], V[:, h, :], start=True, stop=True), w_mm)
                take(fill, 3)
                wait(pe, nw_ready, t)
                wait(pe, qd_ready, t)
                for c in range(2):
                    rows = slice(c * CHUNK, (c + 1) * CHUNK)
                    pe.wait_ge(s_ready.sem, t * 2 + (c + 1))
                    each_head(lambda h: pe.matmul(bank4(5)[rows, h, :], nwT[:, h, rows], S[:, h, :], start=False,
                                                  stop=True, skip_group_check=True), vnew_mm)
                    each_head(lambda h: pe.matmul(bank4(6)[rows, h, :], qd[:, h, rows], S[:, h, :], start=(h == 0),
                                                  stop=False, skip_group_check=True))
                    take(fill, 3)
                    wait(pe, vnew_ready, t, c + 1)
                    each_head(lambda h: pe.matmul(bank4(3)[:, h, :], k_tail[rows, h, :], v_new[rows, h, :],
                                                  start=True, stop=True), s_mm)
                    each_head(lambda h: pe.matmul(bank4(6)[rows, h, :], gm[rows, h, rows], v_new[rows, h, :], start=False,
                                                  stop=True, skip_group_check=True), o_mm)
                    take(fill, 3)
                take(fill, 48)
                wait(pe, on_ready, t)
                each_head(lambda h: pe.transpose(bank4(4)[:, h, :], on_b[:, h, :], ident[:, :]), on_T)

            for s in range(2):
                whole(projection(G_QK + s, G_QK + s))

            def head(h, last):
                fill = projection_pair(h) if not last else iter(())
                wait(pe, c_sq, h)
                wait(pe, yb_ready, NT - 1)
                wait(pe, c_y, h * NT - 1)
                wait(pe, c_q, h)
                for s in range(2):
                    for t in range(NT):
                        at = (s * NT + t) * 2
                        mm = pe.matmul(PS[:, 6, at:at + 2], qk_sq[:, s, t * P:(t + 1) * P], block_ones[:, 0:P:SUB],
                                       start=True, stop=True)
                mm.then_inc(c_stat.sem, 1)
                for t in range(NT):
                    mm = pe.transpose(PS[:, 2 + t // 4, (t % 4) * P:(t % 4 + 1) * P], qk_raw[:, 1, t * P:(t + 1) * P], ident[:, :])
                mm.then_inc(c_kT1.sem, 1)
                wait(pe, c_v, h)
                for t in range(NT):
                    mm = pe.transpose(PS[:, 4 + t // 4, (t % 4) * P:(t % 4 + 1) * P], v_st[:, t * P:(t + 1) * P], ident[:, :])
                mm.then_inc(c_vT.sem, 1)
                take(fill, 12)
                wait(pe, c_ktok, h)
                for t in range(NT):
                    mm = pe.transpose(PS[:, 2 + t // 4, (t % 4) * P:(t % 4 + 1) * P],
                                      k_tok[:, t, :, :].rearrange("p s d -> p (s d)"), ident[:, :])
                mm.then_inc(c_kT2.sem, 1)
                wait(pe, c_kT, h)
                wait(pe, c_vtok, h)

                def scores(t):
                    n = (t + 1) * P
                    for m in range(2):
                        rows = slice(m * SUB, (m + 1) * SUB)
                        wait(pe, c_p, h * NT + t - 1, m + 1)
                        for at in range(0, n, HALF):
                            to = min(at + HALF, n)
                            pe.matmul(PS[:, 2 + 2 * m + at // HALF, 0:to - at], qT[rows, t * P:(t + 1) * P],
                                      kT[rows, at:to], start=True, stop=False, skip_group_check=True)
                        end = (n - 1) % HALF + 1
                        pe.matmul(PS[:, 2 + 2 * m + (n - 1) // HALF, end - CHUNK:end], mask_lhs[rows, :],
                                  neg_rows[rows, :], start=False, stop=True, skip_group_check=True)\
                            .then_inc(c_s.sem, 1)

                scores(0)
                for t in range(NT):
                    st = h * NT + t
                    if t + 1 < NT:
                        scores(t + 1)
                    take(fill, 5)
                    wait(pe, c_pc, st)
                    wait(pe, c_y, st - 1)
                    for k in range(t + 1):
                        mm = pe.transpose(PS[:, 6 + k // 4, (k % 4) * P:(k % 4 + 1) * P], prob_c[:, k * P:(k + 1) * P], ident[:, :])
                    mm.then_inc(c_pT.sem, 1)
                    take(fill, 3)
                    wait(pe, c_pT_sb, st)
                    for k in range(t + 1):
                        mm = pe.matmul(PS[:, 6, 0:P], probT[:, k, :], v_tok[:, k, :], start=(k == 0), stop=(k == t))
                    mm.then_inc(c_o.sem, 1)
                    take(fill, 2 if t + 1 < NT else 48)
                    wait(pe, c_on, st)
                    pe.transpose(PS[:, 7, 0:P], on_a[:, :], ident[:, :]).then_inc(c_oT.sem, 1)

            def projection_pair(h):
                for s in range(2):
                    yield from projection(h * 2 + (G_QK + 2 + s), h * 2 + (G_QK + 2 + s))

            with pe.Fori(0, HEADS - 1) as h:
                head(h, False)
            head(HEADS - 1, True)

            wait(pe, c_y, HEADS * NT - 1)
            with pe.Fori(0, NK) as n:
                for i in range(2):
                    whole(projection(n * 2 + (G_END + i), n * 3 + (PAIR_D + i)))
                wait(pe, ylo_ready, 7)
                for i in range(2):
                    wait(pe, w_lo_ready, n * 6 + (PAIR_D * 2 + 4 + i))
                    for half in range(2):
                        wait(pe, d_gated, n - 1, 1 + half + 2 * i)
                        for k in range(4):
                            cols, toks = slice(k * P, (k + 1) * P), slice(half * HALF, (half + 1) * HALF)
                            for mm in three_passes(PS[:, 2 + 2 * i + half, :], w_hi[:, i, cols], w_lo[:, i, cols],
                                                   y_hi[:, 4 * i + k, toks], y_lo[:, 4 * i + k, toks], k == 0, k == 3):
                                if mm is not None and k == 3:
                                    mm.then_inc((d_up if half == 0 else w_used).sem, 1)

            wait(pe, proj_out, G_END + 2 * NK - 1)
            wait(pe, d_gated, NK - 1)
            with pe.Fori(0, 2) as c:
                for k in range(NK):
                    b = k % 2
                    wait(pe, w_lo_ready, c * NK + (PAIR_E * 2 + k))
                    wait(pe, m_lo_ready, k)
                    for t in range(NT):
                        if k == 0:
                            wait(pe, out_sum, c - 1, t + 1)
                        toks = slice(t * P, (t + 1) * P)
                        pe.matmul(PS[:, t, :], h_hi[:, k, toks], w_hi[:, b, :], start=(k == 0), stop=False)
                        pe.matmul(PS[:, t, :], h_hi[:, k, toks], w_lo[:, b, :], start=False, stop=False)
                        mm = pe.matmul(PS[:, t, :], h_lo[:, k, toks], w_hi[:, b, :], start=False, stop=(k == NK - 1))
                        if t == NT - 1:
                            mm.then_inc(w_used.sem, 1)
                        elif k == NK - 1:
                            mm.then_inc(out_mm.sem, 1)

        @block.vector
        def _(dve):
            for s_ in (h32_ready, conv_acc, conv_done, z_silu, qd_ready, x_ready, s_ready, on_ready, yb_ready,
                       c_z, c_pc, c_on, c_y, d_gated, out_sum):
                dve.sem_inc(s_.sem, s_.lead)
            dve.wait_ge(lam_loaded.sem, 16)
            for i in range(2):
                if i:
                    dve.wait_ge(lam_sums.sem, 1)
                dve.tensor_tensor_reduce(lam_junk[:, :], lam_rows[:, 2 * i, :], lam_rows[:, 2 * i + 1, :], 1.0, 0.0,
                                         ALU.mult, ALU.add, lam_s[:, i:i + 1]).then_inc(lam_sums.sem, 1)
            dve.wait_ge(lam_exp.sem, 1)
            dve.tensor_tensor(neg_lam[:, :], lam_s[:, 3:4], lam_s[:, 2:3], ALU.subtract).then_inc(lam_ready.sem, 1)
            dve.wait_ge(lam_ready.sem, 1)
            dve.tensor_scalar(neg_lam[:, :], neg_lam[:, :], -LAMBDA_INIT, None, ALU.add).then_inc(lam_ready.sem, 1)
            dve.wait_ge(vec_T.sem, 1)
            dve.tensor_copy(vec[:, 0:60], PS[:, 7, 0:60]).then_inc(vec_ready.sem, 1)
            dve.wait_ge(vec_ready.sem, 1)
            dve.tensor_scalar(half_conv[:, :, :].rearrange("p c w -> p w c"),
                              vec[:, 0:48].rearrange("p (w c) -> p w c", c=12), 0.5, None, ALU.mult).then_inc(vec_ready.sem, 1)
            dve.tensor_scalar(gain_b[:, :], vec[:, 56:57], 0.5, None, ALU.mult).then_inc(vec_ready.sem, 1)
            dve.tensor_scalar(gain_a[:, :], vec[:, 57:58], 0.5 * (1.0 - LAMBDA_INIT), None, ALU.mult).then_inc(vec_ready.sem, 1)
            dve.scalar_tensor_tensor(out=gain_qk[:, :], in0=vec[:, 58:59], scalar=SUB ** -0.5, in1=vec[:, 59:60],
                                     op0=ALU.mult, op1=ALU.mult).then_inc(vec_ready.sem, 1)

            def row_mean_square(i, b):
                wait(dve, x_loaded[b], i)
                wait(dve, xs_ready, i * 4 + (b - 4))
                dve.tensor_tensor_reduce(sq_junk[:, b % 2, :], x_in[:, b, :], x_in[:, b, :], 1.0, 0.0, ALU.mult, ALU.add,
                                         row_sq[:, b:b + 1]).then_inc(row_ms_ready.sem, 1)
                wait(dve, row_ms_ready, i * 4 + b, 1)
                dve.tensor_scalar(row_ms[:, b:b + 1], row_sq[:, b:b + 1], 1.0 / DM, EPS, ALU.mult, ALU.add)\
                    .then_inc(row_ms_ready.sem, 1)

            def h_columns(i, b):
                wait(dve, xT_ready, i * 4 + b)
                wait(dve, h_lo_ready, i * 4 + (b - 2))
                dve.tensor_tensor(h32[:, b % 2, :, :],
                                  PS[:, 2 * (b % 2):2 * (b % 2) + 2, :].rearrange("p a (k n) -> p (a k) n", n=P),
                                  vec[:, 48:56].unsqueeze(2).broadcast_to([P, NK, P]), ALU.mult).then_inc(h32_ready.sem, 1)

            with dve.Fori(0, NT // 4) as i:
                row_mean_square(i, 0)
                row_mean_square(i, 1)
                for b in range(4):
                    if b < 2:
                        row_mean_square(i, b + 2)
                    h_columns(i, b)

            wait(dve, h_lo_ready, NT - 1)
            dve.memset(pre[:, 0:TAPS - 1], 0.0).then_inc(pre_zero.sem, 1)
            dve.wait_ge(pre_zero.sem, 1)
            dve.wait_ge(vec_ready.sem, 5)
            with dve.Fori(0, 12) as c:
                wait(dve, conv_acc, c - 1)
                dve.tensor_copy(cw[:, :], half_conv_flat[:, bass.ds(c * TAPS, TAPS)]).then_inc(conv_w_ready.sem, 1)
                wait(dve, proj_out, c)
                wait(dve, conv_w_ready, c)
                wait(dve, conv_done, c - 1)
                for tap in range(TAPS):
                    src = pre[:, tap:tap + SEQ]
                    if tap == 0:
                        ins = dve.tensor_scalar(acc[:, :], src, cw[:, 0:1], None, ALU.mult)
                    else:
                        wait(dve, conv_acc, c, tap)
                        ins = dve.scalar_tensor_tensor(out=acc[:, :], in0=src, scalar=cw[:, tap:tap + 1], in1=acc[:, :],
                                                       op0=ALU.mult, op1=ALU.add)
                    ins.then_inc(conv_acc.sem, 1)
                wait(dve, conv_th, c)
                dve.scalar_tensor_tensor(out=conv_flat[:, bass.ds(c * SEQ, SEQ)], in0=th[:, :], scalar=1.0, in1=acc[:, :],
                                         op0=ALU.add, op1=ALU.mult).then_inc(conv_done.sem, 1)
            with dve.Fori(0, HEADS) as j:
                wait(dve, z_th_ready, j)
                z = zv_flat[:, bass.ds(j * SEQ, SEQ)]
                dve.scalar_tensor_tensor(out=z, in0=th[:, :], scalar=1.0, in1=z, op0=ALU.add, op1=ALU.mult)\
                    .then_inc(z_silu.sem, 1)

            done = [0]

            def link(ins):
                done[0] += 1
                ins.then_inc(a2_dve.sem, 1)
                dve.wait_ge(a2_dve.sem, done[0])

            def bc(v):
                return v.unsqueeze(1).broadcast_to([P, NT, HEADS])

            L = [log1p[:, n, :, :] for n in range(8)]
            T = [token_scalars[:, :, n, :] for n in range(8)]
            dve.wait_ge(ab_T.sem, 1)
            link(dve.tensor_copy(ab[:, :, :].rearrange("p t c -> p (t c)"), PS[:, 2, 0:64]))
            dve.wait_ge(a2_act.sem, 1)
            link(dve.tensor_tensor(L[0], ab[:, :, 0:HEADS], bc(a_dt[:, 1, :]), ALU.add))
            link(dve.tensor_scalar(L[1], L[0], -1.0, None, ALU.mult))
            link(dve.tensor_tensor(L[1], L[1], L[0], ALU.max))
            assert done[0] == A2_ABS
            dve.wait_ge(a2_act.sem, 3)
            link(dve.tensor_scalar(L[3], L[2], 2.0, None, ALU.add))
            link(dve.reciprocal(L[3], L[3]))
            link(dve.tensor_tensor(L[3], L[3], L[2], ALU.mult))
            link(dve.tensor_tensor(L[4], L[3], L[3], ALU.mult))
            link(dve.tensor_scalar(L[5], L[4], 2.0 / 15, 2.0 / 13, ALU.mult, ALU.add))
            for n in (11, 9, 7, 5, 3, 1):
                link(dve.tensor_tensor(L[5], L[5], L[4], ALU.mult))
                link(dve.tensor_scalar(L[5], L[5], 2.0 / n, None, ALU.add))
            link(dve.tensor_tensor(L[5], L[5], L[3], ALU.mult))
            link(dve.scalar_tensor_tensor(out=L[5], in0=L[0], scalar=0.0, in1=L[5], op0=ALU.max, op1=ALU.add))
            link(dve.scalar_tensor_tensor(out=T[6], in0=L[5], scalar=-1.0, in1=bc(a_dt[:, 0, :]), op0=ALU.mult, op1=ALU.mult))
            assert done[0] == A2_G, done[0]
            link(dve.tensor_scalar(L[6], L[7], 1.0, None, ALU.add))
            link(dve.reciprocal(T[2], L[6]))
            dve.wait_ge(a2_cum.sem, 1)
            link(dve.tensor_copy(T[0], PS[:, 4, 0:32].rearrange("p (t h) -> p t h", h=HEADS)))
            link(dve.tensor_tensor(L[3], PS[:, 4, 32:64].rearrange("p (t h) -> p t h", h=HEADS), T[0], ALU.subtract))
            assert done[0] == A2_DECAY, done[0]
            wait(dve, qk_ss, NT - 1)
            link(dve.tensor_scalar(qk_ms[:, :, :].rearrange("p t c -> p (t c)"), PS[:, 3, 0:64], EPS, None, ALU.add))
            assert done[0] == A2_QK_MS, done[0]
            dve.wait_ge(qk_pow.sem, 1)
            rq, rk = qk_r[:, :, 0:HEADS], qk_r[:, :, HEADS:2 * HEADS]
            link(dve.tensor_copy(T[1], rk))
            link(dve.tensor_tensor(T[5], T[2], rk, ALU.mult))
            link(dve.tensor_scalar(T[7], rq, float(HD) ** -0.5, None, ALU.mult))
            dve.wait_ge(a2_act.sem, 5)
            link(dve.tensor_tensor(T[3], T[5], L[0], ALU.mult))
            link(dve.tensor_tensor(T[4], L[1], rk, ALU.mult))

            def wide(col):
                return ts[:, col, :].unsqueeze(2).broadcast_to([P, HEADS, P])

            dve.memset(S[:, :, :], 0.0).then_inc(s_zero.sem, 1)
            dve.wait_ge(s_zero.sem, 1)
            with dve.Fori(0, NT) as t:
                wait(dve, g_b, t - 1)
                wait(dve, on_ready, t - 1)
                dve.tensor_copy(ts[:, :, :].rearrange("p a h -> p (a h)"), ts_flat[:, bass.ds(t * 32, 32)])\
                    .then_inc(ts_ready.sem, 1)
                wait(dve, ts_ready, t)
                wait(dve, g_b, t, 1)
                wait(dve, s_mm, t - 1)
                for h in range(HEADS):
                    dve.tensor_scalar(gam[:, h, :], bank4(6)[:, h, :], ts[:, 0, h:h + 1], 0.0, ALU.subtract, ALU.min)\
                        .then_inc(diff_ready.sem, 1)
                wait(dve, kv_T, t)
                dve.tensor_tensor(k_tail[:, :, :], bank4(2), wide(4), ALU.mult).then_inc(kv_scaled.sem, 1)
                dve.tensor_tensor(k_exp[:, :, :], bank4(2), wide(3), ALU.mult).then_inc(kv_scaled.sem, 1)
                dve.tensor_tensor(v_beta[:, :, :], bank4(3), wide(2), ALU.mult).then_inc(kv_scaled.sem, 1)
                wait(dve, gam_ready, t)
                wait(dve, o_mm, t - 1)
                for h in range(HEADS):
                    dve.scalar_tensor_tensor(out=gm[:, h, :], in0=gam[:, h, :], scalar=ts[:, 1, h:h + 1], in1=tri[:, :],
                                             op0=ALU.mult, op1=ALU.mult).then_inc(gm_ready.sem, 1)
                wait(dve, gm_ready, t)
                wait(dve, g_b, t)
                wait(dve, on_T, t - 1)
                dve.tensor_tensor(U[:, :, :], bank4(7), gm[:, :, :], ALU.mult).then_inc(u_ready.sem, 1)
                wait(dve, u_ready, t, 1)
                wait(dve, kk_qk, t)
                dve.tensor_tensor(U[:, :, :], bank4(4), U[:, :, :], ALU.mult).then_inc(u_ready.sem, 1)
                dve.tensor_tensor(gm[:, :, :], bank4(5), gm[:, :, :], ALU.mult).then_inc(at_ready.sem, 1)
                wait(dve, eg_ready, t)
                dve.tensor_tensor(qd[:, :, :], ct[:, 0:4, :], qd[:, :, :], ALU.mult).then_inc(qd_ready.sem, 1)
                wait(dve, um_ready, t, 1)
                dve.tensor_tensor(V[:, :, :], ident[:, :].unsqueeze(1).broadcast_to([P, HEADS, P]), um[:, 0, :, :],
                                  ALU.subtract).then_inc(v0_ready.sem, 1)
                for level in range(1, LEVELS):
                    if level < LEVELS - 1:
                        wait(dve, x_mm, t, level)
                        if level == 1:
                            wait(dve, x0_ready, t)
                        else:
                            wait(dve, x_ready, t, level - 1)
                        dve.tensor_tensor(X[:, :, :], X[:, :, :], bank4(3), ALU.subtract).then_inc(x_ready.sem, 1)
                    wait(dve, v_mm, t, level)
                    if level > 1:
                        wait(dve, v_ready, t, level - 1)
                    dve.tensor_tensor(V[:, :, :], V[:, :, :], bank4(4), ALU.subtract).then_inc(v_ready.sem, 1)
                for c in range(2):
                    wait(dve, s_mm, t, c + 1)
                    wait(dve, sg_ready, t, c + 1)
                    dve.tensor_tensor(S[:, :, :], Sg[:, :, :], bank4(3), ALU.add).then_inc(s_ready.sem, 1)
                wait(dve, o_ss_ready, t)
                dve.tensor_tensor(o_ms[:, :], o_ss[:, :], ts[:, 7, :], ALU.mult).then_inc(o_ms_ready.sem, 1)
                wait(dve, o_ms_ready, t, 1)
                dve.tensor_tensor(o_ms[:, :], o_ms[:, :], ts[:, 7, :], ALU.mult).then_inc(o_ms_ready.sem, 1)
                wait(dve, o_ms_ready, t, 2)
                dve.tensor_scalar(o_ms[:, :], o_ms[:, :], 1.0 / HD, EPS, ALU.mult, ALU.add).then_inc(o_ms_ready.sem, 1)
                wait(dve, o_pow, t)
                dve.tensor_tensor(o_f[:, :], o_r[:, :], ts[:, 7, :], ALU.mult).then_inc(on_ready.sem, 1)
                wait(dve, on_ready, t, 1)
                wait(dve, o_mm, t)
                dve.tensor_tensor(on_b[:, :, :], bank4(6), o_f[:, :].unsqueeze(2).broadcast_to([P, HEADS, P]), ALU.mult)\
                    .then_inc(on_ready.sem, 1)
                wait(dve, on_T, t)
                y = zv[:, 0:4, bass.ds(t * P, P)]
                dve.scalar_tensor_tensor(out=y, in0=bank4(4), scalar=gain_b[:, 0:1], in1=y, op0=ALU.mult, op1=ALU.mult)\
                    .then_inc(yb_ready.sem, 1)

            def head(h):
                wait(dve, c_stat, h)
                wait(dve, c_p, h * NT - 1)
                for s in range(2):
                    dve.tensor_scalar(r_ms[:, s, :, :].rearrange("p t s -> p (t s)"), PS[:, 6, 16 * s:16 * s + 16],
                                      1.0 / SUB, EPS, ALU.mult, ALU.add).then_inc(c_ms.sem, 1)
                wait(dve, c_zth, h)
                z = zv_flat[:, bass.ds(h * SEQ + 8 * SEQ, SEQ)]
                dve.scalar_tensor_tensor(out=z, in0=z_th[:, :], scalar=1.0, in1=z, op0=ALU.add, op1=ALU.mult)\
                    .then_inc(c_z.sem, 1)
                wait(dve, c_r, h)
                wait(dve, c_kT1, h)
                dve.tensor_tensor(k_tok[:, :, :, :], banks(2).rearrange("p (t s d) -> p t s d", s=2, d=SUB),
                                  r_qk[:, 1, :, :].unsqueeze(3).broadcast_to([P, NT, 2, SUB]), ALU.mult)\
                    .then_inc(c_ktok.sem, 1)

                def maxima(t):
                    st = h * NT + t
                    n = (t + 1) * P
                    for m in range(2):
                        wait(dve, c_s, st, m + 1)
                        dve.reduce_max(mx[:, m:m + 1], banks(2 + 2 * m)[:, 0:n], AX.X).then_inc(c_mx.sem, 1)
                    wait(dve, c_mx, st, 2)
                    wait(dve, c_p, st - 1)
                    dve.scalar_tensor_tensor(out=nm[:, :], in0=mx[:, :], scalar=-1.0, in1=r_qk[:, 0, t, :],
                                             op0=ALU.mult, op1=ALU.mult).then_inc(c_mx.sem, 1)

                maxima(0)
                for t in range(NT):
                    st = h * NT + t
                    n = (t + 1) * P
                    wait(dve, c_p, st)
                    wait(dve, c_on, st - 1)
                    dve.reciprocal(at_s[:, 5:7], l_sum[:, :]).then_inc(c_coef.sem, 1)
                    wait(dve, c_coef, st, 1)
                    dve.tensor_tensor(at_s[:, 7:8], at_s[:, 6:7], l_sum[:, 0:1], ALU.mult).then_inc(c_coef.sem, 1)
                    dve.tensor_tensor(at_s[:, 9:10], at_s[:, 5:6], at_s[:, 5:6], ALU.mult).then_inc(c_coef.sem, 1)
                    wait(dve, c_coef, st, 2)
                    dve.tensor_tensor(at_s[:, 8:9], at_s[:, 7:8], neg_lam[:, :], ALU.mult).then_inc(c_coef.sem, 1)
                    wait(dve, c_coef, st, 4)
                    wait(dve, c_pT, st - 1)
                    dve.scalar_tensor_tensor(out=prob_c[:, 0:n], in0=prob[:, 1, 0:n], scalar=at_s[:, 8:9],
                                             in1=prob[:, 0, 0:n], op0=ALU.mult, op1=ALU.add).then_inc(c_pc.sem, 1)
                    if t + 1 < NT:
                        maxima(t + 1)
                    wait(dve, c_oss, st)
                    dve.tensor_scalar(at_s[:, 2:3], at_s[:, 0:1], at_s[:, 9:10], 1.0 / HD, ALU.mult, ALU.mult)\
                        .then_inc(c_oms.sem, 1)
                    wait(dve, c_oms, st, 1)
                    dve.tensor_scalar(at_s[:, 3:4], at_s[:, 2:3], EPS, None, ALU.add).then_inc(c_oms.sem, 1)
                    wait(dve, c_opow, st)
                    dve.tensor_scalar(on_a[:, :], PS[:, 6, 0:P], at_s[:, 4:5], at_s[:, 5:6], ALU.mult, ALU.mult)\
                        .then_inc(c_on.sem, 1)
                    wait(dve, c_oT, st)
                    y = zv_flat[:, bass.ds(h * SEQ + (8 * SEQ + t * P), P)]
                    if t == 0:
                        wait(dve, c_z, h)
                    dve.scalar_tensor_tensor(out=y, in0=PS[:, 7, 0:P], scalar=gain_a[:, 0:1], in1=y,
                                             op0=ALU.mult, op1=ALU.mult).then_inc(c_y.sem, 1)

            with dve.Fori(0, HEADS - 1) as h:
                head(h)
            head(HEADS - 1)

            for i in range(8):
                wait(dve, yhi_ready, i)
                dve.tensor_tensor(y_lo[:, i, :], zv[:, (i + 8) % 12, :], y_hi[:, i, :].bitcast(F32), ALU.subtract)\
                    .then_inc(ylo_ready.sem, 1)
            wait(dve, ylo_ready, 7)
            with dve.Fori(0, NK) as n:
                m_n = [zv_flat[:, bass.ds(n * SEQ + half * HALF, HALF)] for half in range(2)]
                for i in range(2):
                    wait(dve, proj_out, n * 2 + (G_END + i))
                    for half in range(2):
                        if half == 0:
                            wait(dve, d_up, n, i + 1)
                        else:
                            wait(dve, w_used, n * 6 + (PAIR_D * 2 + 4 + i))
                        g = gate[:, i, half * HALF:(half + 1) * HALF]
                        dve.scalar_tensor_tensor(out=m_n[half] if i == 0 else g, in0=g, scalar=1.0,
                                                 in1=PS[:, 2 + 2 * i + half, :], op0=ALU.add, op1=ALU.mult)\
                            .then_inc(d_gated.sem, 1)
                for half in range(2):
                    wait(dve, d_gated, n, 3 + half)
                    dve.tensor_tensor(m_n[half], m_n[half], gate[:, 1, half * HALF:(half + 1) * HALF], ALU.add)\
                        .then_inc(d_gated.sem, 1)

            wait(dve, d_gated, NK - 1)
            for k in range(NK):
                wait(dve, m_hi_ready, k)
                dve.scalar_tensor_tensor(out=h_lo[:, k, :], in0=m32[:, k, :], scalar=0.5, in1=h_hi[:, k, :].bitcast(F32),
                                         op0=ALU.mult, op1=ALU.subtract).then_inc(m_lo_ready.sem, 1)
            dve.wait_ge(x_res_loaded.sem, 16)
            for c in range(2):
                for t in range(NT):
                    if t < NT - 1:
                        wait(dve, out_mm, c, t + 1)
                    else:
                        wait(dve, w_used, PAIR_E * 2 + (c + 1) * NK - 1)
                    cols = slice(c * HALF, (c + 1) * HALF)
                    dve.tensor_tensor(out_sb[:, t, cols], PS[:, t, :], x_res[:, t, cols], ALU.add).then_inc(out_sum.sem, 1)


_INS = ["x", "norm_w", "w_in", "da_q_gain", "da_k_gain", "da_lambda", "da_out_gain", "gdn_conv_w",
        "gdn_a_log", "gdn_dt_bias", "gdn_norm_w", "w_up_da", "w_up_gdn", "w_out"]


def kernel(**inputs):
    import numpy as _np
    import concourse.bacc as _bacc
    from concourse.bass_utils import run_bass_kernel_spmd as _run

    nc = _bacc.Bacc("TRN2", target_bir_lowering=False, num_devices=1, dynamic_dma_scratch_size=1024)
    arrays, args = {}, []
    for name in _INS:
        a = _np.ascontiguousarray(inputs[name])
        arrays[f"in_{name}"] = a
        args.append(nc.dram_tensor(f"in_{name}", a.shape, F32, kind="ExternalInput").ap())
    args.append(nc.dram_tensor("out_0", (1, SEQ, DM), F32, kind="ExternalOutput").ap())
    hybrid_block(nc, *args)
    r = _run(nc, [arrays], core_ids=[0])
    return r.results[0]["out_0"]
```

```python
import math
from contextlib import ExitStack

import concourse.bass as bass
from concourse import mybir

F32 = mybir.dt.float32
F32R = mybir.dt.float32r
ALU = mybir.AluOpType
ACT = mybir.ActivationFunctionType
AX = mybir.AxisListType

P = 128
SEQ, DM = 1024, 1024
NT = SEQ // P
NK = DM // P
HALF = 512
CHUNK = 64
HEADS = 4
HD = 128
SUB = 64
TAPS = 4
EPS = 1e-6
LAMBDA_INIT = 0.8 - 0.6 * math.exp(-0.3 * 0)
WIDTH = HEADS * HD
COL_QA, COL_KA, COL_VA, COL_ZA = 0, WIDTH, 2 * WIDTH, 3 * WIDTH
COL_QB = 4 * WIDTH
COL_AB = 8 * WIDTH
COL_GATE = COL_AB + 2 * HEADS
LEVELS = 6
NEG = -1.0e30


class Signal:

    def __init__(self, sem, per=1, lead=0):
        self.sem, self.per, self.lead = sem, per, lead

    def at(self, step, k=None):
        return step * self.per + (self.lead + (self.per if k is None else k))


def hybrid_block(nc, x, norm_w, w_in, da_q_gain, da_k_gain, da_lambda, da_out_gain, conv_w,
                 gdn_a_log, gdn_dt_bias, gdn_norm_w, w_up_da, w_up_gdn, w_out, out):
    ctx = ExitStack()
    with ctx:
        def sig(name, per=1, lead=0):
            return Signal(ctx.enter_context(nc.semaphore(name)), per, lead)

        def sb(scope, name, shape, dt=F32):
            return scope.enter_context(nc.sbuf_tensor(name, shape, dt))

        def wait(eng, signal, step=0, k=None):
            eng.wait_ge(signal.sem, signal.at(step, k))

        x_t = x[0].rearrange("(t p) d -> p t d", p=P)
        out_t = out[0].rearrange("(t p) d -> p t d", p=P)
        w_in_k = w_in[0].rearrange("(k p) n -> p k n", p=P)
        w_out_k = w_out[0].rearrange("(k p) n -> p k n", p=P)
        w_up_k = [w[0].rearrange("(k p) n -> p k n", p=P) for w in (w_up_da, w_up_gdn)]

        h_hi = sb(ctx, "h_hi", [P, NK, SEQ], F32R)
        h_lo = sb(ctx, "h_lo", [P, NK, SEQ], F32R)
        w_raw = sb(ctx, "w_raw", [P, 2, HALF])
        w_hi = sb(ctx, "w_hi", [P, 2, HALF], F32R)
        w_lo = sb(ctx, "w_lo", [P, 2, HALF], F32R)
        zv = sb(ctx, "zv", [P, 12, SEQ])
        ident = sb(ctx, "ident", [P, P])
        tri = sb(ctx, "tri", [P, P])
        block_ones = sb(ctx, "block_ones", [P, P])
        vec_rows = sb(ctx, "vec_rows", [64, P])
        vec = sb(ctx, "vec", [P, 64])
        half_conv = sb(ctx, "half_conv", [P, 12, TAPS])
        gain_b = sb(ctx, "gain_b", [P, 1])
        gain_a = sb(ctx, "gain_a", [P, 1])
        gain_qk = sb(ctx, "gain_qk", [P, 1])
        neg_lam = sb(ctx, "neg_lam", [P, 1])
        mask_lhs = sb(ctx, "mask_lhs", [P, P])
        neg_rows = sb(ctx, "neg_rows", [P, CHUNK])
        ones1 = sb(ctx, "ones1", [P, 1])
        token_scalars = sb(ctx, "token_scalars", [P, NT, 8, HEADS])
        masks = sb(ctx, "masks", [P, LEVELS, P])
        a_dt = sb(ctx, "a_dt", [P, 2, HEADS])
        neg_half = sb(ctx, "neg_half", [P, 64])
        PS = ctx.enter_context(nc.psum_tensor("PS", [P, 8, HALF], F32))

        scope = ExitStack()
        x_in = sb(scope, "x_in", [P, 4, DM])
        xs = sb(scope, "xs", [P, 2, DM])
        h32 = sb(scope, "h32", [P, 2, NK, P])
        row_sq = sb(scope, "row_sq", [P, 4])
        row_ms = sb(scope, "row_ms", [P, 4])
        row_r = sb(scope, "row_r", [P, 4])
        sq_junk = sb(scope, "sq_junk", [P, 2, DM])
        lam_rows = sb(scope, "lam_rows", [P, 4, SUB])
        lam_junk = sb(scope, "lam_junk", [P, SUB])
        lam_s = sb(scope, "lam_s", [P, 4])
        scope.close()

        scope_ab = ExitStack()
        conv_out = sb(scope_ab, "conv_out", [P, 12, SEQ])
        scope = ExitStack()
        pre = sb(scope, "pre", [P, TAPS - 1 + SEQ])
        acc = sb(scope, "acc", [P, SEQ])
        th = sb(scope, "th", [P, SEQ])
        cw = sb(scope, "cw", [P, TAPS])
        ab_rows = sb(scope, "ab_rows", [8, SEQ])
        ab = sb(scope, "ab", [P, NT, 8])
        sq8 = sb(scope, "sq8", [P, 2, 8, P])
        log1p = sb(scope, "log1p", [P, 8, NT, HEADS])
        qk_ms = sb(scope, "qk_ms", [P, NT, 8])
        qk_r = sb(scope, "qk_r", [P, NT, 8])
        scope.close()
        scope = ExitStack()
        ct = sb(scope, "ct", [P, 8, P])
        ts = sb(scope, "ts", [P, 8, HEADS])
        gam = sb(scope, "gam", [P, HEADS, P])
        qd = sb(scope, "qd", [P, HEADS, P])
        egl = sb(scope, "egl", [P, 2, HEADS])
        gm = sb(scope, "gm", [P, HEADS, P])
        U = sb(scope, "U", [P, HEADS, P])
        um = sb(scope, "um", [P, 2, HEADS, P])
        V = sb(scope, "V", [P, HEADS, P])
        X = sb(scope, "X", [P, HEADS, P])
        Y = sb(scope, "Y", [P, HEADS, P])
        k_tail = sb(scope, "k_tail", [P, HEADS, P])
        k_exp = sb(scope, "k_exp", [P, HEADS, P])
        v_beta = sb(scope, "v_beta", [P, HEADS, P])
        S = sb(scope, "S", [P, HEADS, P])
        Sg = sb(scope, "Sg", [P, HEADS, P])
        vt = sb(scope, "vt", [P, HEADS, P])
        on_b = sb(scope, "on_b", [P, HEADS, P])
        gate_st = sb(scope, "gate_st", [P, SEQ])
        o_scale = sb(scope, "o_scale", [P, HEADS])
        o_ss = sb(scope, "o_ss", [P, HEADS])
        o_ms = sb(scope, "o_ms", [P, HEADS])
        o_r = sb(scope, "o_r", [P, HEADS])
        o_f = sb(scope, "o_f", [P, HEADS])
        scope.close()
        scope_ab.close()
        v_new, nwT = gam, X

        scope_cd = ExitStack()
        gate_b = sb(scope_cd, "gate_b", [P, HEADS, SEQ])
        scope = ExitStack()
        qk_raw = sb(scope, "qk_raw", [P, 2, SEQ])
        qk_sq = sb(scope, "qk_sq", [P, 2, SEQ])
        qT = sb(scope, "qT", [P, SEQ])
        kT = sb(scope, "kT", [P, SEQ])
        v_st = sb(scope, "v_st", [P, SEQ])
        k_tok = sb(scope, "k_tok", [P, NT, 2, SUB])
        v_tok = sb(scope, "v_tok", [P, NT, P])
        z_th = sb(scope, "z_th", [P, SEQ])
        prob = sb(scope, "prob", [P, 2, SEQ])
        prob_c = sb(scope, "prob_c", [P, SEQ])
        probT = sb(scope, "probT", [P, NT, P])
        on_a = sb(scope, "on_a", [P, P])
        o_junk = sb(scope, "o_junk", [P, P])
        r_ms = sb(scope, "r_ms", [P, 2, NT, 2])
        r_qk = sb(scope, "r_qk", [P, 2, NT, 2])
        mx = sb(scope, "mx", [P, 2])
        nm = sb(scope, "nm", [P, 2])
        l_sum = sb(scope, "l_sum", [P, 2])
        at_s = sb(scope, "at_s", [P, 12])
        scope.close()

        scope = ExitStack()
        y_hi = sb(scope, "y_hi", [P, 8, SEQ], F32R)
        y_lo = sb(scope, "y_lo", [P, 8, SEQ], F32R)
        gate_a = sb(scope, "gate_a", [P, 2, SEQ])
        scope.close()
        scope_cd.close()
        scope = ExitStack()
        x_res = sb(scope, "x_res", [P, NT, DM])
        out_sb = sb(scope, "out_sb", [P, NT, DM])
        scope.close()
        m32 = zv[:, 0:8, :]

        vec_loaded = sig("vec_loaded")
        lam_loaded = sig("lam_loaded")
        ab_loaded = sig("ab_loaded")
        x_loaded = [sig(f"x_loaded{b}", 16) for b in range(4)]
        consts_ready = sig("consts_ready")
        masks_ready = sig("masks_ready")
        pows_ready = sig("pows_ready")
        vec_T = sig("vec_T")
        vec_ready = sig("vec_ready")
        lam_sums = sig("lam_sums")
        lam_exp = sig("lam_exp")
        lam_ready = sig("lam_ready")
        row_ms_ready = sig("row_ms_ready", 2)
        row_r_ready = sig("row_r_ready")
        xs_ready = sig("xs_ready", lead=4)
        xT_ready = sig("xT_ready", lead=2)
        h32_ready = sig("h32_ready", lead=2)
        h_hi_ready = sig("h_hi_ready")
        h_lo_ready = sig("h_lo_ready", lead=2)
        w_loaded = [sig(f"w_loaded{b}", 16) for b in range(2)]
        w_hi_ready = sig("w_hi_ready")
        w_lo_ready = sig("w_lo_ready", lead=2)
        w_used = sig("w_used", lead=2)
        proj_half0 = sig("proj_half0")
        proj_out = sig("proj_out", 2, lead=2)
        conv_w_ready = sig("conv_w_ready")
        conv_acc = sig("conv_acc", TAPS, lead=TAPS)
        conv_th = sig("conv_th", lead=1)
        conv_done = sig("conv_done", lead=1)
        z_th_ready = sig("z_th_ready")
        z_silu = sig("z_silu", lead=1)
        ab_T = sig("ab_T")
        a2_dve = sig("a2_dve")
        a2_act = sig("a2_act")
        a2_cum = sig("a2_cum")
        sq8_ready = sig("sq8_ready")
        qk_ss = sig("qk_ss", lead=2)
        qk_pow = sig("qk_pow")
        tile_in = sig("tile_in", 2)
        o_scale_ready = sig("o_scale_ready")
        gate_stored = sig("gate_stored", 16, lead=16)
        gate_loaded = [sig(f"gate_loaded{b}", 16) for b in range(2)]
        ts_ready = sig("ts_ready")
        kv_T = sig("kv_T", 2)
        kk_qk = sig("kk_qk", 2, lead=2)
        g_b = sig("g_b", 2, lead=2)
        diff_ready = sig("diff_ready", 4)
        gam_ready = sig("gam_ready")
        eg_ready = sig("eg_ready", 2)
        kv_scaled = sig("kv_scaled", 3)
        gm_ready = sig("gm_ready", 4)
        u_ready = sig("u_ready", 2)
        at_ready = sig("at_ready")
        qd_ready = sig("qd_ready", lead=1)
        um_ready = sig("um_ready", LEVELS)
        v0_ready = sig("v0_ready")
        x0_T = sig("x0_T")
        x0_ready = sig("x0_ready")
        y_mm = sig("y_mm", LEVELS - 1)
        y_ready = sig("y_ready", LEVELS - 1, lead=1)
        x_mm = sig("x_mm", LEVELS - 2)
        v_mm = sig("v_mm", LEVELS - 1, lead=1)
        x_ready = sig("x_ready", LEVELS - 2, lead=1)
        v_ready = sig("v_ready", LEVELS - 1)
        w_mm = sig("w_mm", 2)
        nw_ready = sig("nw_ready", lead=1)
        vnew_mm = sig("vnew_mm", 2)
        vnew_ready = sig("vnew_ready", 2, lead=2)
        o_mm = sig("o_mm", 2, lead=2)
        s_mm = sig("s_mm", 2, lead=2)
        sg_ready = sig("sg_ready", 2, lead=2)
        s_ready = sig("s_ready", 2, lead=1)
        o_ss_ready = sig("o_ss_ready", 4)
        o_ms_ready = sig("o_ms_ready", 3)
        o_pow = sig("o_pow")
        on_ready = sig("on_ready", 2, lead=2)
        on_T = sig("on_T", lead=1)
        yb_ready = sig("yb_ready", lead=1)
        c_sq = sig("c_sq", 2)
        c_q = sig("c_q")
        c_v = sig("c_v")
        c_stat = sig("c_stat", 2, lead=2)
        c_ms = sig("c_ms", 2)
        c_r = sig("c_r", 2)
        c_kT1 = sig("c_kT1", lead=1)
        c_vT = sig("c_vT")
        c_ktok = sig("c_ktok")
        c_vtok = sig("c_vtok", lead=1)
        c_kT2 = sig("c_kT2")
        c_kT = sig("c_kT")
        c_zth = sig("c_zth")
        c_z = sig("c_z", lead=1)
        c_s = sig("c_s", 2)
        c_mx = sig("c_mx", 3)
        c_p = sig("c_p", 2, lead=2)
        c_coef = sig("c_coef", 4)
        c_pc = sig("c_pc", lead=1)
        c_pT = sig("c_pT", lead=1)
        c_pT_sb = sig("c_pT_sb", lead=1)
        c_o = sig("c_o", lead=1)
        c_oss = sig("c_oss")
        c_oms = sig("c_oms", 2)
        c_opow = sig("c_opow")
        c_on = sig("c_on", lead=1)
        c_oT = sig("c_oT")
        c_y = sig("c_y", lead=1)
        yhi_ready = sig("yhi_ready")
        ylo_ready = sig("ylo_ready")
        d_up = sig("d_up", 2)
        d_gated = sig("d_gated", 6, lead=12)
        m_hi_ready = sig("m_hi_ready")
        m_lo_ready = sig("m_lo_ready")
        x_res_loaded = sig("x_res_loaded", 16)
        out_mm = sig("out_mm", NT - 1)
        out_sum = sig("out_sum", NT, lead=NT)
        stored = sig("stored", 16)

        G_ZB, G_AB, G_FILL = 12, 16, 17
        G_QK = G_FILL + 2 * NT
        G_C = G_QK + 2
        G_END = G_C + 4 * (HEADS - 1) + 2
        PAIR_D = G_END
        PAIR_E = PAIR_D + NK
        pre_zero = sig("pre_zero")
        passed = sig("passed")

        def settle(eng):
            eng.sem_inc(passed.sem, 1)

        s_zero = sig("s_zero")
        A2_ABS, A2_G, A2_DECAY, A2_QK_MS = 4, 24, 28, 29
        N_CONSTS = 15 + 3 * LEVELS
        B_FRONT = (8, 22)
        C_START, C_TILE = (20, 12, 8), (6, 5, 5, 3)
        C_START_LAST, C_TILE_LAST = (12, 8, 8), (2, 2, 3, 2)

        def stream_order(tiles, start, tile):
            places, n = [], sum(start[:2])
            places.append(("start", 0, n, n))
            n += start[2]
            places.append(("start", 1, n, n + sum(tile[:2])))
            for t in range(NT):
                places.append(("scores", t, n + sum(tile[:2]), n + sum(tile[:3])))
                n += sum(tile)
                places.append(("output", t, n - tile[3], n + tile[0] if t < NT - 1 else 48 * tiles))
            events = []
            for g in range(tiles):
                events += [(48 * g + 24, 48 * g + 48, ("split", g, 0)), (48 * g + 36, 48 * g + 48, ("take", g, 0)),
                           (48 * g + 48, 48 * g + 60, ("take", g, 1)), (48 * g + 48, 48 * g + 72, ("split", g, 1))]
            order = {}
            for can, need, what in events:
                kind, t, behind, ahead = next(p for p in places if can <= p[3])
                assert need >= behind or need > 48 * tiles, (what, kind, t)
                order.setdefault((kind, t), []).append(what)
            return order

        VEC_ROWS = [(0, conv_w[0].rearrange("w (c p) -> (w c) p", p=P)), (48, norm_w[0].rearrange("(k p) -> k p", p=P)),
                    (56, gdn_norm_w), (57, da_out_gain), (58, da_q_gain), (59, da_k_gain)]
        x_rows = x[0]
        zv_flat = zv[:, :, :].rearrange("p c n -> p (c n)")
        conv_flat = conv_out[:, :, :].rearrange("p c n -> p (c n)")
        half_conv_flat = half_conv[:, :, :].rearrange("p c w -> p (c w)")
        ts_flat = token_scalars[:, :, :, :].rearrange("p t a h -> p (t a h)")

        def bank4(b):
            return PS[:, b, :].rearrange("p (h n) -> p h n", h=HEADS)

        def banks(b):
            return PS[:, b:b + 2, :].rearrange("p a n -> p (a n)")

        h_hi_flat = h_hi[:, :, :].rearrange("p k s -> p (k s)")
        h_lo_flat = h_lo[:, :, :].rearrange("p k s -> p (k s)")
        o_sq = Y
        gate_dram = nc.dram_tensor("gate_dram", (NK * P, SEQ), F32, kind="Internal")
        gate_dram_flat = gate_dram.ap()
        gate_b_flat = gate_b[:, :, :].rearrange("p n s -> p (n s)")
        block = ctx.enter_context(nc.Block())

        @block.sync
        def _(sp):
            def load_slab(pair, b, src):
                wait(sp, w_lo_ready, pair * 2 + (b - 2))
                settle(sp)
                dst = w_raw[:, b, :]
                if len(src.shape) == 3:
                    dst = dst.rearrange("p (k n) -> p k n", k=src.shape[1])
                sp.dma_start(dst, src).then_inc(w_loaded[b].sem, 16)

            def load_tile(pair, col):
                for b in range(2):
                    load_slab(pair, b, w_in_k[:, 4 * b:4 * b + 4, bass.ds(col, P)])

            sp.sem_inc(gate_stored.sem, gate_stored.lead)
            with sp.Fori(0, NT // 4) as i:
                for b in range(4):
                    wait(sp, xs_ready, i * 4 + (b - 4))
                    settle(sp)
                    sp.dma_start(x_in[:, b, :], x_rows[bass.ds((i * 4 + b) * P, P), :]).then_inc(x_loaded[b].sem, 16)
            with sp.Fori(0, G_AB) as j:
                load_tile(j, j * P + COL_QB)
            load_tile(G_AB, COL_AB)

            def store_gate(t):
                wait(sp, proj_out, t * 2 + (G_FILL + 1))
                settle(sp)
                sp.dma_start(gate_dram_flat[bass.ds(t * P, P), :], gate_st[:, :]).then_inc(gate_stored.sem, 16)

            load_tile(G_FILL, COL_VA)
            load_tile(G_FILL + 1, COL_GATE)
            with sp.Fori(1, NT) as t:
                load_tile(t * 2 + G_FILL, t * P + COL_VA)
                store_gate(t - 1)
                load_tile(t * 2 + (G_FILL + 1), t * P + COL_GATE)
            load_tile(G_QK, COL_QA)
            store_gate(NT - 1)
            load_tile(G_QK + 1, COL_KA)
            with sp.Fori(1, HEADS) as h:
                load_tile(h * 4 + (G_C - 4), h * P + COL_QA)
                load_tile(h * 4 + (G_C - 3), h * P + COL_KA)
                for i in range(2):
                    load_tile(h * 4 + (G_C - 2 + i), h * P + (COL_GATE + DM + (HEADS * i - 1) * P))
            for i in range(2):
                load_tile(G_C + 4 * (HEADS - 1) + i, COL_GATE + DM + (HEADS * i + HEADS - 1) * P)
            with sp.Fori(0, NK // 2) as j:
                for b in range(2):
                    for i in range(2):
                        load_slab(j * 2 + (PAIR_D + b), i, w_up_k[i][:, :, bass.ds((j * 2 + b) * P, P)])
                    wait(sp, gate_stored, NT - 1)
                    wait(sp, c_y, HEADS * NT - 1)
                    wait(sp, d_gated, j * 2 + (b - 2))
                    settle(sp)
                    sp.dma_start(gate_a[:, b, :], gate_dram_flat[bass.ds((j * 2 + b) * P, P), :])\
                        .then_inc(gate_loaded[b].sem, 16)
            for c in range(2):
                for k in range(NK):
                    load_slab(PAIR_E + c * NK // 2 + k // 2, k % 2, w_out_k[:, k, c * HALF:(c + 1) * HALF])
                    if c == 0 and k == 1:
                        wait(sp, w_used, PAIR_E * 2 - 1)
                        wait(sp, d_gated, NK - 1)
                        sp.dma_start(x_res[:, :, :], x_t).then_inc(x_res_loaded.sem, 16)
                    if c == 1:
                        wait(sp, out_sum, 0, k + 1)
                        sp.dma_start(out_t[:, k, 0:HALF], out_sb[:, k, 0:HALF]).then_inc(stored.sem, 16)
            for t in range(NT):
                wait(sp, out_sum, 1, t + 1)
                sp.dma_start(out_t[:, t, HALF:DM], out_sb[:, t, HALF:DM]).then_inc(stored.sem, 16)
            wait(sp, stored, 2 * NT - 1)

        @block.gpsimd
        def _(pool):
            made = [0]

            def link(ins):
                made[0] += 1
                ins.then_inc(consts_ready.sem, 1)
                pool.wait_ge(consts_ready.sem, made[0])

            pool.sem_inc(w_lo_ready.sem, w_lo_ready.lead)
            pool.sem_inc(h_lo_ready.sem, h_lo_ready.lead)
            pool.sem_inc(sg_ready.sem, sg_ready.lead)
            link(pool.memset(ident[:, :], 0.0))
            link(pool.affine_select(out=ident[:, :], in_=ident[:, :], compare_op=ALU.not_equal, fill=1.0,
                                    base=0, pattern=[[-1, P]], channel_multiplier=1))
            link(pool.memset(neg_half[:, :], -0.5))
            link(pool.memset(ones1[:, :], 1.0))
            link(pool.memset(tri[:, :], 1.0))
            link(pool.affine_select(out=tri[:, :], in_=tri[:, :], compare_op=ALU.is_ge, fill=0.0,
                                    base=0, pattern=[[1, P]], channel_multiplier=-1))
            link(pool.memset(tri[0:CHUNK, CHUNK:P], 0.0))
            link(pool.memset(block_ones[:, :], 0.0))
            link(pool.memset(block_ones[0:CHUNK, 0:CHUNK], 1.0))
            link(pool.memset(block_ones[CHUNK:P, CHUNK:P], 1.0))
            link(pool.memset(mask_lhs[:, :], 0.0))
            link(pool.memset(mask_lhs[0:1, 0:CHUNK], 1.0))
            link(pool.memset(mask_lhs[CHUNK:CHUNK + 1, 0:CHUNK], 1.0))
            link(pool.memset(neg_rows[:, :], NEG))
            link(pool.memset(masks[:, :, :], 0.0))
            for level in range(LEVELS):
                s = 1 << level
                second = masks[:, level, :].rearrange("p (b two s) -> p b two s", two=2, s=s)[:, :, 1, :]
                nb = P // (2 * s)
                link(pool.memset(second, 1.0))
                link(pool.affine_select(out=second, in_=second, compare_op=ALU.is_ge, fill=0.0,
                                        base=0, pattern=[[-2 * s, nb], [0, s]], channel_multiplier=1))
                link(pool.affine_select(out=second, in_=second, compare_op=ALU.is_ge, fill=0.0,
                                        base=s - 1, pattern=[[2 * s, nb], [0, s]], channel_multiplier=-1))
            assert made[0] == N_CONSTS

            def split_lo(pair, b):
                wait(pool, w_hi_ready, pair * 2 + b)
                pool.tensor_tensor(w_lo[:, b, :], w_raw[:, b, :], w_hi[:, b, :].bitcast(F32), ALU.subtract)\
                    .then_inc(w_lo_ready.sem, 1)

            def row_pow(i, b):
                wait(pool, row_ms_ready, i * 4 + b)
                pool.tensor_tensor(row_r[:, b:b + 1], row_ms[:, b:b + 1], neg_half[:, 0:1], ALU.pow)\
                    .then_inc(row_r_ready.sem, 1)

            def h_rest(i, b):
                wait(pool, h_hi_ready, i * 4 + b)
                cols = bass.ds((i * 4 + b) * P, P)
                settle(pool)
                pool.tensor_tensor(h_lo[:, :, cols], h32[:, b % 2, :, :], h_hi[:, :, cols].bitcast(F32), ALU.subtract)\
                    .then_inc(h_lo_ready.sem, 1)

            with pool.Fori(0, NT // 4) as i:
                row_pow(i, 0)
                row_pow(i, 1)
                for b in range(4):
                    if b < 2:
                        row_pow(i, b + 2)
                    h_rest(i, b)
            for b in range(2):
                split_lo(0, b)

            with pool.Fori(0, G_FILL) as g:
                for b in range(2):
                    split_lo(g + 1, b)

            wait(pool, conv_done, 11)
            with pool.Fori(0, NT // 2) as i:
                for b in range(2):
                    wait(pool, qk_ss, i * 2 + (b - 2))
                    settle(pool)
                    src = conv_out[:, 0:8, bass.ds((i * 2 + b) * P, P)]
                    pool.tensor_tensor(sq8[:, b, :, :], src, src, ALU.mult).then_inc(sq8_ready.sem, 1)
            pool.wait_ge(a2_dve.sem, A2_QK_MS)
            pool.tensor_tensor(qk_r[:, :, :].rearrange("p t c -> p (t c)"), qk_ms[:, :, :].rearrange("p t c -> p (t c)"),
                               neg_half[:, :], ALU.pow).then_inc(qk_pow.sem, 1)

            with pool.Fori(0, NT) as t:
                for level in range(LEVELS):
                    if level == 0:
                        wait(pool, u_ready, t)
                    if level == 2:
                        wait(pool, v0_ready, t)
                    if level >= 3:
                        wait(pool, y_mm, t, level - 2)
                    pool.tensor_tensor(um[:, level % 2, :, :], U[:, :, :],
                                       masks[:, level, :].unsqueeze(1).broadcast_to([P, HEADS, P]), ALU.mult)\
                        .then_inc(um_ready.sem, 1)
                    if level == 2:
                        split_lo(t * 2 + (G_FILL + 1), 0)
                split_lo(t * 2 + (G_FILL + 1), 1)
                for c in range(2):
                    if c == 0:
                        wait(pool, eg_ready, t)
                    pool.wait_ge(s_ready.sem, t * 2 + (c + 1))
                    pool.tensor_tensor(Sg[:, :, :], S[:, :, :],
                                       egl[:, c, :].unsqueeze(2).broadcast_to([P, HEADS, P]), ALU.mult)\
                        .then_inc(sg_ready.sem, 1)
                split_lo(t * 2 + (G_FILL + 2), 0)
                wait(pool, o_ms_ready, t)
                pool.tensor_tensor(o_r[:, :], o_ms[:, :], neg_half[:, 0:HEADS], ALU.pow).then_inc(o_pow.sem, 1)
                split_lo(t * 2 + (G_FILL + 2), 1)

            split_lo(G_QK + 1, 0)
            split_lo(G_QK + 1, 1)
            split_lo(G_QK + 2, 0)
            split_lo(G_QK + 2, 1)

            def head(h, last):
                order = stream_order(2, C_START_LAST, C_TILE_LAST) if last else stream_order(4, C_START, C_TILE)

                def stream(kind, t):
                    for what, g, b in order.get((kind, t), []):
                        if what == "split":
                            split_lo(h * 4 + (G_C + 1 + g), b)

                for s in (1, 0):
                    wait(pool, c_ms, h, 2 - s)
                    pool.tensor_tensor(r_qk[:, s, :, :].rearrange("p t s -> p (t s)"),
                                       r_ms[:, s, :, :].rearrange("p t s -> p (t s)"),
                                       neg_half[:, 0:2 * NT], ALU.pow).then_inc(c_r.sem, 1)
                stream("start", 0)
                stream("start", 1)
                for t in range(NT):
                    stream("scores", t)
                    wait(pool, c_oms, h * NT + t)
                    pool.tensor_tensor(at_s[:, 4:5], at_s[:, 3:4], neg_half[:, 0:1], ALU.pow).then_inc(c_opow.sem, 1)
                    stream("output", t)

            with pool.Fori(0, HEADS - 1) as h:
                head(h, False)
            head(HEADS - 1, True)

            with pool.Fori(0, NK) as p:
                for b in range(2):
                    split_lo(p + (PAIR_D + 1), b)
            with pool.Fori(0, NK - 1) as p:
                for b in range(2):
                    split_lo(p + (PAIR_E + 1), b)

        @block.scalar
        def _(act):
            act.sem_inc(proj_out.sem, proj_out.lead)
            act.sem_inc(conv_th.sem, conv_th.lead)
            act.sem_inc(xs_ready.sem, xs_ready.lead)
            act.sem_inc(y_ready.sem, y_ready.lead)
            act.sem_inc(nw_ready.sem, nw_ready.lead)
            act.sem_inc(vnew_ready.sem, vnew_ready.lead)
            act.sem_inc(c_p.sem, c_p.lead)
            act.sem_inc(c_pT_sb.sem, c_pT_sb.lead)
            act.sem_inc(c_vtok.sem, c_vtok.lead)
            for row, src in VEC_ROWS:
                act.dma_start(vec_rows[row:row + src.shape[0], 0:src.shape[1]], src).then_inc(vec_loaded.sem, 16)
            for row, src in ((58, da_q_gain), (59, da_k_gain)):
                act.dma_start(vec_rows[row:row + 1, SUB:P], src).then_inc(vec_loaded.sem, 16)
            act.dma_start(lam_rows[:, :, :].rearrange("p a b -> p (a b)"),
                          da_lambda.rearrange("o a b -> o (a b)").broadcast_to([P, 4 * SUB])).then_inc(lam_loaded.sem, 16)
            act.dma_start(a_dt[:, 0, :], gdn_a_log.broadcast_to([P, HEADS])).then_inc(ab_loaded.sem, 16)
            act.dma_start(a_dt[:, 1, :], gdn_dt_bias.broadcast_to([P, HEADS])).then_inc(ab_loaded.sem, 16)
            act.wait_ge(lam_sums.sem, 2)
            act.activation(lam_s[:, 2:4], lam_s[:, 0:2], ACT.Exp).then_inc(lam_exp.sem, 1)

            def split_hi(pair, b):
                wait(act, w_loaded[b], pair)
                wait(act, w_used, pair * 2 + (b - 2))
                act.activation(w_hi[:, b, :], w_raw[:, b, :], ACT.Copy).then_inc(w_hi_ready.sem, 1)

            def scale_rows(i, b):
                wait(act, row_r_ready, i * 4 + b)
                wait(act, xT_ready, i * 4 + (b - 2))
                act.activation(xs[:, b % 2, :], x_in[:, b, :], ACT.Copy, scale=row_r[:, b:b + 1]).then_inc(xs_ready.sem, 1)

            def round_h(i, b):
                wait(act, h32_ready, i * 4 + b)
                settle(act)
                act.activation(h_hi[:, :, bass.ds((i * 4 + b) * P, P)], h32[:, b % 2, :, :], ACT.Copy)\
                    .then_inc(h_hi_ready.sem, 1)

            with act.Fori(0, NT // 4) as i:
                scale_rows(i, 0)
                scale_rows(i, 1)
                for b in range(4):
                    round_h(i, b)
                    if b < 2:
                        scale_rows(i, b + 2)
            for b in range(2):
                split_hi(0, b)

            def take_bank(dst, g, pair, half, func=ACT.Copy, scale=1.0):
                if half == 0:
                    wait(act, proj_half0, g)
                else:
                    wait(act, w_used, pair * 2 + 1)
                n = dst.shape[0]
                settle(act)
                act.activation(dst, PS[0:n, half, :], func, scale=scale).then_inc(proj_out.sem, 1)

            def conv_tile(g):
                split_hi(g + 1, 0)
                wait(act, conv_acc, g - 1)
                for half in range(2):
                    at = TAPS - 1 + half * HALF
                    take_bank(pre[:, at:at + HALF], g, g, half)
                split_hi(g + 1, 1)
                wait(act, conv_acc, g)
                wait(act, conv_done, g - 1)
                act.activation(th[:, :], acc[:, :], ACT.Tanh).then_inc(conv_th.sem, 1)

            with act.Fori(0, 12) as g:
                conv_tile(g)
            with act.Fori(0, HEADS) as j:
                split_hi(j + 13, 0)
                for half in range(2):
                    take_bank(zv_flat[:, bass.ds(j * SEQ + half * HALF, HALF)], j + G_ZB, j + G_ZB, half)
                split_hi(j + 13, 1)
                wait(act, proj_out, j + G_ZB)
                act.wait_ge(z_silu.sem, j + 1)
                wait(act, conv_done, 11)
                settle(act)
                act.activation(th[:, :], zv_flat[:, bass.ds(j * SEQ, SEQ)], ACT.Tanh, scale=0.5).then_inc(z_th_ready.sem, 1)
            split_hi(G_FILL, 0)
            for half in range(2):
                take_bank(ab_rows[:, half * HALF:(half + 1) * HALF], G_AB, G_AB, half)
            split_hi(G_FILL, 1)

            act.wait_ge(ab_loaded.sem, 32)
            act.activation(a_dt[:, 0, :], a_dt[:, 0, :], ACT.Exp).then_inc(a2_act.sem, 1)
            act.wait_ge(a2_dve.sem, A2_ABS)
            act.activation(log1p[:, 2, :, :], log1p[:, 1, :, :], ACT.Exp, scale=-1.0).then_inc(a2_act.sem, 1)
            act.activation(log1p[:, 7, :, :], ab[:, :, HEADS:2 * HEADS], ACT.Exp, scale=-1.0).then_inc(a2_act.sem, 1)
            act.wait_ge(a2_dve.sem, A2_DECAY)
            act.activation(log1p[:, 0, :, :], token_scalars[:, :, 0, :], ACT.Exp).then_inc(a2_act.sem, 1)
            act.activation(log1p[:, 1, :, :], log1p[:, 3, :, :], ACT.Exp).then_inc(a2_act.sem, 1)

            with act.Fori(0, NT) as t:
                wait(act, diff_ready, t)
                act.activation(gam[:, :, :], gam[:, :, :], ACT.Exp).then_inc(gam_ready.sem, 1)
                wait(act, o_mm, t - 1)
                act.activation(qd[:, :, :], bank4(7), ACT.Exp)\
                    .then_inc(eg_ready.sem, 1)
                wait(act, eg_ready, t, 1)
                wait(act, sg_ready, t - 1)
                act.activation(egl[:, :, :], qd[:, :, CHUNK - 1:P:CHUNK].rearrange("p h c -> p c h"), ACT.Copy)\
                    .then_inc(eg_ready.sem, 1)
                g_v, g_gate = t * 2 + G_FILL, t * 2 + (G_FILL + 1)
                split_hi(g_gate, 0)
                wait(act, x0_T, t)
                act.activation(X[:, :, :], bank4(2), ACT.Copy).then_inc(x0_ready.sem, 1)
                for level in range(1, LEVELS):
                    wait(act, y_mm, t, level)
                    if level > 1:
                        wait(act, v_mm, t, level - 1)
                    act.activation(Y[:, :, :], bank4(2), ACT.Copy).then_inc(y_ready.sem, 1)
                    if level == 1:
                        take_bank(zv_flat[:, bass.ds(t * SEQ + 4 * SEQ, HALF)], g_v, g_v, 0)
                    if level == 3:
                        take_bank(zv_flat[:, bass.ds(t * SEQ + (4 * SEQ + HALF), HALF)], g_v, g_v, 1)
                    if level == 4:
                        split_hi(g_gate, 1)
                wait(act, w_mm, t)
                act.activation(nwT[:, :, :], bank4(7), ACT.Copy, scale=-1.0).then_inc(nw_ready.sem, 1)
                for c in range(2):
                    rows = slice(c * CHUNK, (c + 1) * CHUNK)
                    wait(act, vnew_mm, t, c + 1)
                    act.activation(v_new[rows, :, :], bank4(5)[rows], ACT.Copy).then_inc(vnew_ready.sem, 1)
                    if c == 0:
                        split_hi(t * 2 + (G_FILL + 2), 0)
                wait(act, gate_stored, t - 1)
                take_bank(gate_st[:, 0:HALF], g_gate, g_gate, 0, ACT.Tanh, 0.5)
                wait(act, o_mm, t)
                for h in range(HEADS):
                    if h == 0:
                        wait(act, on_ready, t - 1)
                    act.activation(o_sq[:, h, :], bank4(6)[:, h, :], ACT.Square, accum_out=o_ss[:, h:h + 1])\
                        .then_inc(o_ss_ready.sem, 1)
                take_bank(gate_st[:, HALF:SEQ], g_gate, g_gate, 1, ACT.Tanh, 0.5)
                split_hi(t * 2 + (G_FILL + 2), 1)

            for s in range(2):
                split_hi(G_QK + s + 1, 0)
                if s == 0:
                    wait(act, yb_ready, NT - 1)
                for half in range(2):
                    take_bank(qk_raw[:, s, half * HALF:(half + 1) * HALF], G_QK + s, G_QK + s, half)
                split_hi(G_QK + s + 1, 1)

            def head(h, last):
                order = stream_order(2, C_START_LAST, C_TILE_LAST) if last else stream_order(4, C_START, C_TILE)

                def stream(kind, t):
                    for what, g, b in order.get((kind, t), []):
                        if what == "split":
                            split_hi(h * 4 + (G_C + 1 + g), b)
                        elif not last and g < 2:
                            take_bank(qk_raw[:, g, b * HALF:(b + 1) * HALF], h * 4 + (G_C + g), h * 4 + (G_C + g), b)
                        else:
                            second = (g if last else g - 2) == 1
                            if second:
                                wait(act, c_v, h)
                            dst, at = (zv_flat, 4 * SEQ) if second else (gate_b_flat, 0)
                            take_bank(dst[:, bass.ds(h * SEQ + (at + b * HALF), HALF)],
                                      h * 4 + (G_C + g), h * 4 + (G_C + g), b, ACT.Tanh, 0.5)

                wait(act, proj_out, h * 4 + (G_C - 3))
                wait(act, c_stat, h - 1)
                for s in (1, 0):
                    act.activation(qk_sq[:, s, :], qk_raw[:, s, :], ACT.Square).then_inc(c_sq.sem, 1)
                act.wait_ge(c_z.sem, h + 1)
                settle(act)
                act.activation(z_th[:, :], zv_flat[:, bass.ds(h * SEQ + 8 * SEQ, SEQ)], ACT.Tanh, scale=0.5)\
                    .then_inc(c_zth.sem, 1)
                stream("start", 0)
                wait(act, c_vT, h)
                wait(act, c_o, h * NT - 1)
                act.activation(v_tok[:, :, :].rearrange("p t d -> p (t d)"), banks(6), ACT.Copy).then_inc(c_vtok.sem, 1)
                wait(act, c_kT2, h)
                act.activation(kT[:, :], banks(2), ACT.Copy, scale=gain_qk[:, 0:1]).then_inc(c_kT.sem, 1)

                def exps(t):
                    n = (t + 1) * P
                    st = h * NT + t
                    wait(act, c_mx, st)
                    wait(act, c_pc, st - 1)
                    for m in range(2):
                        act.activation(prob[:, m, 0:n], banks(2 + 2 * m)[:, 0:n], ACT.Exp, bias=nm[:, m:m + 1],
                                       scale=r_qk[:, 0, t, m:m + 1], accum_out=l_sum[:, m:m + 1]).then_inc(c_p.sem, 1)

                exps(0)
                stream("start", 1)
                for t in range(NT):
                    st = h * NT + t
                    n = (t + 1) * P
                    wait(act, c_pT, st)
                    wait(act, c_o, st - 1)
                    act.activation(probT[:, 0:t + 1, :].rearrange("p t d -> p (t d)"), banks(6)[:, 0:n], ACT.Copy)\
                        .then_inc(c_pT_sb.sem, 1)
                    if t + 1 < NT:
                        exps(t + 1)
                    stream("scores", t)
                    wait(act, c_o, st)
                    act.activation(o_junk[:, :], PS[:, 6, 0:P], ACT.Square, accum_out=at_s[:, 0:1]).then_inc(c_oss.sem, 1)
                    stream("output", t)

            wait(act, proj_out, G_QK + 1)
            with act.Fori(0, HEADS - 1) as h:
                head(h, False)
            head(HEADS - 1, True)

            wait(act, c_y, HEADS * NT - 1)
            for i in range(8):
                act.activation(y_hi[:, i, :], zv[:, (i + 8) % 12, :], ACT.Copy).then_inc(yhi_ready.sem, 1)

            def round_m(n):
                wait(act, d_gated, n)
                settle(act)
                act.activation(h_hi_flat[:, bass.ds(n * SEQ, SEQ)], zv_flat[:, bass.ds(n * SEQ, SEQ)], ACT.Copy, scale=0.5)\
                    .then_inc(m_hi_ready.sem, 1)

            split_hi(PAIR_D + 1, 0)
            split_hi(PAIR_D + 1, 1)
            with act.Fori(1, NK) as n:
                split_hi(n + (PAIR_D + 1), 0)
                round_m(n - 1)
                split_hi(n + (PAIR_D + 1), 1)
            act.wait_ge(d_gated.sem, d_gated.at(NK - 1))
            act.activation(h_hi[:, NK - 1, :], m32[:, NK - 1, :], ACT.Copy, scale=0.5).then_inc(m_hi_ready.sem, 1)

            with act.Fori(0, NK - 1) as p:
                for b in range(2):
                    split_hi(p + (PAIR_E + 1), b)

        @block.tensor
        def _(pe):
            pe.sem_inc(w_used.sem, w_used.lead)
            for s_ in (xT_ready, qk_ss, kk_qk, g_b, v_mm, o_mm, s_mm, on_T, c_stat, c_kT1, c_pT, c_o):
                pe.sem_inc(s_.sem, s_.lead)
            pe.wait_ge(vec_loaded.sem, 16 * (len(VEC_ROWS) + 2))
            pe.wait_ge(consts_ready.sem, N_CONSTS)
            pe.transpose(PS[:, 7, 0:60], vec_rows[0:60, :], ident[0:60, 0:60]).then_inc(vec_T.sem, 1)

            def transpose_x(i, b):
                wait(pe, xs_ready, i * 4 + b)
                wait(pe, h32_ready, i * 4 + (b - 2))
                for k in range(NK):
                    last = pe.transpose(PS[:, 2 * (b % 2) + k // 4, (k % 4) * P:(k % 4 + 1) * P],
                                        xs[:, b % 2, k * P:(k + 1) * P], ident[:, :])
                last.then_inc(xT_ready.sem, 1)

            with pe.Fori(0, NT // 4) as i:
                for b in range(4):
                    transpose_x(i, b)

            def three_passes(dst, w, lo_w, hi, lo, first, last):
                pe.matmul(dst, w, hi, start=first, stop=False)
                yield None
                pe.matmul(dst, w, lo, start=False, stop=False)
                yield None
                mm = pe.matmul(dst, lo_w, hi, start=False, stop=last)
                yield mm

            def projection(g, pair):
                for kh in range(2):
                    wait(pe, w_lo_ready, pair * 2 + kh)
                    for half in range(2):
                        if kh == 0:
                            wait(pe, proj_out, g - 1, half + 1)
                        for k in range(4):
                            cols = slice(k * P, (k + 1) * P)
                            toks = slice(half * HALF, (half + 1) * HALF)
                            steps = three_passes(PS[:, half, :], w_hi[:, kh, cols], w_lo[:, kh, cols],
                                                 h_hi[:, 4 * kh + k, toks], h_lo[:, 4 * kh + k, toks],
                                                 kh == 0 and k == 0, kh == 1 and k == 3)
                            for mm in steps:
                                if mm is not None and k == 3:
                                    if half == 1:
                                        mm.then_inc(w_used.sem, 1)
                                    elif kh == 1:
                                        mm.then_inc(proj_half0.sem, 1)
                                yield

            def projection_pair(g):
                yield from projection(g, g)
                yield from projection(g + 1, g + 1)

            def whole(steps):
                for _ in steps:
                    pass

            def take(steps, n):
                for _ in range(n):
                    next(steps, None)

            wait(pe, h_lo_ready, NT - 1)
            with pe.Fori(0, G_FILL) as g:
                whole(projection(g, g))

            pe.wait_ge(proj_out.sem, proj_out.at(G_AB))
            for t in range(NT):
                last = pe.transpose(PS[:, 2, t * 8:(t + 1) * 8], ab_rows[:, t * P:(t + 1) * P], ident[0:8, 0:8])
            last.then_inc(ab_T.sem, 1)
            with pe.Fori(0, NT // 2) as i:
                for b in range(2):
                    wait(pe, sq8_ready, i * 2 + b)
                    for c in range(8):
                        last = pe.matmul(PS[:, 3, bass.ds(i * 16 + (b * 8 + c), 1)], sq8[:, b, c, :], ones1[:, :],
                                         start=True, stop=True)
                    last.then_inc(qk_ss.sem, 1)
            pe.wait_ge(a2_dve.sem, A2_G)
            g_all = token_scalars[:, :, 6, :]
            pe.matmul(PS[:, 4, 0:32], tri[:, :], g_all, start=True, stop=True)
            pe.matmul(PS[:, 4, 32:64], block_ones[:, :], g_all, start=True, stop=True, skip_group_check=True)\
                .then_inc(a2_cum.sem, 1)

            def each_head(fn, signal=None):
                for h in range(HEADS):
                    last = fn(h)
                if signal is not None:
                    last.then_inc(signal.sem, 1)

            def delta_tiles(t, first):
                fill = projection_pair(t * 2 + G_FILL)
                wait(pe, ts_ready, t)
                each_head(lambda h: pe.matmul(bank4(7)[:, h, :], ts[:, 6, h:h + 1].broadcast_to([P, P]), tri[:, :],
                                              start=True, stop=True), g_b)
                wait(pe, tile_in, t, 1)
                each_head(lambda h: pe.transpose(bank4(2)[:, h, :], ct[:, 4 + h, :], ident[:, :]), kv_T)
                each_head(lambda h: pe.matmul(bank4(4)[:, h, :], ct[:, 4 + h, :], ct[:, 4 + h, :], start=True, stop=True), kk_qk)
                each_head(lambda h: pe.matmul(bank4(5)[:, h, :], ct[:, 4 + h, :], ct[:, h, :], start=True, stop=True), kk_qk)
                pe.wait_ge(s_ready.sem, t * 2 + 1)
                wait(pe, tile_in, t, 2)
                each_head(lambda h: pe.transpose(bank4(3)[:, h, :], vt[:, h, :], ident[:, :]), kv_T)
                if not first:
                    out_transpose(t - 1)
                take(fill, B_FRONT[0])
                wait(pe, yb_ready, t - 1)
                each_head(lambda h: pe.matmul(bank4(6)[:, h, :], ts[:, 5, h:h + 1].broadcast_to([P, P]), ident[:, :],
                                              start=True, stop=True), g_b)
                take(fill, B_FRONT[1])
                wait(pe, v0_ready, t)
                wait(pe, kv_scaled, t, 2)
                each_head(lambda h: pe.transpose(bank4(2)[:, h, :], V[:, h, :], ident[:, :]), x0_T)
                take(fill, 4)
                wait(pe, x0_ready, t)
                wait(pe, kv_scaled, t)
                for level in range(1, LEVELS):
                    if level > 1:
                        wait(pe, x_ready, t, level - 1)
                    wait(pe, um_ready, t, level + 1)
                    each_head(lambda h: pe.matmul(bank4(2)[:, h, :], um[:, level % 2, h, :], X[:, h, :],
                                                  start=True, stop=True), y_mm)
                    take(fill, 4)
                    wait(pe, y_ready, t, level)
                    if level > 1:
                        wait(pe, v_ready, t, level - 1)
                    if level < LEVELS - 1:
                        each_head(lambda h: pe.matmul(bank4(3)[:, h, :], V[:, h, :], Y[:, h, :], start=True, stop=True), x_mm)
                    wait(pe, u_ready, t)
                    each_head(lambda h: pe.matmul(bank4(4)[:, h, :], Y[:, h, :], V[:, h, :], start=True, stop=True), v_mm)
                    take(fill, 2)
                wait(pe, v_ready, t)
                wait(pe, at_ready, t)
                wait(pe, eg_ready, t, 1)
                each_head(lambda h: pe.matmul(bank4(5)[:, h, :], V[:, h, :], v_beta[:, h, :], start=(h == 0), stop=False,
                                              skip_group_check=True), w_mm)
                each_head(lambda h: pe.matmul(bank4(7)[:, h, :], k_exp[:, h, :], V[:, h, :], start=True, stop=True), w_mm)
                take(fill, 6)
                wait(pe, nw_ready, t)
                wait(pe, qd_ready, t)
                for c in range(2):
                    rows = slice(c * CHUNK, (c + 1) * CHUNK)
                    pe.wait_ge(s_ready.sem, t * 2 + (c + 1))
                    each_head(lambda h: pe.matmul(bank4(5)[rows, h, :], nwT[:, h, rows], S[:, h, :], start=False,
                                                  stop=True, skip_group_check=True), vnew_mm)
                    each_head(lambda h: pe.matmul(bank4(6)[rows, h, :], qd[:, h, rows], S[:, h, :], start=(h == 0),
                                                  stop=False, skip_group_check=True))
                    take(fill, 6)
                    wait(pe, vnew_ready, t, c + 1)
                    each_head(lambda h: pe.matmul(bank4(3)[:, h, :], k_tail[rows, h, :], v_new[rows, h, :],
                                                  start=True, stop=True), s_mm)
                    each_head(lambda h: pe.matmul(bank4(6)[rows, h, :], gm[rows, h, rows], v_new[rows, h, :], start=False,
                                                  stop=True, skip_group_check=True), o_mm)
                    take(fill, 5)
                whole(fill)

            def out_transpose(t):
                wait(pe, on_ready, t)
                each_head(lambda h: pe.transpose(bank4(6)[:, h, :], on_b[:, h, :], ident[:, :]), on_T)

            delta_tiles(0, True)
            with pe.Fori(1, NT) as t:
                delta_tiles(t, False)
            out_transpose(NT - 1)

            for s in range(2):
                whole(projection(G_QK + s, G_QK + s))

            def k_transposes(h):
                wait(pe, c_p, h * NT - 1)
                wait(pe, proj_out, h * 4 + (G_C - 3))
                for t in range(NT):
                    mm = pe.transpose(PS[:, 2 + t // 4, (t % 4) * P:(t % 4 + 1) * P], qk_raw[:, 1, t * P:(t + 1) * P], ident[:, :])
                mm.then_inc(c_kT1.sem, 1)

            def out_transpose(st):
                wait(pe, c_on, st)
                pe.transpose(PS[:, 7, 0:P], on_a[:, :], ident[:, :]).then_inc(c_oT.sem, 1)

            def head(h, last):
                fill, start, tile = next_tiles(h, last), *((C_START_LAST, C_TILE_LAST) if last else (C_START, C_TILE))
                for s in (1, 0):
                    wait(pe, c_sq, h, 2 - s)
                    for t in range(NT):
                        mm = pe.matmul(PS[:, 5 - s, 2 * t:2 * t + 2], qk_sq[:, s, t * P:(t + 1) * P], block_ones[:, 0:P:SUB],
                                       start=True, stop=True)
                    mm.then_inc(c_stat.sem, 1)
                take(fill, start[0])
                wait(pe, c_y, h * NT - 1)
                wait(pe, c_v, h)
                for t in range(NT):
                    mm = pe.transpose(PS[:, 6 + t // 4, (t % 4) * P:(t % 4 + 1) * P], v_st[:, t * P:(t + 1) * P], ident[:, :])
                mm.then_inc(c_vT.sem, 1)
                take(fill, start[1])
                wait(pe, c_ktok, h)
                for t in range(NT):
                    mm = pe.transpose(PS[:, 2 + t // 4, (t % 4) * P:(t % 4 + 1) * P],
                                      k_tok[:, t, :, :].rearrange("p s d -> p (s d)"), ident[:, :])
                mm.then_inc(c_kT2.sem, 1)
                take(fill, start[2])
                wait(pe, c_kT, h)
                wait(pe, c_q, h)
                wait(pe, c_vtok, h)

                def scores(t):
                    n = (t + 1) * P
                    for m in range(2):
                        rows = slice(m * SUB, (m + 1) * SUB)
                        wait(pe, c_p, h * NT + t - 1, m + 1)
                        for at in range(0, n, HALF):
                            to = min(at + HALF, n)
                            pe.matmul(PS[:, 2 + 2 * m + at // HALF, 0:to - at], qT[rows, t * P:(t + 1) * P],
                                      kT[rows, at:to], start=True, stop=False, skip_group_check=True)
                        end = (n - 1) % HALF + 1
                        pe.matmul(PS[:, 2 + 2 * m + (n - 1) // HALF, end - CHUNK:end], mask_lhs[rows, :],
                                  neg_rows[rows, :], start=False, stop=True, skip_group_check=True)\
                            .then_inc(c_s.sem, 1)

                scores(0)
                for t in range(NT):
                    st = h * NT + t
                    if t + 1 < NT:
                        scores(t + 1)
                    take(fill, tile[0])
                    if t > 0:
                        out_transpose(st - 1)
                    take(fill, tile[1])
                    wait(pe, c_pc, st)
                    wait(pe, c_y, st - 1)
                    for k in range(t + 1):
                        mm = pe.transpose(PS[:, 6 + k // 4, (k % 4) * P:(k % 4 + 1) * P], prob_c[:, k * P:(k + 1) * P], ident[:, :])
                    mm.then_inc(c_pT.sem, 1)
                    take(fill, tile[2])
                    wait(pe, c_pT_sb, st)
                    for k in range(t + 1):
                        mm = pe.matmul(PS[:, 6, 0:P], probT[:, k, :], v_tok[:, k, :], start=(k == 0), stop=(k == t))
                    mm.then_inc(c_o.sem, 1)
                    take(fill, tile[3])
                whole(fill)
                if not last:
                    k_transposes(h + 1)
                out_transpose(h * NT + (NT - 1))

            def next_tiles(h, last):
                for i in range(2 if last else 4):
                    yield from projection(h * 4 + (G_C + i), h * 4 + (G_C + i))

            wait(pe, proj_out, G_QK + 1)
            k_transposes(0)
            with pe.Fori(0, HEADS - 1) as h:
                head(h, False)
            head(HEADS - 1, True)

            wait(pe, c_y, HEADS * NT - 1)
            with pe.Fori(0, NK) as n:
                for i in range(2):
                    wait(pe, w_lo_ready, n * 2 + (PAIR_D * 2 + i))
                    for half in range(2):
                        wait(pe, d_gated, n - 1, 1 + half + 2 * i)
                        for k in range(4):
                            wait(pe, ylo_ready, 4 * i + k)
                            cols, toks = slice(k * P, (k + 1) * P), slice(half * HALF, (half + 1) * HALF)
                            for mm in three_passes(PS[:, 2 + 2 * i + half, :], w_hi[:, i, cols], w_lo[:, i, cols],
                                                   y_hi[:, 4 * i + k, toks], y_lo[:, 4 * i + k, toks], k == 0, k == 3):
                                if mm is not None and k == 3:
                                    mm.then_inc((d_up if half == 0 else w_used).sem, 1)

            wait(pe, proj_out, G_END - 1)
            wait(pe, d_gated, NK - 1)
            with pe.Fori(0, 2) as c:
                for k in range(NK):
                    b = k % 2
                    wait(pe, w_lo_ready, c * NK + (PAIR_E * 2 + k))
                    wait(pe, m_lo_ready, k)
                    for t in range(NT):
                        if k == 0:
                            wait(pe, out_sum, c - 1, t + 1)
                        toks = slice(t * P, (t + 1) * P)
                        pe.matmul(PS[:, t, :], h_hi[:, k, toks], w_hi[:, b, :], start=(k == 0), stop=False)
                        pe.matmul(PS[:, t, :], h_hi[:, k, toks], w_lo[:, b, :], start=False, stop=False)
                        mm = pe.matmul(PS[:, t, :], h_lo[:, k, toks], w_hi[:, b, :], start=False, stop=(k == NK - 1))
                        if t == NT - 1:
                            mm.then_inc(w_used.sem, 1)
                        elif k == NK - 1:
                            mm.then_inc(out_mm.sem, 1)

        @block.vector
        def _(dve):
            for s_ in (h32_ready, conv_acc, conv_done, z_silu, qd_ready, x_ready, s_ready, on_ready, yb_ready,
                       c_z, c_pc, c_on, c_y, d_gated, out_sum):
                dve.sem_inc(s_.sem, s_.lead)
            dve.wait_ge(lam_loaded.sem, 16)
            for i in range(2):
                if i:
                    dve.wait_ge(lam_sums.sem, 1)
                dve.tensor_tensor_reduce(lam_junk[:, :], lam_rows[:, 2 * i, :], lam_rows[:, 2 * i + 1, :], 1.0, 0.0,
                                         ALU.mult, ALU.add, lam_s[:, i:i + 1]).then_inc(lam_sums.sem, 1)
            dve.wait_ge(lam_exp.sem, 1)
            dve.tensor_tensor(neg_lam[:, :], lam_s[:, 3:4], lam_s[:, 2:3], ALU.subtract).then_inc(lam_ready.sem, 1)
            dve.wait_ge(lam_ready.sem, 1)
            dve.tensor_scalar(neg_lam[:, :], neg_lam[:, :], -LAMBDA_INIT, None, ALU.add).then_inc(lam_ready.sem, 1)
            dve.wait_ge(vec_T.sem, 1)
            dve.tensor_copy(vec[:, 0:60], PS[:, 7, 0:60]).then_inc(vec_ready.sem, 1)
            dve.wait_ge(vec_ready.sem, 1)
            dve.tensor_scalar(half_conv[:, :, :].rearrange("p c w -> p w c"),
                              vec[:, 0:48].rearrange("p (w c) -> p w c", c=12), 0.5, None, ALU.mult).then_inc(vec_ready.sem, 1)
            dve.tensor_scalar(gain_b[:, :], vec[:, 56:57], 0.5, None, ALU.mult).then_inc(vec_ready.sem, 1)
            dve.tensor_scalar(gain_a[:, :], vec[:, 57:58], 0.5 * (1.0 - LAMBDA_INIT), None, ALU.mult).then_inc(vec_ready.sem, 1)
            dve.scalar_tensor_tensor(out=gain_qk[:, :], in0=vec[:, 58:59], scalar=SUB ** -0.5, in1=vec[:, 59:60],
                                     op0=ALU.mult, op1=ALU.mult).then_inc(vec_ready.sem, 1)

            def row_mean_square(i, b):
                wait(dve, x_loaded[b], i)
                wait(dve, xs_ready, i * 4 + (b - 4))
                dve.tensor_tensor_reduce(sq_junk[:, b % 2, :], x_in[:, b, :], x_in[:, b, :], 1.0, 0.0, ALU.mult, ALU.add,
                                         row_sq[:, b:b + 1]).then_inc(row_ms_ready.sem, 1)
                wait(dve, row_ms_ready, i * 4 + b, 1)
                dve.tensor_scalar(row_ms[:, b:b + 1], row_sq[:, b:b + 1], 1.0 / DM, EPS, ALU.mult, ALU.add)\
                    .then_inc(row_ms_ready.sem, 1)

            def h_columns(i, b):
                wait(dve, xT_ready, i * 4 + b)
                wait(dve, h_lo_ready, i * 4 + (b - 2))
                dve.tensor_tensor(h32[:, b % 2, :, :],
                                  PS[:, 2 * (b % 2):2 * (b % 2) + 2, :].rearrange("p a (k n) -> p (a k) n", n=P),
                                  vec[:, 48:56].unsqueeze(2).broadcast_to([P, NK, P]), ALU.mult).then_inc(h32_ready.sem, 1)

            with dve.Fori(0, NT // 4) as i:
                row_mean_square(i, 0)
                row_mean_square(i, 1)
                for b in range(4):
                    if b < 2:
                        row_mean_square(i, b + 2)
                    h_columns(i, b)

            wait(dve, h_lo_ready, NT - 1)
            dve.memset(pre[:, 0:TAPS - 1], 0.0).then_inc(pre_zero.sem, 1)
            dve.wait_ge(pre_zero.sem, 1)
            dve.wait_ge(vec_ready.sem, 5)
            with dve.Fori(0, 12) as c:
                wait(dve, conv_acc, c - 1)
                dve.tensor_copy(cw[:, :], half_conv_flat[:, bass.ds(c * TAPS, TAPS)]).then_inc(conv_w_ready.sem, 1)
                wait(dve, proj_out, c)
                wait(dve, conv_w_ready, c)
                wait(dve, conv_done, c - 1)
                for tap in range(TAPS):
                    src = pre[:, tap:tap + SEQ]
                    if tap == 0:
                        ins = dve.tensor_scalar(acc[:, :], src, cw[:, 0:1], None, ALU.mult)
                    else:
                        wait(dve, conv_acc, c, tap)
                        ins = dve.scalar_tensor_tensor(out=acc[:, :], in0=src, scalar=cw[:, tap:tap + 1], in1=acc[:, :],
                                                       op0=ALU.mult, op1=ALU.add)
                    ins.then_inc(conv_acc.sem, 1)
                wait(dve, conv_th, c)
                dve.scalar_tensor_tensor(out=conv_flat[:, bass.ds(c * SEQ, SEQ)], in0=th[:, :], scalar=1.0, in1=acc[:, :],
                                         op0=ALU.add, op1=ALU.mult).then_inc(conv_done.sem, 1)
            with dve.Fori(0, HEADS) as j:
                wait(dve, z_th_ready, j)
                z = zv_flat[:, bass.ds(j * SEQ, SEQ)]
                dve.scalar_tensor_tensor(out=z, in0=th[:, :], scalar=1.0, in1=z, op0=ALU.add, op1=ALU.mult)\
                    .then_inc(z_silu.sem, 1)

            done = [0]

            def link(ins):
                done[0] += 1
                ins.then_inc(a2_dve.sem, 1)
                dve.wait_ge(a2_dve.sem, done[0])

            def bc(v):
                return v.unsqueeze(1).broadcast_to([P, NT, HEADS])

            L = [log1p[:, n, :, :] for n in range(8)]
            T = [token_scalars[:, :, n, :] for n in range(8)]
            dve.wait_ge(ab_T.sem, 1)
            link(dve.tensor_copy(ab[:, :, :].rearrange("p t c -> p (t c)"), PS[:, 2, 0:64]))
            dve.wait_ge(a2_act.sem, 1)
            link(dve.tensor_tensor(L[0], ab[:, :, 0:HEADS], bc(a_dt[:, 1, :]), ALU.add))
            link(dve.tensor_scalar(L[1], L[0], -1.0, None, ALU.mult))
            link(dve.tensor_tensor(L[1], L[1], L[0], ALU.max))
            assert done[0] == A2_ABS
            dve.wait_ge(a2_act.sem, 3)
            link(dve.tensor_scalar(L[3], L[2], 2.0, None, ALU.add))
            link(dve.reciprocal(L[3], L[3]))
            link(dve.tensor_tensor(L[3], L[3], L[2], ALU.mult))
            link(dve.tensor_tensor(L[4], L[3], L[3], ALU.mult))
            link(dve.tensor_scalar(L[5], L[4], 2.0 / 15, 2.0 / 13, ALU.mult, ALU.add))
            for n in (11, 9, 7, 5, 3, 1):
                link(dve.tensor_tensor(L[5], L[5], L[4], ALU.mult))
                link(dve.tensor_scalar(L[5], L[5], 2.0 / n, None, ALU.add))
            link(dve.tensor_tensor(L[5], L[5], L[3], ALU.mult))
            link(dve.scalar_tensor_tensor(out=L[5], in0=L[0], scalar=0.0, in1=L[5], op0=ALU.max, op1=ALU.add))
            link(dve.scalar_tensor_tensor(out=T[6], in0=L[5], scalar=-1.0, in1=bc(a_dt[:, 0, :]), op0=ALU.mult, op1=ALU.mult))
            assert done[0] == A2_G, done[0]
            link(dve.tensor_scalar(L[6], L[7], 1.0, None, ALU.add))
            link(dve.reciprocal(T[2], L[6]))
            dve.wait_ge(a2_cum.sem, 1)
            link(dve.tensor_copy(T[0], PS[:, 4, 0:32].rearrange("p (t h) -> p t h", h=HEADS)))
            link(dve.tensor_tensor(L[3], PS[:, 4, 32:64].rearrange("p (t h) -> p t h", h=HEADS), T[0], ALU.subtract))
            assert done[0] == A2_DECAY, done[0]
            wait(dve, qk_ss, NT - 1)
            link(dve.tensor_scalar(qk_ms[:, :, :].rearrange("p t c -> p (t c)"), PS[:, 3, 0:64], EPS, None, ALU.add))
            assert done[0] == A2_QK_MS, done[0]
            dve.wait_ge(qk_pow.sem, 1)
            rq, rk = qk_r[:, :, 0:HEADS], qk_r[:, :, HEADS:2 * HEADS]
            link(dve.tensor_copy(T[1], rk))
            link(dve.tensor_tensor(T[5], T[2], rk, ALU.mult))
            link(dve.tensor_scalar(T[7], rq, float(HD) ** -0.5, None, ALU.mult))
            dve.wait_ge(a2_act.sem, 5)
            link(dve.tensor_tensor(T[3], T[5], L[0], ALU.mult))
            link(dve.tensor_tensor(T[4], L[1], rk, ALU.mult))

            def wide(col):
                return ts[:, col, :].unsqueeze(2).broadcast_to([P, HEADS, P])

            dve.memset(S[:, :, :], 0.0).then_inc(s_zero.sem, 1)
            dve.wait_ge(s_zero.sem, 1)
            dve.tensor_copy(ts[:, :, :].rearrange("p a h -> p (a h)"), ts_flat[:, 0:32]).then_inc(ts_ready.sem, 1)
            dve.tensor_copy(ct[:, :, :], conv_out[:, 0:8, 0:P]).then_inc(tile_in.sem, 1)
            dve.tensor_copy(vt[:, :, :], conv_out[:, 8:12, 0:P]).then_inc(tile_in.sem, 1)

            def write_y(t):
                wait(dve, on_T, t)
                y = zv[:, 0:4, bass.ds(t * P, P)]
                dve.scalar_tensor_tensor(out=y, in0=bank4(6), scalar=gain_b[:, 0:1], in1=y, op0=ALU.mult, op1=ALU.mult)\
                    .then_inc(yb_ready.sem, 1)

            def norm_out(t):
                wait(dve, o_pow, t)
                dve.tensor_tensor(o_f[:, :], o_r[:, :], o_scale[:, :], ALU.mult).then_inc(on_ready.sem, 1)
                wait(dve, on_ready, t, 1)
                dve.tensor_tensor(on_b[:, :, :], bank4(6), o_f[:, :].unsqueeze(2).broadcast_to([P, HEADS, P]), ALU.mult)\
                    .then_inc(on_ready.sem, 1)

            def delta_tiles(t, first, last):
                wait(dve, ts_ready, t)
                wait(dve, g_b, t, 1)
                wait(dve, o_mm, t - 1)
                for h in range(HEADS):
                    dve.tensor_scalar(gam[:, h, :], bank4(7)[:, h, :], ts[:, 0, h:h + 1], 0.0, ALU.subtract, ALU.min)\
                        .then_inc(diff_ready.sem, 1)
                if not first:
                    norm_out(t - 1)
                dve.tensor_copy(o_scale[:, :], ts[:, 7, :]).then_inc(o_scale_ready.sem, 1)
                wait(dve, kv_T, t, 1)
                dve.tensor_tensor(k_tail[:, :, :], bank4(2), wide(4), ALU.mult).then_inc(kv_scaled.sem, 1)
                wait(dve, gam_ready, t)
                for h in range(HEADS):
                    dve.scalar_tensor_tensor(out=gm[:, h, :], in0=gam[:, h, :], scalar=ts[:, 1, h:h + 1], in1=tri[:, :],
                                             op0=ALU.mult, op1=ALU.mult).then_inc(gm_ready.sem, 1)
                dve.tensor_tensor(k_exp[:, :, :], bank4(2), wide(3), ALU.mult).then_inc(kv_scaled.sem, 1)
                wait(dve, gm_ready, t)
                wait(dve, kk_qk, t)
                dve.tensor_tensor(U[:, :, :], bank4(4), gm[:, :, :], ALU.mult).then_inc(u_ready.sem, 1)
                dve.tensor_tensor(gm[:, :, :], bank4(5), gm[:, :, :], ALU.mult).then_inc(at_ready.sem, 1)
                wait(dve, kv_T, t)
                dve.tensor_tensor(v_beta[:, :, :], bank4(3), wide(2), ALU.mult).then_inc(kv_scaled.sem, 1)
                if not first:
                    write_y(t - 1)
                wait(dve, eg_ready, t)
                dve.tensor_tensor(qd[:, :, :], ct[:, 0:4, :], qd[:, :, :], ALU.mult).then_inc(qd_ready.sem, 1)
                wait(dve, u_ready, t, 1)
                wait(dve, g_b, t)
                dve.tensor_tensor(U[:, :, :], bank4(6), U[:, :, :], ALU.mult).then_inc(u_ready.sem, 1)
                wait(dve, um_ready, t, 1)
                dve.tensor_tensor(V[:, :, :], ident[:, :].unsqueeze(1).broadcast_to([P, HEADS, P]), um[:, 0, :, :],
                                  ALU.subtract).then_inc(v0_ready.sem, 1)
                for level in range(1, LEVELS):
                    if level < LEVELS - 1:
                        wait(dve, x_mm, t, level)
                        if level == 1:
                            wait(dve, x0_ready, t)
                        else:
                            wait(dve, x_ready, t, level - 1)
                        dve.tensor_tensor(X[:, :, :], X[:, :, :], bank4(3), ALU.subtract).then_inc(x_ready.sem, 1)
                    wait(dve, v_mm, t, level)
                    if level > 1:
                        wait(dve, v_ready, t, level - 1)
                    dve.tensor_tensor(V[:, :, :], V[:, :, :], bank4(4), ALU.subtract).then_inc(v_ready.sem, 1)
                    if last:
                        continue
                    cols = bass.ds(t * P + P, P)
                    if level == 1:
                        wait(dve, qd_ready, t)
                        dve.tensor_copy(ct[:, :, :], conv_out[:, 0:8, cols]).then_inc(tile_in.sem, 1)
                    if level == 2:
                        dve.tensor_copy(vt[:, :, :], conv_out[:, 8:12, cols]).then_inc(tile_in.sem, 1)
                    if level == 3:
                        wait(dve, o_scale_ready, t)
                        dve.tensor_copy(ts[:, :, :].rearrange("p a h -> p (a h)"), ts_flat[:, bass.ds(t * 32 + 32, 32)])\
                            .then_inc(ts_ready.sem, 1)
                for c in range(2):
                    wait(dve, s_mm, t, c + 1)
                    wait(dve, sg_ready, t, c + 1)
                    dve.tensor_tensor(S[:, :, :], Sg[:, :, :], bank4(3), ALU.add).then_inc(s_ready.sem, 1)
                wait(dve, o_ss_ready, t)
                dve.tensor_tensor(o_ms[:, :], o_ss[:, :], o_scale[:, :], ALU.mult).then_inc(o_ms_ready.sem, 1)
                wait(dve, o_ms_ready, t, 1)
                dve.tensor_tensor(o_ms[:, :], o_ms[:, :], o_scale[:, :], ALU.mult).then_inc(o_ms_ready.sem, 1)
                wait(dve, o_ms_ready, t, 2)
                dve.tensor_scalar(o_ms[:, :], o_ms[:, :], 1.0 / HD, EPS, ALU.mult, ALU.add).then_inc(o_ms_ready.sem, 1)

            delta_tiles(0, True, False)
            with dve.Fori(1, NT - 1) as t:
                delta_tiles(t, False, False)
            delta_tiles(NT - 1, False, True)
            norm_out(NT - 1)
            write_y(NT - 1)

            def head(h):
                wait(dve, proj_out, h * 4 + (G_C - 4))
                dve.tensor_copy(qT[:, :], qk_raw[:, 0, :]).then_inc(c_q.sem, 1)
                dve.tensor_copy(v_st[:, :], zv_flat[:, bass.ds(h * SEQ + 4 * SEQ, SEQ)]).then_inc(c_v.sem, 1)
                for s in (1, 0):
                    wait(dve, c_stat, h, 2 - s)
                    dve.tensor_scalar(r_ms[:, s, :, :].rearrange("p t s -> p (t s)"), PS[:, 5 - s, 0:16],
                                      1.0 / SUB, EPS, ALU.mult, ALU.add).then_inc(c_ms.sem, 1)
                wait(dve, c_r, h, 1)
                wait(dve, c_kT1, h)
                dve.tensor_tensor(k_tok[:, :, :, :], banks(2).rearrange("p (t s d) -> p t s d", s=2, d=SUB),
                                  r_qk[:, 1, :, :].unsqueeze(3).broadcast_to([P, NT, 2, SUB]), ALU.mult)\
                    .then_inc(c_ktok.sem, 1)
                wait(dve, c_zth, h)
                z = zv_flat[:, bass.ds(h * SEQ + 8 * SEQ, SEQ)]
                dve.scalar_tensor_tensor(out=z, in0=z_th[:, :], scalar=1.0, in1=z, op0=ALU.add, op1=ALU.mult)\
                    .then_inc(c_z.sem, 1)
                wait(dve, c_r, h)

                def maxima(t):
                    st = h * NT + t
                    n = (t + 1) * P
                    for m in range(2):
                        wait(dve, c_s, st, m + 1)
                        dve.reduce_max(mx[:, m:m + 1], banks(2 + 2 * m)[:, 0:n], AX.X).then_inc(c_mx.sem, 1)
                    wait(dve, c_mx, st, 2)
                    wait(dve, c_p, st - 1)
                    dve.scalar_tensor_tensor(out=nm[:, :], in0=mx[:, :], scalar=-1.0, in1=r_qk[:, 0, t, :],
                                             op0=ALU.mult, op1=ALU.mult).then_inc(c_mx.sem, 1)

                def combine(t):
                    st = h * NT + t
                    n = (t + 1) * P
                    wait(dve, c_p, st)
                    wait(dve, c_on, st - 1)
                    dve.reciprocal(at_s[:, 5:7], l_sum[:, :]).then_inc(c_coef.sem, 1)
                    wait(dve, c_coef, st, 1)
                    dve.tensor_tensor(at_s[:, 7:8], at_s[:, 6:7], l_sum[:, 0:1], ALU.mult).then_inc(c_coef.sem, 1)
                    dve.tensor_tensor(at_s[:, 9:10], at_s[:, 5:6], at_s[:, 5:6], ALU.mult).then_inc(c_coef.sem, 1)
                    wait(dve, c_coef, st, 2)
                    dve.tensor_tensor(at_s[:, 8:9], at_s[:, 7:8], neg_lam[:, :], ALU.mult).then_inc(c_coef.sem, 1)
                    wait(dve, c_coef, st, 4)
                    wait(dve, c_pT, st - 1)
                    dve.scalar_tensor_tensor(out=prob_c[:, 0:n], in0=prob[:, 1, 0:n], scalar=at_s[:, 8:9],
                                             in1=prob[:, 0, 0:n], op0=ALU.mult, op1=ALU.add).then_inc(c_pc.sem, 1)

                maxima(0)
                combine(0)
                for t in range(NT):
                    st = h * NT + t
                    if t + 1 < NT:
                        maxima(t + 1)
                    wait(dve, c_oss, st)
                    dve.tensor_scalar(at_s[:, 2:3], at_s[:, 0:1], at_s[:, 9:10], 1.0 / HD, ALU.mult, ALU.mult)\
                        .then_inc(c_oms.sem, 1)
                    wait(dve, c_oms, st, 1)
                    dve.tensor_scalar(at_s[:, 3:4], at_s[:, 2:3], EPS, None, ALU.add).then_inc(c_oms.sem, 1)
                    wait(dve, c_opow, st)
                    dve.tensor_scalar(on_a[:, :], PS[:, 6, 0:P], at_s[:, 4:5], at_s[:, 5:6], ALU.mult, ALU.mult)\
                        .then_inc(c_on.sem, 1)
                    if t + 1 < NT:
                        combine(t + 1)
                    wait(dve, c_oT, st)
                    y = zv_flat[:, bass.ds(h * SEQ + (8 * SEQ + t * P), P)]
                    if t == 0:
                        wait(dve, c_z, h)
                    dve.scalar_tensor_tensor(out=y, in0=PS[:, 7, 0:P], scalar=gain_a[:, 0:1], in1=y,
                                             op0=ALU.mult, op1=ALU.mult).then_inc(c_y.sem, 1)

            wait(dve, proj_out, G_QK + 1)
            with dve.Fori(0, HEADS - 1) as h:
                head(h)
            head(HEADS - 1)

            for i in range(8):
                wait(dve, yhi_ready, i)
                dve.tensor_tensor(y_lo[:, i, :], zv[:, (i + 8) % 12, :], y_hi[:, i, :].bitcast(F32), ALU.subtract)\
                    .then_inc(ylo_ready.sem, 1)
            wait(dve, ylo_ready, 7)

            def m_rest(n):
                wait(dve, m_hi_ready, n)
                m_hi = h_hi_flat[:, bass.ds(n * SEQ, SEQ)].bitcast(F32)
                dve.scalar_tensor_tensor(out=h_lo_flat[:, bass.ds(n * SEQ, SEQ)], in0=zv_flat[:, bass.ds(n * SEQ, SEQ)],
                                         scalar=0.5, in1=m_hi, op0=ALU.mult, op1=ALU.subtract).then_inc(m_lo_ready.sem, 1)

            def merge(n, j, b, gates_b, first=False):
                g_a = [gate_a[:, b, half * HALF:(half + 1) * HALF] for half in range(2)]
                g_b = [gates_b[:, bass.ds(n * SEQ + half * HALF, HALF)] for half in range(2)]
                for i, g in enumerate((g_a, g_b)):
                    if i == 0:
                        wait(dve, gate_loaded[b], j)
                    for half in range(2):
                        if half == 0:
                            wait(dve, d_up, n, i + 1)
                        else:
                            wait(dve, w_used, n * 2 + (PAIR_D * 2 + i))
                        dve.scalar_tensor_tensor(out=g[half], in0=g[half], scalar=1.0, in1=PS[:, 2 + 2 * i + half, :],
                                                 op0=ALU.add, op1=ALU.mult).then_inc(d_gated.sem, 1)
                    if i == 0 and not first:
                        m_rest(n - 1)
                for half in range(2):
                    wait(dve, d_gated, n, 3 + half)
                    dve.tensor_tensor(zv_flat[:, bass.ds(n * SEQ + half * HALF, HALF)], g_a[half], g_b[half], ALU.add)\
                        .then_inc(d_gated.sem, 1)

            merge(0, 0, 0, gate_b_flat, first=True)
            for n in range(1, HEADS):
                merge(n, n // 2, n % 2, gate_b_flat)
            with dve.Fori(2, NK // 2) as j:
                for b in range(2):
                    merge(j * 2 + b, j, b, zv_flat)
            m_rest(NK - 1)

            dve.wait_ge(x_res_loaded.sem, 16)
            for c in range(2):
                for t in range(NT):
                    if t < NT - 1:
                        wait(dve, out_mm, c, t + 1)
                    else:
                        wait(dve, w_used, PAIR_E * 2 + (c + 1) * NK - 1)
                    cols = slice(c * HALF, (c + 1) * HALF)
                    dve.tensor_tensor(out_sb[:, t, cols], PS[:, t, :], x_res[:, t, cols], ALU.add).then_inc(out_sum.sem, 1)


_INS = ["x", "norm_w", "w_in", "da_q_gain", "da_k_gain", "da_lambda", "da_out_gain", "gdn_conv_w",
        "gdn_a_log", "gdn_dt_bias", "gdn_norm_w", "w_up_da", "w_up_gdn", "w_out"]


def kernel(**inputs):
    import numpy as _np
    import concourse.bacc as _bacc
    from concourse.bass_utils import run_bass_kernel_spmd as _run

    nc = _bacc.Bacc("TRN2", target_bir_lowering=False, num_devices=1, dynamic_dma_scratch_size=1024)
    arrays, args = {}, []
    for name in _INS:
        a = _np.ascontiguousarray(inputs[name])
        arrays[f"in_{name}"] = a
        args.append(nc.dram_tensor(f"in_{name}", a.shape, F32, kind="ExternalInput").ap())
    args.append(nc.dram_tensor("out_0", (1, SEQ, DM), F32, kind="ExternalOutput").ap())
    hybrid_block(nc, *args)
    r = _run(nc, [arrays], core_ids=[0])
    return r.results[0]["out_0"]
```

```python
import math
from contextlib import ExitStack

import concourse.bass as bass
from concourse import mybir

F32 = mybir.dt.float32
F32R = mybir.dt.float32r
ALU = mybir.AluOpType
ACT = mybir.ActivationFunctionType
AX = mybir.AxisListType

P = 128
SEQ, DM = 1024, 1024
NT = SEQ // P
NK = DM // P
HALF = 512
CHUNK = 64
HEADS = 4
HD = 128
SUB = 64
TAPS = 4
EPS = 1e-6
LAMBDA_INIT = 0.8 - 0.6 * math.exp(-0.3 * 0)
WIDTH = HEADS * HD
COL_QA, COL_KA, COL_VA, COL_ZA = 0, WIDTH, 2 * WIDTH, 3 * WIDTH
COL_QB = 4 * WIDTH
COL_AB = 8 * WIDTH
COL_GATE = COL_AB + 2 * HEADS
LEVELS = 6
NEG = -1.0e30


class Signal:

    def __init__(self, sem, per=1, lead=0):
        self.sem, self.per, self.lead = sem, per, lead

    def at(self, step, k=None):
        return step * self.per + (self.lead + (self.per if k is None else k))


def hybrid_block(nc, x, norm_w, w_in, da_q_gain, da_k_gain, da_lambda, da_out_gain, conv_w,
                 gdn_a_log, gdn_dt_bias, gdn_norm_w, w_up_da, w_up_gdn, w_out, out):
    ctx = ExitStack()
    with ctx:
        def sig(name, per=1, lead=0):
            return Signal(ctx.enter_context(nc.semaphore(name)), per, lead)

        def sb(scope, name, shape, dt=F32):
            return scope.enter_context(nc.sbuf_tensor(name, shape, dt))

        x_t = x[0].rearrange("(t p) d -> p t d", p=P)
        out_t = out[0].rearrange("(t p) d -> p t d", p=P)
        w_in_k = w_in[0].rearrange("(k p) n -> p k n", p=P)
        w_out_k = w_out[0].rearrange("(k p) n -> p k n", p=P)
        w_up_k = [w[0].rearrange("(k p) n -> p k n", p=P) for w in (w_up_da, w_up_gdn)]

        h_hi = sb(ctx, "h_hi", [P, NK, SEQ], F32R)
        h_lo = sb(ctx, "h_lo", [P, NK, SEQ], F32R)
        w_raw = sb(ctx, "w_raw", [P, 2, HALF])
        w_hi = sb(ctx, "w_hi", [P, 2, HALF], F32R)
        w_lo = sb(ctx, "w_lo", [P, 2, HALF], F32R)
        zv = sb(ctx, "zv", [P, 12, SEQ])
        ident = sb(ctx, "ident", [P, P])
        tri = sb(ctx, "tri", [P, P])
        block_ones = sb(ctx, "block_ones", [P, P])
        vec_rows = sb(ctx, "vec_rows", [64, P])
        vec = sb(ctx, "vec", [P, 64])
        half_conv = sb(ctx, "half_conv", [P, 12, TAPS])
        gain_b = sb(ctx, "gain_b", [P, 1])
        gain_a = sb(ctx, "gain_a", [P, 1])
        gain_qk = sb(ctx, "gain_qk", [P, 1])
        neg_lam = sb(ctx, "neg_lam", [P, 1])
        mask_lhs = sb(ctx, "mask_lhs", [P, P])
        neg_rows = sb(ctx, "neg_rows", [P, CHUNK])
        ones1 = sb(ctx, "ones1", [P, 1])
        token_scalars = sb(ctx, "token_scalars", [P, NT, 8, HEADS])
        a_dt = sb(ctx, "a_dt", [P, 2, HEADS])
        neg_half = sb(ctx, "neg_half", [P, 64])
        lam_rows = sb(ctx, "lam_rows", [P, 4, SUB])
        lam_junk = sb(ctx, "lam_junk", [P, SUB])
        lam_s = sb(ctx, "lam_s", [P, 4])
        PS = ctx.enter_context(nc.psum_tensor("PS", [P, 8, HALF], F32))

        scope = ExitStack()
        x_in = sb(scope, "x_in", [P, NT, DM])
        xs = sb(scope, "xs", [P, 2, DM])
        h32 = sb(scope, "h32", [P, 2, NK, P])
        row_sq = sb(scope, "row_sq", [P, NT])
        row_ms = sb(scope, "row_ms", [P, NT])
        row_r = sb(scope, "row_r", [P, NT])
        sq_junk = sb(scope, "sq_junk", [P, 2, DM])
        scope.close()

        scope_ab = ExitStack()
        conv_out = sb(scope_ab, "conv_out", [P, 12, SEQ])
        ct = sb(scope_ab, "ct", [P, 8, P])
        vt = sb(scope_ab, "vt", [P, HEADS, P])
        masks = sb(scope_ab, "masks", [P, LEVELS, P])
        S = sb(scope_ab, "S", [P, HEADS, P])
        scope = ExitStack()
        pre = sb(scope, "pre", [P, TAPS - 1 + SEQ])
        acc = sb(scope, "acc", [P, SEQ])
        th = sb(scope, "th", [P, SEQ])
        cw = sb(scope, "cw", [P, TAPS])
        ab_rows = sb(scope, "ab_rows", [8, SEQ])
        ab = sb(scope, "ab", [P, NT, 8])
        qk_st = sb(scope, "qk_st", [P, 2, 8, P])
        sq8 = sb(scope, "sq8", [P, 2, 8, P])
        log1p = sb(scope, "log1p", [P, 8, NT, HEADS])
        qk_ms = sb(scope, "qk_ms", [P, 2, 8])
        qk_r = sb(scope, "qk_r", [P, NT, 8])
        scope.close()
        scope = ExitStack()
        ts = sb(scope, "ts", [P, 8, HEADS])
        gam = sb(scope, "gam", [P, HEADS, P])
        qd = sb(scope, "qd", [P, HEADS, P])
        egl = sb(scope, "egl", [P, 2, HEADS])
        gm = sb(scope, "gm", [P, HEADS, P])
        U = sb(scope, "U", [P, HEADS, P])
        um = sb(scope, "um", [P, 2, HEADS, P])
        V = sb(scope, "V", [P, HEADS, P])
        X = sb(scope, "X", [P, HEADS, P])
        Y = sb(scope, "Y", [P, HEADS, P])
        k_tail = sb(scope, "k_tail", [P, HEADS, P])
        k_exp = sb(scope, "k_exp", [P, HEADS, P])
        v_beta = sb(scope, "v_beta", [P, HEADS, P])
        Sg = sb(scope, "Sg", [P, HEADS, P])
        on_b = sb(scope, "on_b", [P, HEADS, P])
        gate_st = sb(scope, "gate_st", [P, SEQ])
        o_scale = sb(scope, "o_scale", [P, HEADS])
        o_ss = sb(scope, "o_ss", [P, HEADS])
        o_ms = sb(scope, "o_ms", [P, HEADS])
        o_r = sb(scope, "o_r", [P, HEADS])
        o_f = sb(scope, "o_f", [P, HEADS])
        scope.close()
        scope_ab.close()
        v_new, nwT = gam, X

        scope_cd = ExitStack()
        gate_b = sb(scope_cd, "gate_b", [P, HEADS + 1, SEQ])
        scope = ExitStack()
        qk_raw = sb(scope, "qk_raw", [P, 2, SEQ])
        qk_sq = sb(scope, "qk_sq", [P, 2, SEQ])
        q_hi = sb(scope, "q_hi", [P, SEQ], F32R)
        q_lo = sb(scope, "q_lo", [P, SEQ], F32R)
        k_hi = sb(scope, "k_hi", [P, SEQ], F32R)
        k_lo = sb(scope, "k_lo", [P, SEQ], F32R)
        v_st = sb(scope, "v_st", [P, SEQ])
        k_tok = sb(scope, "k_tok", [P, NT, 2, SUB])
        v_tok = sb(scope, "v_tok", [P, NT, P])
        z_th = sb(scope, "z_th", [P, SEQ])
        prob = sb(scope, "prob", [P, 2, SEQ])
        prob_c = sb(scope, "prob_c", [P, SEQ])
        probT = sb(scope, "probT", [P, NT, P])
        on_a = sb(scope, "on_a", [P, P])
        o_junk = sb(scope, "o_junk", [P, P])
        r_ms = sb(scope, "r_ms", [P, 2, NT, 2])
        r_qk = sb(scope, "r_qk", [P, 2, NT, 2])
        mx = sb(scope, "mx", [P, 2])
        nm = sb(scope, "nm", [P, 2])
        l_sum = sb(scope, "l_sum", [P, 2])
        at_s = sb(scope, "at_s", [P, 12])
        scope.close()

        scope = ExitStack()
        y_hi = sb(scope, "y_hi", [P, 8, SEQ], F32R)
        y_lo = sb(scope, "y_lo", [P, 8, SEQ], F32R)
        gate_a = sb(scope, "gate_a", [P, 2, SEQ])
        scope.close()
        scope_cd.close()
        scope = ExitStack()
        x_res = sb(scope, "x_res", [P, NT, DM])
        out_sb = sb(scope, "out_sb", [P, NT, DM])
        scope.close()
        m32 = zv[:, 0:8, :]

        vec_loaded = sig("vec_loaded")
        lam_loaded = sig("lam_loaded")
        ab_loaded = sig("ab_loaded")
        x_loaded = [sig(f"x_loaded{b}", 16) for b in range(NT)]
        consts_ready = sig("consts_ready")
        vec_T = sig("vec_T")
        vec_ready = sig("vec_ready")
        lam_sums = sig("lam_sums")
        lam_exp = sig("lam_exp")
        lam_ready = sig("lam_ready")
        row_ms_ready = sig("row_ms_ready", 2)
        row_r_ready = sig("row_r_ready")
        xs_ready = sig("xs_ready")
        xT_ready = sig("xT_ready", lead=2)
        h32_ready = sig("h32_ready", lead=2)
        h_hi_ready = sig("h_hi_ready")
        h_lo_ready = sig("h_lo_ready", lead=2)
        w_loaded = [sig(f"w_loaded{b}", 16) for b in range(2)]
        w_hi_ready = sig("w_hi_ready")
        w_lo_ready = sig("w_lo_ready", lead=2)
        w_used = sig("w_used", lead=2)
        proj_half0 = sig("proj_half0")
        proj_out = sig("proj_out", 2, lead=2)
        conv_w_ready = sig("conv_w_ready")
        conv_acc = sig("conv_acc", TAPS, lead=TAPS)
        conv_th = sig("conv_th", lead=1)
        conv_done = sig("conv_done", lead=1)
        z_th_ready = sig("z_th_ready")
        z_silu = sig("z_silu", lead=1)
        ab_T = sig("ab_T")
        a2_dve = sig("a2_dve")
        a2_act = sig("a2_act")
        a2_cum = sig("a2_cum")
        pre_zero = sig("pre_zero")
        s_zero = sig("s_zero")
        st_ready = sig("st_ready")
        st_T = sig("st_T", lead=2)
        st_sq = sig("st_sq", lead=2)
        st_sum = sig("st_sum", 2, lead=4)
        qk_pow = sig("qk_pow", lead=2)
        tile_in = sig("tile_in", 2)
        o_scale_ready = sig("o_scale_ready")
        gate_stored = sig("gate_stored", 16, lead=16)
        gate_loaded = [sig(f"gate_loaded{b}", 16) for b in range(2)]
        ts_ready = sig("ts_ready")
        kv_T = sig("kv_T", 2)
        kk_qk = sig("kk_qk", 2, lead=2)
        g_b = sig("g_b", 2, lead=2)
        diff_ready = sig("diff_ready", 4)
        gam_ready = sig("gam_ready")
        eg_ready = sig("eg_ready", 2)
        kv_scaled = sig("kv_scaled", 3)
        gm_ready = sig("gm_ready", 4)
        u_ready = sig("u_ready", 2)
        at_ready = sig("at_ready")
        qd_ready = sig("qd_ready", lead=1)
        um_ready = sig("um_ready", LEVELS)
        v0_ready = sig("v0_ready")
        x0_T = sig("x0_T")
        x0_ready = sig("x0_ready")
        y_mm = sig("y_mm", LEVELS - 1)
        y_ready = sig("y_ready", LEVELS - 1)
        x_mm = sig("x_mm", LEVELS - 1)
        v_mm = sig("v_mm", LEVELS - 1)
        x_ready = sig("x_ready", LEVELS - 1)
        v_ready = sig("v_ready", LEVELS - 1)
        w_mm = sig("w_mm", 2)
        nw_ready = sig("nw_ready", lead=1)
        vnew_mm = sig("vnew_mm", 2)
        vnew_ready = sig("vnew_ready", 2, lead=2)
        o_mm = sig("o_mm", 2, lead=2)
        s_mm = sig("s_mm", 2, lead=2)
        sg_ready = sig("sg_ready", 2, lead=2)
        s_ready = sig("s_ready", 2, lead=1)
        o_ss_ready = sig("o_ss_ready", 4)
        o_ms_ready = sig("o_ms_ready", 3)
        o_pow = sig("o_pow")
        on_ready = sig("on_ready", 2, lead=2)
        on_T = sig("on_T", lead=1)
        yb_ready = sig("yb_ready", lead=1)
        c_sq = sig("c_sq", 2)
        c_q = sig("c_q", 2)
        c_v = sig("c_v")
        c_ms = sig("c_ms", 4, lead=4)
        c_r = sig("c_r", 2)
        c_kT1 = sig("c_kT1", 2, lead=2)
        c_vT = sig("c_vT")
        c_ktok = sig("c_ktok")
        c_vtok = sig("c_vtok", lead=1)
        c_kT2 = sig("c_kT2")
        c_kT = sig("c_kT")
        c_klo = sig("c_klo")
        c_zth = sig("c_zth")
        c_z = sig("c_z", lead=1)
        c_s = sig("c_s", 2)
        c_mx = sig("c_mx", 3)
        c_p = sig("c_p", 2, lead=2)
        c_coef = sig("c_coef", 4)
        c_pc = sig("c_pc", lead=1)
        c_pT = sig("c_pT", lead=1)
        c_pT_sb = sig("c_pT_sb", lead=1)
        c_o = sig("c_o", lead=1)
        c_oss = sig("c_oss")
        c_oms = sig("c_oms", 2)
        c_opow = sig("c_opow")
        c_on = sig("c_on", lead=1)
        c_oT = sig("c_oT")
        c_y = sig("c_y", lead=1)
        yhi_ready = sig("yhi_ready")
        ylo_ready = sig("ylo_ready")
        d_up = sig("d_up", 2)
        d_gated = sig("d_gated", 6, lead=12)
        m_hi_ready = sig("m_hi_ready")
        m_lo_ready = sig("m_lo_ready")
        x_res_loaded = sig("x_res_loaded", 16 * NT)
        out_mm = sig("out_mm", NT - 1)
        out_sum = sig("out_sum", NT, lead=NT)
        stored = sig("stored", 16)

        G_AB, G_ZB, G_FILL = 12, 13, 17
        G_QK = G_FILL + 2 * NT - 1
        G_C = G_QK + 2
        LAST_TILES = 3
        G_END = G_C + 4 * (HEADS - 1) + LAST_TILES
        PAIR_D = G_END
        PAIR_E = PAIR_D + NK
        passed = sig("passed")

        def settle(eng):
            eng.sem_inc(passed.sem, 1)

        A2_ABS, A2_G, A2_DECAY = 4, 24, 28
        N_CONSTS = 14
        Y_ORDER = [(i, half, k) for i in range(2) for half in range(2) for k in range(4)]
        B_FRONT = (14, 16)
        B_LEVEL = (3, 3)
        C_START, C_TILE = (24, 16, 8), (6, 5, 4, 3)
        C_START_LAST, C_TILE_LAST = (20, 14, 8), (4, 4, 3, 2)

        SLACK = 12

        def stream_order(tiles, start, tile):
            places, n = [], sum(start[:2])
            places.append(("start", 0, n, n))
            n += start[2]
            places.append(("start", 1, n, n + sum(tile[:2])))
            for t in range(NT):
                places.append(("scores", t, n + sum(tile[:2]), n + sum(tile[:3])))
                n += sum(tile)
                places.append(("output", t, n - tile[3], n + tile[0] if t < NT - 1 else 48 * tiles))
            events = []
            for g in range(tiles):
                events += [(48 * g + 24, 48 * g + 48, ("split", g, 0)), (48 * g + 36, 48 * g + 48, ("take", g, 0)),
                           (48 * g + 48, 48 * g + 60, ("take", g, 1)), (48 * g + 48, 48 * g + 72, ("split", g, 1))]
            order = {}
            for can, need, what in events:
                at = next(i for i, p in enumerate(places) if can <= p[3])
                if places[at][0] == "scores" and need >= places[at + 1][2] + SLACK:
                    at += 1
                kind, t, behind, ahead = places[at]
                assert need >= behind or need > 48 * tiles, (what, kind, t)
                order.setdefault((kind, t), []).append(what)
            return order

        VEC_ROWS = [(0, conv_w[0].rearrange("w (c p) -> (w c) p", p=P)), (48, norm_w[0].rearrange("(k p) -> k p", p=P)),
                    (56, gdn_norm_w), (57, da_out_gain), (58, da_q_gain), (59, da_k_gain)]
        x_rows = x[0]
        zv_flat = zv[:, :, :].rearrange("p c n -> p (c n)")
        conv_flat = conv_out[:, :, :].rearrange("p c n -> p (c n)")
        qk_r_flat = qk_r[:, :, :].rearrange("p t c -> p (t c)")
        half_conv_flat = half_conv[:, :, :].rearrange("p c w -> p (c w)")
        ts_flat = token_scalars[:, :, :, :].rearrange("p t a h -> p (t a h)")

        def bank4(b):
            return PS[:, b, :].rearrange("p (h n) -> p h n", h=HEADS)

        def banks(b):
            return PS[:, b:b + 2, :].rearrange("p a n -> p (a n)")

        h_hi_flat = h_hi[:, :, :].rearrange("p k s -> p (k s)")
        h_lo_flat = h_lo[:, :, :].rearrange("p k s -> p (k s)")

        def halves(tile, level, which):
            return tile.rearrange("p h n -> p (h n)").rearrange("p (b two s) -> p b two s", two=2, s=1 << level)[:, :, which, :]

        def blocks(tile, level):
            return tile.rearrange("p (b s) -> p b s", s=1 << level)

        Y_flat = Y[:, :, :].rearrange("p h n -> p (h n)")[:, 0:HEADS * CHUNK]
        o_sq = Y
        gate_dram = nc.dram_tensor("gate_dram", ((NK - 1) * P, SEQ), F32, kind="Internal")
        gate_dram_flat = gate_dram.ap()
        gate_b_flat = gate_b[:, :, :].rearrange("p n s -> p (n s)")
        block = ctx.enter_context(nc.Block())

        @block.sync
        def _(sp):
            def load_slab(pair, b, src):
                sp.wait_ge(w_lo_ready.sem, w_lo_ready.at(pair * 2 + (b - 2)))
                settle(sp)
                dst = w_raw[:, b, :]
                if len(src.shape) == 3:
                    dst = dst.rearrange("p (k n) -> p k n", k=src.shape[1])
                sp.dma_start(dst, src).then_inc(w_loaded[b].sem, 16)

            def load_tile(pair, col):
                for b in range(2):
                    load_slab(pair, b, w_in_k[:, 4 * b:4 * b + 4, bass.ds(col, P)])

            sp.sem_inc(gate_stored.sem, gate_stored.lead)
            def load_x(t):
                sp.dma_start(x_in[:, t, :], x_rows[t * P:(t + 1) * P, :]).then_inc(x_loaded[t].sem, 16)

            load_x(0)
            load_x(1)
            for row, src in VEC_ROWS:
                sp.dma_start(vec_rows[row:row + src.shape[0], 0:src.shape[1]], src).then_inc(vec_loaded.sem, 16)
            for row, src in ((58, da_q_gain), (59, da_k_gain)):
                sp.dma_start(vec_rows[row:row + 1, SUB:P], src).then_inc(vec_loaded.sem, 16)
            for t in range(2, NT):
                load_x(t)
                if t == NT // 2 - 1:
                    load_tile(0, COL_QB)
            sp.dma_start(lam_rows[:, :, :].rearrange("p a b -> p (a b)"),
                          da_lambda.rearrange("o a b -> o (a b)").broadcast_to([P, 4 * SUB])).then_inc(lam_loaded.sem, 16)
            sp.dma_start(a_dt[:, 0, :], gdn_a_log.broadcast_to([P, HEADS])).then_inc(ab_loaded.sem, 16)
            sp.dma_start(a_dt[:, 1, :], gdn_dt_bias.broadcast_to([P, HEADS])).then_inc(ab_loaded.sem, 16)
            with sp.Fori(1, 12) as j:
                load_tile(j, j * P + COL_QB)
            load_tile(G_AB, COL_AB)
            with sp.Fori(0, HEADS) as j:
                load_tile(j + G_ZB, j * P + (COL_QB + 3 * WIDTH))

            def store_gate(t):
                sp.wait_ge(proj_out.sem, proj_out.at(t * 2 + (G_FILL + 1)))
                settle(sp)
                sp.dma_start(gate_dram_flat[bass.ds(t * P, P), :], gate_st[:, :]).then_inc(gate_stored.sem, 16)

            load_tile(G_FILL, COL_VA)
            load_tile(G_FILL + 1, COL_GATE)
            with sp.Fori(1, NT - 1) as t:
                load_tile(t * 2 + G_FILL, t * P + COL_VA)
                store_gate(t - 1)
                load_tile(t * 2 + (G_FILL + 1), t * P + COL_GATE)
            load_tile(G_QK - 1, (NT - 1) * P + COL_VA)
            store_gate(NT - 2)
            load_tile(G_QK, COL_QA)
            load_tile(G_QK + 1, COL_KA)
            with sp.Fori(1, HEADS) as h:
                load_tile(h * 4 + (G_C - 4), h * P + COL_QA)
                load_tile(h * 4 + (G_C - 3), h * P + COL_KA)
                for i in range(2):
                    load_tile(h * 4 + (G_C - 2 + i), h * P + (COL_GATE + DM + (HEADS * i - 1) * P))
            for i in range(2):
                load_tile(G_C + 4 * (HEADS - 1) + i, COL_GATE + DM + (HEADS * i + HEADS - 1) * P)
            load_tile(G_END - 1, COL_GATE + (NK - 1) * P)

            def load_up(n):
                for i in range(2):
                    load_slab(n + PAIR_D, i, w_up_k[i][:, :, bass.ds(n * P, P)])

            def load_gate(j, b):
                sp.wait_ge(gate_stored.sem, gate_stored.at(NT - 2))
                sp.wait_ge(c_y.sem, c_y.at(HEADS * NT - 1))
                sp.wait_ge(d_gated.sem, d_gated.at(j * 2 + (b - 2)))
                settle(sp)
                sp.dma_start(gate_a[:, b, :], gate_dram_flat[bass.ds((j * 2 + b) * P, P), :]).then_inc(gate_loaded[b].sem, 16)

            with sp.Fori(0, NK // 2 - 1) as j:
                for b in range(2):
                    load_up(j * 2 + b)
                    load_gate(j, b)
            load_up(NK - 2)
            load_gate(NK // 2 - 1, 0)
            load_up(NK - 1)
            for c in range(2):
                for k in range(NK):
                    load_slab(PAIR_E + c * NK // 2 + k // 2, k % 2, w_out_k[:, k, c * HALF:(c + 1) * HALF])
                    for t in {7: [NT - 2, NT - 1]}.get(k, [k - 1] if k else []) if c == 0 else []:
                        sp.wait_ge(w_used.sem, w_used.at(PAIR_E * 2 - 1))
                        sp.wait_ge(d_gated.sem, d_gated.at(NK - 1))
                        sp.dma_start(x_res[:, t, :], x_t[:, t, :]).then_inc(x_res_loaded.sem, 16)
                    if c == 1:
                        sp.wait_ge(out_sum.sem, out_sum.at(0, k + 1))
                        sp.dma_start(out_t[:, k, 0:HALF], out_sb[:, k, 0:HALF]).then_inc(stored.sem, 16)
            for t in range(NT):
                sp.wait_ge(out_sum.sem, out_sum.at(1, t + 1))
                sp.dma_start(out_t[:, t, HALF:DM], out_sb[:, t, HALF:DM]).then_inc(stored.sem, 16)
            sp.wait_ge(stored.sem, stored.at(2 * NT - 1))

        @block.gpsimd
        def _(pool):
            made = [0]

            def link(ins):
                made[0] += 1
                ins.then_inc(consts_ready.sem, 1)
                pool.wait_ge(consts_ready.sem, made[0])

            pool.sem_inc(w_lo_ready.sem, w_lo_ready.lead)
            pool.sem_inc(h_lo_ready.sem, h_lo_ready.lead)
            pool.sem_inc(sg_ready.sem, sg_ready.lead)
            pool.sem_inc(qk_pow.sem, qk_pow.lead)
            link(pool.memset(ident[:, :], 0.0))
            link(pool.affine_select(out=ident[:, :], in_=ident[:, :], compare_op=ALU.not_equal, fill=1.0,
                                    base=0, pattern=[[-1, P]], channel_multiplier=1))
            link(pool.memset(neg_half[:, :], -0.5))
            link(pool.memset(ones1[:, :], 1.0))
            link(pool.memset(tri[:, :], 1.0))
            link(pool.affine_select(out=tri[:, :], in_=tri[:, :], compare_op=ALU.is_ge, fill=0.0,
                                    base=0, pattern=[[1, P]], channel_multiplier=-1))
            link(pool.memset(tri[0:CHUNK, CHUNK:P], 0.0))
            link(pool.memset(block_ones[:, :], 0.0))
            link(pool.memset(block_ones[0:CHUNK, 0:CHUNK], 1.0))
            link(pool.memset(block_ones[CHUNK:P, CHUNK:P], 1.0))
            link(pool.memset(mask_lhs[:, :], 0.0))
            link(pool.memset(mask_lhs[0:1, 0:CHUNK], 1.0))
            link(pool.memset(mask_lhs[CHUNK:CHUNK + 1, 0:CHUNK], 1.0))
            link(pool.memset(neg_rows[:, :], NEG))
            assert made[0] == N_CONSTS

            def split_lo(pair, b):
                pool.wait_ge(w_hi_ready.sem, w_hi_ready.at(pair * 2 + b))
                pool.tensor_tensor(w_lo[:, b, :], w_raw[:, b, :], w_hi[:, b, :].bitcast(F32), ALU.subtract)\
                    .then_inc(w_lo_ready.sem, 1)

            def row_pow(t):
                pool.wait_ge(row_ms_ready.sem, row_ms_ready.at(t))
                pool.tensor_tensor(row_r[:, t:t + 1], row_ms[:, t:t + 1], neg_half[:, 0:1], ALU.pow)\
                    .then_inc(row_r_ready.sem, 1)

            def h_rest(t):
                pool.wait_ge(h_hi_ready.sem, h_hi_ready.at(t))
                cols = slice(t * P, (t + 1) * P)
                pool.tensor_tensor(h_lo[:, :, cols], h32[:, t % 2, :, :], h_hi[:, :, cols].bitcast(F32), ALU.subtract)\
                    .then_inc(h_lo_ready.sem, 1)

            row_pow(0)
            row_pow(1)
            for t in range(NT):
                if t + 2 < NT:
                    row_pow(t + 2)
                if t == NT // 2:
                    for b in range(2):
                        split_lo(0, b)
                h_rest(t)

            link(pool.memset(masks[:, :, :], 0.0))
            for level in range(LEVELS):
                split_lo(level + 1, 0)
                split_lo(level + 1, 1)
                s = 1 << level
                second = masks[:, level, :].rearrange("p (b two s) -> p b two s", two=2, s=s)[:, :, 1, :]
                nb = P // (2 * s)
                link(pool.memset(second, 1.0))
                link(pool.affine_select(out=second, in_=second, compare_op=ALU.is_ge, fill=0.0,
                                        base=0, pattern=[[-2 * s, nb], [0, s]], channel_multiplier=1))
                link(pool.affine_select(out=second, in_=second, compare_op=ALU.is_ge, fill=0.0,
                                        base=s - 1, pattern=[[2 * s, nb], [0, s]], channel_multiplier=-1))

            with pool.Fori(LEVELS, G_ZB) as g:
                for b in range(2):
                    split_lo(g + 1, b)
            with pool.Fori(0, HEADS) as j:
                split_lo(j + (G_ZB + 1), 0)
                for b in range(2):
                    pool.wait_ge(st_sum.sem, st_sum.at(j * 2 + b))
                    settle(pool)
                    pool.tensor_tensor(qk_r_flat[:, bass.ds((j * 2 + b) * 8, 8)], qk_ms[:, b, :], neg_half[:, 0:8], ALU.pow)\
                        .then_inc(qk_pow.sem, 1)
                split_lo(j + (G_ZB + 1), 1)

            with pool.Fori(0, NT) as t:
                for level in range(LEVELS):
                    if level == 0:
                        pool.wait_ge(u_ready.sem, u_ready.at(t))
                    if level == 2:
                        pool.wait_ge(v0_ready.sem, v0_ready.at(t))
                    if level >= 3:
                        pool.wait_ge(y_mm.sem, y_mm.at(t, level - 2))
                    pool.tensor_tensor(um[:, level % 2, :, :], U[:, :, :],
                                       masks[:, level, :].unsqueeze(1).broadcast_to([P, HEADS, P]), ALU.mult)\
                        .then_inc(um_ready.sem, 1)
                    if level == 2:
                        split_lo(t * 2 + (G_FILL + 1), 0)
                split_lo(t * 2 + (G_FILL + 1), 1)
                for c in range(2):
                    if c == 0:
                        pool.wait_ge(eg_ready.sem, eg_ready.at(t))
                    pool.wait_ge(s_ready.sem, t * 2 + (c + 1))
                    pool.tensor_tensor(Sg[:, :, :], S[:, :, :],
                                       egl[:, c, :].unsqueeze(2).broadcast_to([P, HEADS, P]), ALU.mult)\
                        .then_inc(sg_ready.sem, 1)
                split_lo(t * 2 + (G_FILL + 2), 0)
                pool.wait_ge(o_ms_ready.sem, o_ms_ready.at(t))
                pool.tensor_tensor(o_r[:, :], o_ms[:, :], neg_half[:, 0:HEADS], ALU.pow).then_inc(o_pow.sem, 1)
                split_lo(t * 2 + (G_FILL + 2), 1)

            split_lo(G_QK + 2, 0)
            split_lo(G_QK + 2, 1)

            def head(h, last):
                order = stream_order(LAST_TILES, C_START_LAST, C_TILE_LAST) if last else stream_order(4, C_START, C_TILE)

                def stream(kind, t):
                    for what, g, b in order.get((kind, t), []):
                        if what == "split":
                            split_lo(h * 4 + (G_C + 1 + g), b)

                for s in (1, 0):
                    pool.wait_ge(c_ms.sem, c_ms.at(h, 4 - 2 * s))
                    pool.tensor_tensor(r_qk[:, s, :, :].rearrange("p t s -> p (t s)"),
                                       r_ms[:, s, :, :].rearrange("p t s -> p (t s)"),
                                       neg_half[:, 0:2 * NT], ALU.pow).then_inc(c_r.sem, 1)
                stream("start", 0)
                stream("start", 1)
                for t in range(NT):
                    stream("scores", t)
                    pool.wait_ge(c_oms.sem, c_oms.at(h * NT + t))
                    pool.tensor_tensor(at_s[:, 4:5], at_s[:, 3:4], neg_half[:, 0:1], ALU.pow).then_inc(c_opow.sem, 1)
                    stream("output", t)

            with pool.Fori(0, HEADS - 1) as h:
                head(h, False)
            head(HEADS - 1, True)

            with pool.Fori(0, NK) as p:
                for b in range(2):
                    split_lo(p + (PAIR_D + 1), b)
            with pool.Fori(0, NK - 1) as p:
                for b in range(2):
                    split_lo(p + (PAIR_E + 1), b)

        @block.scalar
        def _(act):
            act.sem_inc(proj_out.sem, proj_out.lead)
            act.sem_inc(conv_th.sem, conv_th.lead)
            act.sem_inc(nw_ready.sem, nw_ready.lead)
            act.sem_inc(vnew_ready.sem, vnew_ready.lead)
            act.sem_inc(c_p.sem, c_p.lead)
            act.sem_inc(c_pT_sb.sem, c_pT_sb.lead)
            act.sem_inc(c_vtok.sem, c_vtok.lead)
            act.sem_inc(st_sq.sem, st_sq.lead)
            def split_hi(pair, b):
                act.wait_ge(w_loaded[b].sem, w_loaded[b].at(pair))
                act.wait_ge(w_used.sem, w_used.at(pair * 2 + (b - 2)))
                act.activation(w_hi[:, b, :], w_raw[:, b, :], ACT.Copy).then_inc(w_hi_ready.sem, 1)

            def scale_rows(t):
                act.wait_ge(row_r_ready.sem, row_r_ready.at(t))
                act.wait_ge(xT_ready.sem, xT_ready.at(t - 2))
                act.activation(xs[:, t % 2, :], x_in[:, t, :], ACT.Copy, scale=row_r[:, t:t + 1]).then_inc(xs_ready.sem, 1)

            def round_h(t):
                act.wait_ge(h32_ready.sem, h32_ready.at(t))
                act.activation(h_hi[:, :, t * P:(t + 1) * P], h32[:, t % 2, :, :], ACT.Copy)\
                    .then_inc(h_hi_ready.sem, 1)

            scale_rows(0)
            scale_rows(1)
            for t in range(NT):
                round_h(t)
                if t + 2 < NT:
                    scale_rows(t + 2)
                if t == NT // 2 - 1:
                    for b in range(2):
                        split_hi(0, b)
            act.wait_ge(lam_sums.sem, 2)
            act.activation(lam_s[:, 2:4], lam_s[:, 0:2], ACT.Exp).then_inc(lam_exp.sem, 1)

            def take_bank(dst, g, pair, half, func=ACT.Copy, scale=1.0):
                if half == 0:
                    act.wait_ge(proj_half0.sem, proj_half0.at(g))
                else:
                    act.wait_ge(w_used.sem, w_used.at(pair * 2 + 1))
                n = dst.shape[0]
                settle(act)
                act.activation(dst, PS[0:n, half, :], func, scale=scale).then_inc(proj_out.sem, 1)

            def conv_tile(g):
                split_hi(g + 1, 0)
                act.wait_ge(conv_acc.sem, conv_acc.at(g - 1))
                for half in range(2):
                    at = TAPS - 1 + half * HALF
                    take_bank(pre[:, at:at + HALF], g, g, half)
                split_hi(g + 1, 1)
                act.wait_ge(conv_acc.sem, conv_acc.at(g))
                act.wait_ge(conv_done.sem, conv_done.at(g - 1))
                act.activation(th[:, :], acc[:, :], ACT.Tanh).then_inc(conv_th.sem, 1)

            with act.Fori(0, 12) as g:
                conv_tile(g)
            split_hi(G_AB + 1, 0)
            for half in range(2):
                take_bank(ab_rows[:, half * HALF:(half + 1) * HALF], G_AB, G_AB, half)
            split_hi(G_AB + 1, 1)
            act.wait_ge(ab_loaded.sem, 32)
            act.activation(a_dt[:, 0, :], a_dt[:, 0, :], ACT.Exp).then_inc(a2_act.sem, 1)
            act.wait_ge(a2_dve.sem, A2_ABS)
            act.activation(log1p[:, 2, :, :], log1p[:, 1, :, :], ACT.Exp, scale=-1.0).then_inc(a2_act.sem, 1)
            act.activation(log1p[:, 7, :, :], ab[:, :, HEADS:2 * HEADS], ACT.Exp, scale=-1.0).then_inc(a2_act.sem, 1)

            def z_tile(j):
                split_hi(j + (G_ZB + 1), 0)
                for half in range(2):
                    i = j * 2 + half
                    act.wait_ge(st_T.sem, st_T.at(i))
                    act.wait_ge(st_sum.sem, st_sum.at(i - 2, 1))
                    act.activation(sq8[:, half, :, :].rearrange("p c d -> p (c d)"), banks(2 + 2 * half), ACT.Square)\
                        .then_inc(st_sq.sem, 1)
                    take_bank(zv_flat[:, bass.ds(j * SEQ + half * HALF, HALF)], j + G_ZB, j + G_ZB, half)
                split_hi(j + (G_ZB + 1), 1)
                act.wait_ge(proj_out.sem, proj_out.at(j + G_ZB))
                act.wait_ge(z_silu.sem, j + 1)
                act.wait_ge(conv_done.sem, conv_done.at(11))
                settle(act)
                act.activation(th[:, :], zv_flat[:, bass.ds(j * SEQ, SEQ)], ACT.Tanh, scale=0.5).then_inc(z_th_ready.sem, 1)

            z_tile(0)
            act.wait_ge(a2_dve.sem, A2_DECAY)
            act.activation(log1p[:, 0, :, :], token_scalars[:, :, 0, :], ACT.Exp).then_inc(a2_act.sem, 1)
            act.activation(log1p[:, 1, :, :], log1p[:, 3, :, :], ACT.Exp).then_inc(a2_act.sem, 1)
            with act.Fori(1, HEADS) as j:
                z_tile(j)

            def delta_tiles(t, last):
                act.wait_ge(diff_ready.sem, diff_ready.at(t))
                act.activation(gam[:, :, :], gam[:, :, :], ACT.Exp).then_inc(gam_ready.sem, 1)
                act.wait_ge(o_mm.sem, o_mm.at(t - 1))
                act.activation(qd[:, :, :], bank4(7), ACT.Exp)\
                    .then_inc(eg_ready.sem, 1)
                act.wait_ge(eg_ready.sem, eg_ready.at(t, 1))
                act.wait_ge(sg_ready.sem, sg_ready.at(t - 1))
                act.activation(egl[:, :, :], qd[:, :, CHUNK - 1:P:CHUNK].rearrange("p h c -> p c h"), ACT.Copy)\
                    .then_inc(eg_ready.sem, 1)
                g_v, g_gate = t * 2 + G_FILL, t * 2 + (G_FILL + 1)
                split_hi(g_gate, 0)
                act.wait_ge(x0_T.sem, x0_T.at(t))
                act.activation(X[:, :, :], bank4(2), ACT.Copy).then_inc(x0_ready.sem, 1)
                def take_V(level):
                    act.wait_ge(v_mm.sem, v_mm.at(t, level))
                    act.activation(halves(V[:, :, :], level, 1), halves(bank4(4), level, 1), ACT.Copy).then_inc(v_ready.sem, 1)

                for level in range(1, LEVELS):
                    act.wait_ge(y_mm.sem, y_mm.at(t, level))
                    act.activation(Y_flat, PS[:, 2, 0:HEADS * CHUNK], ACT.Copy).then_inc(y_ready.sem, 1)
                    if level > 1:
                        take_V(level - 1)
                    if level == 1:
                        take_bank(zv_flat[:, bass.ds(t * SEQ + 4 * SEQ, HALF)], g_v, g_v, 0)
                    if level == 3:
                        take_bank(zv_flat[:, bass.ds(t * SEQ + (4 * SEQ + HALF), HALF)], g_v, g_v, 1)
                    if level == 4:
                        split_hi(g_gate, 1)
                take_V(LEVELS - 1)
                act.wait_ge(w_mm.sem, w_mm.at(t))
                act.activation(nwT[:, :, :], bank4(7), ACT.Copy, scale=-1.0).then_inc(nw_ready.sem, 1)
                for c in range(2):
                    rows = slice(c * CHUNK, (c + 1) * CHUNK)
                    act.wait_ge(vnew_mm.sem, vnew_mm.at(t, c + 1))
                    act.activation(v_new[rows, :, :], bank4(5)[rows], ACT.Copy).then_inc(vnew_ready.sem, 1)
                    if c == 0:
                        split_hi(t * 2 + (G_FILL + 2), 0)

                def take_second(half):
                    toks = slice(half * HALF, (half + 1) * HALF)
                    if last:
                        act.wait_ge(tile_in.sem, tile_in.at(NT - 1))
                        take_bank(qk_raw[:, 0, toks], g_gate, g_gate, half)
                    else:
                        act.wait_ge(gate_stored.sem, gate_stored.at(t - 1))
                        take_bank(gate_st[:, toks], g_gate, g_gate, half, ACT.Tanh, 0.5)

                take_second(0)
                act.wait_ge(o_mm.sem, o_mm.at(t))
                for h in range(HEADS):
                    if h == 0:
                        act.wait_ge(on_ready.sem, on_ready.at(t - 1))
                    act.activation(o_sq[:, h, :], bank4(6)[:, h, :], ACT.Square, accum_out=o_ss[:, h:h + 1])\
                        .then_inc(o_ss_ready.sem, 1)
                take_second(1)
                split_hi(t * 2 + (G_FILL + 2), 1)

            with act.Fori(0, NT - 1) as t:
                delta_tiles(t, False)
            delta_tiles(NT - 1, True)

            split_hi(G_QK + 2, 0)
            act.wait_ge(yb_ready.sem, yb_ready.at(NT - 1))
            for half in range(2):
                take_bank(qk_raw[:, 1, half * HALF:(half + 1) * HALF], G_QK + 1, G_QK + 1, half)
            split_hi(G_QK + 2, 1)

            def head(h, last):
                order = stream_order(LAST_TILES, C_START_LAST, C_TILE_LAST) if last else stream_order(4, C_START, C_TILE)

                def stream(kind, t):
                    for what, g, b in order.get((kind, t), []):
                        if what == "split":
                            split_hi(h * 4 + (G_C + 1 + g), b)
                        elif not last and g < 2:
                            take_bank(qk_raw[:, g, b * HALF:(b + 1) * HALF], h * 4 + (G_C + g), h * 4 + (G_C + g), b)
                        else:
                            n = g if last else g - 2
                            if n == 1:
                                act.wait_ge(c_v.sem, c_v.at(h))
                            dst, at = ((gate_b_flat, 0), (zv_flat, 4 * SEQ), (gate_b_flat, SEQ))[n]
                            take_bank(dst[:, bass.ds(h * SEQ + (at + b * HALF), HALF)],
                                      h * 4 + (G_C + g), h * 4 + (G_C + g), b, ACT.Tanh, 0.5)

                act.wait_ge(c_ms.sem, c_ms.at(h - 1))
                for s in (1, 0):
                    act.wait_ge(c_kT1.sem, c_kT1.at(h, 2 - s))
                    act.activation(qk_sq[:, s, :], banks(4 - 2 * s), ACT.Square).then_inc(c_sq.sem, 1)
                act.wait_ge(c_z.sem, h + 1)
                settle(act)
                act.activation(z_th[:, :], zv_flat[:, bass.ds(h * SEQ + 8 * SEQ, SEQ)], ACT.Tanh, scale=0.5)\
                    .then_inc(c_zth.sem, 1)
                stream("start", 0)
                act.wait_ge(c_vT.sem, c_vT.at(h))
                act.wait_ge(c_o.sem, c_o.at(h * NT - 1))
                act.activation(v_tok[:, :, :].rearrange("p t d -> p (t d)"), banks(6), ACT.Copy).then_inc(c_vtok.sem, 1)
                act.wait_ge(c_kT2.sem, c_kT2.at(h))
                act.activation(k_hi[:, :], banks(2), ACT.Copy, scale=gain_qk[:, 0:1]).then_inc(c_kT.sem, 1)

                def exps(t):
                    n = (t + 1) * P
                    st = h * NT + t
                    act.wait_ge(c_mx.sem, c_mx.at(st))
                    act.wait_ge(c_pc.sem, c_pc.at(st - 1))
                    for m in range(2):
                        act.activation(prob[:, m, 0:n], banks(2 + 2 * m)[:, 0:n], ACT.Exp, bias=nm[:, m:m + 1],
                                       scale=r_qk[:, 0, t, m:m + 1], accum_out=l_sum[:, m:m + 1]).then_inc(c_p.sem, 1)

                exps(0)
                stream("start", 1)
                for t in range(NT):
                    st = h * NT + t
                    n = (t + 1) * P
                    act.wait_ge(c_pT.sem, c_pT.at(st))
                    act.wait_ge(c_o.sem, c_o.at(st - 1))
                    act.activation(probT[:, 0:t + 1, :].rearrange("p t d -> p (t d)"), banks(6)[:, 0:n], ACT.Copy)\
                        .then_inc(c_pT_sb.sem, 1)
                    if t + 1 < NT:
                        exps(t + 1)
                    stream("scores", t)
                    act.wait_ge(c_o.sem, c_o.at(st))
                    act.activation(o_junk[:, :], PS[:, 6, 0:P], ACT.Square, accum_out=at_s[:, 0:1]).then_inc(c_oss.sem, 1)
                    stream("output", t)

            act.wait_ge(proj_out.sem, proj_out.at(G_QK + 1))
            with act.Fori(0, HEADS - 1) as h:
                head(h, False)
            head(HEADS - 1, True)

            act.wait_ge(c_y.sem, c_y.at(HEADS * NT - 1))
            for i, half, k in Y_ORDER:
                toks = slice(half * HALF, (half + 1) * HALF)
                act.activation(y_hi[:, 4 * i + k, toks], zv[:, (8, 0)[i] + k, toks], ACT.Copy).then_inc(yhi_ready.sem, 1)

            def round_m(n):
                act.wait_ge(d_gated.sem, d_gated.at(n))
                settle(act)
                act.activation(h_hi_flat[:, bass.ds(n * SEQ, SEQ)], zv_flat[:, bass.ds(n * SEQ, SEQ)], ACT.Copy, scale=0.5)\
                    .then_inc(m_hi_ready.sem, 1)

            split_hi(PAIR_D + 1, 0)
            split_hi(PAIR_D + 1, 1)
            with act.Fori(1, NK) as n:
                split_hi(n + (PAIR_D + 1), 0)
                round_m(n - 1)
                split_hi(n + (PAIR_D + 1), 1)
            act.wait_ge(d_gated.sem, d_gated.at(NK - 1))
            act.activation(h_hi[:, NK - 1, :], m32[:, NK - 1, :], ACT.Copy, scale=0.5).then_inc(m_hi_ready.sem, 1)

            with act.Fori(0, NK - 1) as p:
                for b in range(2):
                    split_hi(p + (PAIR_E + 1), b)

        @block.tensor
        def _(pe):
            pe.sem_inc(w_used.sem, w_used.lead)
            for s_ in (xT_ready, kk_qk, g_b, o_mm, s_mm, on_T, c_kT1, c_pT, c_o, st_T):
                pe.sem_inc(s_.sem, s_.lead)
            pe.wait_ge(consts_ready.sem, N_CONSTS)

            def transpose_x(t):
                pe.wait_ge(xs_ready.sem, xs_ready.at(t))
                pe.wait_ge(h32_ready.sem, h32_ready.at(t - 2))
                for k in range(NK):
                    last = pe.transpose(PS[:, 2 + 2 * (t % 2) + k // 4, (k % 4) * P:(k % 4 + 1) * P],
                                        xs[:, t % 2, k * P:(k + 1) * P], ident[:, :])
                last.then_inc(xT_ready.sem, 1)

            def three_passes(dst, w, lo_w, hi, lo, first, last):
                pe.matmul(dst, w, hi, start=first, stop=False)
                yield None
                pe.matmul(dst, w, lo, start=False, stop=False)
                yield None
                mm = pe.matmul(dst, lo_w, hi, start=False, stop=last)
                yield mm

            def projection(g, pair, first=False):
                order = [(0, 0), (1, 0), (0, 1), (1, 1)] if first else [(0, 0), (0, 1), (1, 0), (1, 1)]
                for kh, half in order:
                    pe.wait_ge(w_lo_ready.sem, w_lo_ready.at(pair * 2 + kh))
                    if first and kh == 0:
                        pe.wait_ge(h_lo_ready.sem, h_lo_ready.at(NT // 2 * (half + 1) - 1))
                    if kh == 0:
                        pe.wait_ge(proj_out.sem, proj_out.at(g - 1, half + 1))
                    for k in range(4):
                        cols = slice(k * P, (k + 1) * P)
                        toks = slice(half * HALF, (half + 1) * HALF)
                        steps = three_passes(PS[:, half, :], w_hi[:, kh, cols], w_lo[:, kh, cols],
                                             h_hi[:, 4 * kh + k, toks], h_lo[:, 4 * kh + k, toks],
                                             kh == 0 and k == 0, kh == 1 and k == 3)
                        for mm in steps:
                            if mm is not None and k == 3:
                                if half == 1:
                                    mm.then_inc(w_used.sem, 1)
                                elif kh == 1:
                                    mm.then_inc(proj_half0.sem, 1)
                            yield

            def projection_pair(g):
                yield from projection(g, g)
                yield from projection(g + 1, g + 1)

            def whole(steps):
                for _ in steps:
                    pass

            def take(steps, n):
                for _ in range(n):
                    next(steps, None)

            first_tile = projection(0, 0, first=True)
            for t in range(NT):
                transpose_x(t)
                if t == 0:
                    pe.wait_ge(vec_loaded.sem, 16 * (len(VEC_ROWS) + 2))
                    pe.transpose(PS[:, 7, 0:60], vec_rows[0:60, :], ident[0:60, 0:60]).then_inc(vec_T.sem, 1)
                if t > NT // 2:
                    take(first_tile, 8)
            whole(first_tile)

            with pe.Fori(1, G_ZB) as g:
                whole(projection(g, g))

            def z_tile(j, between=None):
                fill = projection(j + G_ZB, j + G_ZB)
                take(fill, 12)
                if between is not None:
                    between()
                take(fill, 14)
                for b in range(2):
                    pe.wait_ge(st_ready.sem, st_ready.at(j * 2 + b))
                    pe.wait_ge(st_sq.sem, st_sq.at(j * 2 + (b - 2)))
                    for c in range(8):
                        last = pe.transpose(PS[:, 2 + 2 * b + c // 4, (c % 4) * P:(c % 4 + 1) * P], qk_st[:, b, c, :], ident[:, :])
                    last.then_inc(st_T.sem, 1)
                    take(fill, 6 if b == 0 else 48)

            def ab_transposes():
                pe.wait_ge(proj_out.sem, proj_out.at(G_AB))
                for t in range(NT):
                    last = pe.transpose(PS[:, 6, t * 8:(t + 1) * 8], ab_rows[:, t * P:(t + 1) * P], ident[0:8, 0:8])
                last.then_inc(ab_T.sem, 1)

            def decay_sums():
                pe.wait_ge(a2_dve.sem, A2_G)
                g_all = token_scalars[:, :, 6, :]
                pe.matmul(PS[:, 7, 0:32], tri[:, :], g_all, start=True, stop=True)
                pe.matmul(PS[:, 7, 32:64], block_ones[:, :], g_all, start=True, stop=True, skip_group_check=True)\
                    .then_inc(a2_cum.sem, 1)

            z_tile(0, ab_transposes)
            z_tile(1, decay_sums)
            with pe.Fori(2, HEADS) as j:
                z_tile(j)

            def each_head(fn, signal=None):
                for h in range(HEADS):
                    last = fn(h)
                if signal is not None:
                    last.then_inc(signal.sem, 1)

            def delta_tiles(t, first):
                fill = projection_pair(t * 2 + G_FILL)
                def decay_rows():
                    pe.wait_ge(ts_ready.sem, ts_ready.at(t))
                    each_head(lambda h: pe.matmul(bank4(7)[:, h, :], ts[:, 6, h:h + 1].broadcast_to([P, P]), tri[:, :],
                                                  start=True, stop=True), g_b)

                if not first:
                    decay_rows()
                pe.wait_ge(tile_in.sem, tile_in.at(t, 1))
                each_head(lambda h: pe.transpose(bank4(2)[:, h, :], ct[:, 4 + h, :], ident[:, :]), kv_T)
                each_head(lambda h: pe.matmul(bank4(4)[:, h, :], ct[:, 4 + h, :], ct[:, 4 + h, :], start=True, stop=True), kk_qk)
                each_head(lambda h: pe.matmul(bank4(5)[:, h, :], ct[:, 4 + h, :], ct[:, h, :], start=True, stop=True), kk_qk)
                pe.wait_ge(s_ready.sem, t * 2 + 1)
                pe.wait_ge(tile_in.sem, tile_in.at(t, 2))
                each_head(lambda h: pe.transpose(bank4(3)[:, h, :], vt[:, h, :], ident[:, :]), kv_T)
                if first:
                    decay_rows()
                else:
                    out_transpose(t - 1)
                take(fill, B_FRONT[0])
                pe.wait_ge(yb_ready.sem, yb_ready.at(t - 1))
                each_head(lambda h: pe.matmul(bank4(6)[:, h, :], ts[:, 5, h:h + 1].broadcast_to([P, P]), ident[:, :],
                                              start=True, stop=True), g_b)
                take(fill, B_FRONT[1])
                def transpose_X():
                    each_head(lambda h: pe.transpose(bank4(4)[:, h, :], X[:, h, :], ident[:, :]), v_mm)

                pe.wait_ge(v0_ready.sem, v0_ready.at(t))
                pe.wait_ge(kv_scaled.sem, kv_scaled.at(t, 2))
                each_head(lambda h: pe.transpose(bank4(2)[:, h, :], V[:, h, :], ident[:, :]), x0_T)
                take(fill, 4)
                pe.wait_ge(x0_ready.sem, x0_ready.at(t))
                pe.wait_ge(kv_scaled.sem, kv_scaled.at(t))
                for level in range(1, LEVELS):
                    if level > 1:
                        pe.wait_ge(x_ready.sem, x_ready.at(t, level - 1))
                    pe.wait_ge(um_ready.sem, um_ready.at(t, level + 1))
                    each_head(lambda h: pe.matmul(PS[:, 2, h * CHUNK:(h + 1) * CHUNK], um[:, level % 2, h, :],
                                                  halves(X[:, h:h + 1, :], level, 0), start=True, stop=True), y_mm)
                    if level > 1:
                        transpose_X()
                    take(fill, B_LEVEL[0])
                    pe.wait_ge(y_ready.sem, y_ready.at(t, level))
                    if level > 1:
                        pe.wait_ge(v_ready.sem, v_ready.at(t, level - 1))
                    else:
                        pe.wait_ge(u_ready.sem, u_ready.at(t))
                    each_head(lambda h: pe.matmul(PS[:, 3, h * CHUNK:(h + 1) * CHUNK], V[:, h, :],
                                                  Y_flat[:, h * CHUNK:(h + 1) * CHUNK], start=True, stop=True), x_mm)
                    take(fill, B_LEVEL[1])
                pe.wait_ge(x_ready.sem, x_ready.at(t))
                transpose_X()
                take(fill, B_LEVEL[0])
                pe.wait_ge(v_ready.sem, v_ready.at(t))
                pe.wait_ge(at_ready.sem, at_ready.at(t))
                pe.wait_ge(eg_ready.sem, eg_ready.at(t, 1))
                each_head(lambda h: pe.matmul(bank4(5)[:, h, :], V[:, h, :], v_beta[:, h, :], start=(h == 0), stop=False,
                                              skip_group_check=True), w_mm)
                each_head(lambda h: pe.matmul(bank4(7)[:, h, :], k_exp[:, h, :], V[:, h, :], start=True, stop=True), w_mm)
                take(fill, 4)
                pe.wait_ge(nw_ready.sem, nw_ready.at(t))
                pe.wait_ge(qd_ready.sem, qd_ready.at(t))
                for c in range(2):
                    rows = slice(c * CHUNK, (c + 1) * CHUNK)
                    pe.wait_ge(s_ready.sem, t * 2 + (c + 1))
                    each_head(lambda h: pe.matmul(bank4(5)[rows, h, :], nwT[:, h, rows], S[:, h, :], start=False,
                                                  stop=True, skip_group_check=True), vnew_mm)
                    each_head(lambda h: pe.matmul(bank4(6)[rows, h, :], qd[:, h, rows], S[:, h, :], start=(h == 0),
                                                  stop=False, skip_group_check=True))
                    take(fill, 6)
                    pe.wait_ge(vnew_ready.sem, vnew_ready.at(t, c + 1))
                    each_head(lambda h: pe.matmul(bank4(3)[:, h, :], k_tail[rows, h, :], v_new[rows, h, :],
                                                  start=True, stop=True), s_mm)
                    each_head(lambda h: pe.matmul(bank4(6)[rows, h, :], gm[rows, h, rows], v_new[rows, h, :], start=False,
                                                  stop=True, skip_group_check=True), o_mm)
                    take(fill, 5)
                whole(fill)

            def out_transpose(t):
                pe.wait_ge(on_ready.sem, on_ready.at(t))
                each_head(lambda h: pe.transpose(bank4(6)[:, h, :], on_b[:, h, :], ident[:, :]), on_T)

            pe.wait_ge(st_sq.sem, st_sq.at(NT - 1))
            delta_tiles(0, True)
            with pe.Fori(1, NT) as t:
                delta_tiles(t, False)
            out_transpose(NT - 1)

            whole(projection(G_QK + 1, G_QK + 1))

            def qk_transposes(h):
                pe.wait_ge(c_p.sem, c_p.at(h * NT - 1))
                pe.wait_ge(proj_out.sem, proj_out.at(h * 4 + (G_C - 3)))
                for s in (1, 0):
                    for t in range(NT):
                        mm = pe.transpose(PS[:, 4 - 2 * s + t // 4, (t % 4) * P:(t % 4 + 1) * P],
                                          qk_raw[:, s, t * P:(t + 1) * P], ident[:, :])
                    mm.then_inc(c_kT1.sem, 1)

            def out_transpose(st):
                pe.wait_ge(c_on.sem, c_on.at(st))
                pe.transpose(PS[:, 7, 0:P], on_a[:, :], ident[:, :]).then_inc(c_oT.sem, 1)

            def head(h, last):
                fill, start, tile = next_tiles(h, last), *((C_START_LAST, C_TILE_LAST) if last else (C_START, C_TILE))
                take(fill, start[0])
                pe.wait_ge(c_y.sem, c_y.at(h * NT - 1))
                pe.wait_ge(c_v.sem, c_v.at(h))
                for t in range(NT):
                    mm = pe.transpose(PS[:, 6 + t // 4, (t % 4) * P:(t % 4 + 1) * P], v_st[:, t * P:(t + 1) * P], ident[:, :])
                mm.then_inc(c_vT.sem, 1)
                take(fill, start[1])
                pe.wait_ge(c_ktok.sem, c_ktok.at(h))
                for t in range(NT):
                    mm = pe.transpose(PS[:, 2 + t // 4, (t % 4) * P:(t % 4 + 1) * P],
                                      k_tok[:, t, :, :].rearrange("p s d -> p (s d)"), ident[:, :])
                mm.then_inc(c_kT2.sem, 1)
                take(fill, start[2])
                pe.wait_ge(c_klo.sem, c_klo.at(h))
                pe.wait_ge(c_q.sem, c_q.at(h))
                pe.wait_ge(c_vtok.sem, c_vtok.at(h))

                def scores(t):
                    n = (t + 1) * P
                    for m in range(2):
                        rows = slice(m * SUB, (m + 1) * SUB)
                        pe.wait_ge(c_p.sem, c_p.at(h * NT + t - 1, m + 1))
                        for at in range(0, n, HALF):
                            to = min(at + HALF, n)
                            q_cols = slice(t * P, (t + 1) * P)
                            for q, k, first in ((q_hi, k_hi, True), (q_hi, k_lo, False), (q_lo, k_hi, False)):
                                pe.matmul(PS[:, 2 + 2 * m + at // HALF, 0:to - at], q[rows, q_cols], k[rows, at:to],
                                          start=first, stop=False, skip_group_check=True)
                        end = (n - 1) % HALF + 1
                        pe.matmul(PS[:, 2 + 2 * m + (n - 1) // HALF, end - CHUNK:end], mask_lhs[rows, :],
                                  neg_rows[rows, :], start=False, stop=True, skip_group_check=True)\
                            .then_inc(c_s.sem, 1)

                scores(0)
                for t in range(NT):
                    st = h * NT + t
                    if t == 0:
                        take(fill, tile[0])
                    if t + 1 < NT:
                        scores(t + 1)
                    if t > 0:
                        take(fill, tile[0])
                    if t > 0:
                        out_transpose(st - 1)
                    take(fill, tile[1])
                    pe.wait_ge(c_pc.sem, c_pc.at(st))
                    pe.wait_ge(c_y.sem, c_y.at(st - 1))
                    for k in range(t + 1):
                        mm = pe.transpose(PS[:, 6 + k // 4, (k % 4) * P:(k % 4 + 1) * P], prob_c[:, k * P:(k + 1) * P], ident[:, :])
                    mm.then_inc(c_pT.sem, 1)
                    take(fill, tile[2])
                    pe.wait_ge(c_pT_sb.sem, c_pT_sb.at(st))
                    for k in range(t + 1):
                        mm = pe.matmul(PS[:, 6, 0:P], probT[:, k, :], v_tok[:, k, :], start=(k == 0), stop=(k == t))
                    mm.then_inc(c_o.sem, 1)
                    take(fill, tile[3])
                whole(fill)
                if not last:
                    qk_transposes(h + 1)
                out_transpose(h * NT + (NT - 1))

            def next_tiles(h, last):
                for i in range(LAST_TILES if last else 4):
                    yield from projection(h * 4 + (G_C + i), h * 4 + (G_C + i))

            pe.wait_ge(proj_out.sem, proj_out.at(G_QK + 1))
            qk_transposes(0)
            with pe.Fori(0, HEADS - 1) as h:
                head(h, False)
            head(HEADS - 1, True)

            pe.wait_ge(c_y.sem, c_y.at(HEADS * NT - 1))
            with pe.Fori(0, NK) as n:
                for i in range(2):
                    pe.wait_ge(w_lo_ready.sem, w_lo_ready.at(n * 2 + (PAIR_D * 2 + i)))
                    for half in range(2):
                        pe.wait_ge(d_gated.sem, d_gated.at(n - 1, 1 + half + 2 * i))
                        for k in range(4):
                            pe.wait_ge(ylo_ready.sem, ylo_ready.at(Y_ORDER.index((i, half, k))))
                            cols, toks = slice(k * P, (k + 1) * P), slice(half * HALF, (half + 1) * HALF)
                            for mm in three_passes(PS[:, 2 + 2 * i + half, :], w_hi[:, i, cols], w_lo[:, i, cols],
                                                   y_hi[:, 4 * i + k, toks], y_lo[:, 4 * i + k, toks], k == 0, k == 3):
                                if mm is not None and k == 3:
                                    mm.then_inc((d_up if half == 0 else w_used).sem, 1)

            pe.wait_ge(proj_out.sem, proj_out.at(G_END - 1))
            with pe.Fori(0, 2) as c:
                for k in range(NK):
                    b = k % 2
                    pe.wait_ge(w_lo_ready.sem, w_lo_ready.at(c * NK + (PAIR_E * 2 + k)))
                    pe.wait_ge(m_lo_ready.sem, m_lo_ready.at(k))
                    order = [0, 1, 6, 7, 2, 3, 4, 5] if k == 0 else list(range(NT))
                    for t in order:
                        if k == 0 and t == 2:
                            pe.wait_ge(d_gated.sem, d_gated.at(NK - 1))
                        if k == 0:
                            pe.wait_ge(out_sum.sem, out_sum.at(c - 1, t + 1))
                        toks = slice(t * P, (t + 1) * P)
                        pe.matmul(PS[:, t, :], h_hi[:, k, toks], w_hi[:, b, :], start=(k == 0), stop=False)
                        pe.matmul(PS[:, t, :], h_hi[:, k, toks], w_lo[:, b, :], start=False, stop=False)
                        mm = pe.matmul(PS[:, t, :], h_lo[:, k, toks], w_hi[:, b, :], start=False, stop=(k == NK - 1))
                        if t == order[-1]:
                            mm.then_inc(w_used.sem, 1)
                        elif k == NK - 1:
                            mm.then_inc(out_mm.sem, 1)

        @block.vector
        def _(dve):
            for s_ in (h32_ready, conv_acc, conv_done, z_silu, qd_ready, s_ready, on_ready, yb_ready,
                       c_z, c_ms, st_sum, c_pc, c_on, c_y, d_gated, out_sum):
                dve.sem_inc(s_.sem, s_.lead)
            def channel_parameters():
                dve.wait_ge(vec_T.sem, 1)
                dve.tensor_copy(vec[:, 0:60], PS[:, 7, 0:60]).then_inc(vec_ready.sem, 1)
                dve.wait_ge(vec_ready.sem, 1)
                dve.tensor_scalar(half_conv[:, :, :].rearrange("p c w -> p w c"),
                                  vec[:, 0:48].rearrange("p (w c) -> p w c", c=12), 0.5, None, ALU.mult).then_inc(vec_ready.sem, 1)
                dve.tensor_scalar(gain_b[:, :], vec[:, 56:57], 0.5, None, ALU.mult).then_inc(vec_ready.sem, 1)
                dve.tensor_scalar(gain_a[:, :], vec[:, 57:58], 0.5 * (1.0 - LAMBDA_INIT), None, ALU.mult).then_inc(vec_ready.sem, 1)
                dve.scalar_tensor_tensor(out=gain_qk[:, :], in0=vec[:, 58:59], scalar=SUB ** -0.5, in1=vec[:, 59:60],
                                         op0=ALU.mult, op1=ALU.mult).then_inc(vec_ready.sem, 1)

            def row_mean_square(t):
                dve.wait_ge(x_loaded[t].sem, x_loaded[t].at(0))
                dve.tensor_tensor_reduce(sq_junk[:, t % 2, :], x_in[:, t, :], x_in[:, t, :], 1.0, 0.0, ALU.mult, ALU.add,
                                         row_sq[:, t:t + 1]).then_inc(row_ms_ready.sem, 1)
                dve.wait_ge(row_ms_ready.sem, row_ms_ready.at(t, 1))
                dve.tensor_scalar(row_ms[:, t:t + 1], row_sq[:, t:t + 1], 1.0 / DM, EPS, ALU.mult, ALU.add)\
                    .then_inc(row_ms_ready.sem, 1)

            def h_columns(t):
                dve.wait_ge(xT_ready.sem, xT_ready.at(t))
                dve.wait_ge(h_lo_ready.sem, h_lo_ready.at(t - 2))
                dve.tensor_tensor(h32[:, t % 2, :, :],
                                  PS[:, 2 + 2 * (t % 2):4 + 2 * (t % 2), :].rearrange("p a (k n) -> p (a k) n", n=P),
                                  vec[:, 48:56].unsqueeze(2).broadcast_to([P, NK, P]), ALU.mult).then_inc(h32_ready.sem, 1)

            row_mean_square(0)
            row_mean_square(1)
            channel_parameters()
            for t in range(NT):
                if t + 2 < NT:
                    row_mean_square(t + 2)
                h_columns(t)

            dve.wait_ge(lam_loaded.sem, 16)
            for i in range(2):
                if i:
                    dve.wait_ge(lam_sums.sem, 1)
                dve.tensor_tensor_reduce(lam_junk[:, :], lam_rows[:, 2 * i, :], lam_rows[:, 2 * i + 1, :], 1.0, 0.0,
                                         ALU.mult, ALU.add, lam_s[:, i:i + 1]).then_inc(lam_sums.sem, 1)
            dve.wait_ge(lam_exp.sem, 1)
            dve.tensor_tensor(neg_lam[:, :], lam_s[:, 3:4], lam_s[:, 2:3], ALU.subtract).then_inc(lam_ready.sem, 1)
            dve.wait_ge(lam_ready.sem, 1)
            dve.tensor_scalar(neg_lam[:, :], neg_lam[:, :], -LAMBDA_INIT, None, ALU.add).then_inc(lam_ready.sem, 1)

            dve.wait_ge(h_lo_ready.sem, h_lo_ready.at(NT - 1))
            dve.memset(pre[:, 0:TAPS - 1], 0.0).then_inc(pre_zero.sem, 1)
            dve.wait_ge(pre_zero.sem, 1)
            dve.wait_ge(vec_ready.sem, 5)
            with dve.Fori(0, 12) as c:
                dve.wait_ge(conv_acc.sem, conv_acc.at(c - 1))
                dve.tensor_copy(cw[:, :], half_conv_flat[:, bass.ds(c * TAPS, TAPS)]).then_inc(conv_w_ready.sem, 1)
                dve.wait_ge(proj_out.sem, proj_out.at(c))
                dve.wait_ge(conv_w_ready.sem, conv_w_ready.at(c))
                dve.wait_ge(conv_done.sem, conv_done.at(c - 1))
                for tap in range(TAPS):
                    src = pre[:, tap:tap + SEQ]
                    if tap == 0:
                        ins = dve.tensor_scalar(acc[:, :], src, cw[:, 0:1], None, ALU.mult)
                    else:
                        dve.wait_ge(conv_acc.sem, conv_acc.at(c, tap))
                        ins = dve.scalar_tensor_tensor(out=acc[:, :], in0=src, scalar=cw[:, tap:tap + 1], in1=acc[:, :],
                                                       op0=ALU.mult, op1=ALU.add)
                    ins.then_inc(conv_acc.sem, 1)
                dve.wait_ge(conv_th.sem, conv_th.at(c))
                dve.scalar_tensor_tensor(out=conv_flat[:, bass.ds(c * SEQ, SEQ)], in0=th[:, :], scalar=1.0, in1=acc[:, :],
                                         op0=ALU.add, op1=ALU.mult).then_inc(conv_done.sem, 1)
            def stage(j):
                for b in range(2):
                    i = j * 2 + b
                    dve.wait_ge(st_T.sem, st_T.at(i - 2))
                    dve.tensor_copy(qk_st[:, b, :, :], conv_out[:, 0:8, bass.ds(i * P, P)]).then_inc(st_ready.sem, 1)

            def z_tile(j):
                for b in range(2):
                    i = j * 2 + b
                    dve.wait_ge(st_sq.sem, st_sq.at(i))
                    dve.wait_ge(qk_pow.sem, qk_pow.at(i - 2))
                    dve.reduce_sum(qk_ms[:, b, :], sq8[:, b, :, :], AX.X).then_inc(st_sum.sem, 1)
                    dve.wait_ge(st_sum.sem, st_sum.at(i, 1))
                    dve.tensor_scalar(qk_ms[:, b, :], qk_ms[:, b, :], EPS, None, ALU.add).then_inc(st_sum.sem, 1)
                dve.wait_ge(z_th_ready.sem, z_th_ready.at(j))
                z = zv_flat[:, bass.ds(j * SEQ, SEQ)]
                dve.scalar_tensor_tensor(out=z, in0=th[:, :], scalar=1.0, in1=z, op0=ALU.add, op1=ALU.mult)\
                    .then_inc(z_silu.sem, 1)

            dve.wait_ge(conv_done.sem, conv_done.at(11))
            stage(0)
            dve.memset(S[:, :, :], 0.0).then_inc(s_zero.sem, 1)
            dve.wait_ge(s_zero.sem, 1)
            dve.tensor_copy(ct[:, :, :], conv_out[:, 0:8, 0:P]).then_inc(tile_in.sem, 1)
            dve.tensor_copy(vt[:, :, :], conv_out[:, 8:12, 0:P]).then_inc(tile_in.sem, 1)

            done = [0]

            def link(ins):
                done[0] += 1
                ins.then_inc(a2_dve.sem, 1)
                dve.wait_ge(a2_dve.sem, done[0])

            def bc(v):
                return v.unsqueeze(1).broadcast_to([P, NT, HEADS])

            L = [log1p[:, n, :, :] for n in range(8)]
            T = [token_scalars[:, :, n, :] for n in range(8)]
            dve.wait_ge(ab_T.sem, 1)
            link(dve.tensor_copy(ab[:, :, :].rearrange("p t c -> p (t c)"), PS[:, 6, 0:64]))
            dve.wait_ge(a2_act.sem, 1)
            link(dve.tensor_tensor(L[0], ab[:, :, 0:HEADS], bc(a_dt[:, 1, :]), ALU.add))
            link(dve.tensor_scalar(L[1], L[0], -1.0, None, ALU.mult))
            link(dve.tensor_tensor(L[1], L[1], L[0], ALU.max))
            assert done[0] == A2_ABS
            dve.wait_ge(a2_act.sem, 3)
            link(dve.tensor_scalar(L[3], L[2], 2.0, None, ALU.add))
            link(dve.reciprocal(L[3], L[3]))
            link(dve.tensor_tensor(L[3], L[3], L[2], ALU.mult))
            link(dve.tensor_tensor(L[4], L[3], L[3], ALU.mult))
            link(dve.tensor_scalar(L[5], L[4], 2.0 / 15, 2.0 / 13, ALU.mult, ALU.add))
            for n in (11, 9, 7, 5, 3, 1):
                link(dve.tensor_tensor(L[5], L[5], L[4], ALU.mult))
                link(dve.tensor_scalar(L[5], L[5], 2.0 / n, None, ALU.add))
            link(dve.tensor_tensor(L[5], L[5], L[3], ALU.mult))
            link(dve.scalar_tensor_tensor(out=L[5], in0=L[0], scalar=0.0, in1=L[5], op0=ALU.max, op1=ALU.add))
            link(dve.scalar_tensor_tensor(out=T[6], in0=L[5], scalar=-1.0, in1=bc(a_dt[:, 0, :]), op0=ALU.mult, op1=ALU.mult))
            assert done[0] == A2_G, done[0]
            link(dve.tensor_scalar(L[6], L[7], 1.0, None, ALU.add))
            link(dve.reciprocal(T[2], L[6]))
            z_tile(0)
            stage(1)
            dve.wait_ge(a2_cum.sem, 1)
            link(dve.tensor_copy(T[0], PS[:, 7, 0:32].rearrange("p (t h) -> p t h", h=HEADS)))
            link(dve.tensor_tensor(L[3], PS[:, 7, 32:64].rearrange("p (t h) -> p t h", h=HEADS), T[0], ALU.subtract))
            assert done[0] == A2_DECAY, done[0]
            z_tile(1)
            with dve.Fori(2, HEADS) as j:
                stage(j)
                z_tile(j)
            dve.wait_ge(qk_pow.sem, qk_pow.at(NT - 1))
            rq, rk = qk_r[:, :, 0:HEADS], qk_r[:, :, HEADS:2 * HEADS]
            link(dve.tensor_copy(T[1], rk))
            link(dve.tensor_tensor(T[5], T[2], rk, ALU.mult))
            link(dve.tensor_scalar(T[7], rq, float(HD) ** -0.5, None, ALU.mult))
            dve.wait_ge(a2_act.sem, 5)
            link(dve.tensor_tensor(T[3], T[5], L[0], ALU.mult))
            link(dve.tensor_tensor(T[4], L[1], rk, ALU.mult))

            def wide(col):
                return ts[:, col, :].unsqueeze(2).broadcast_to([P, HEADS, P])

            dve.tensor_copy(ts[:, :, :].rearrange("p a h -> p (a h)"), ts_flat[:, 0:32]).then_inc(ts_ready.sem, 1)

            def write_y(t):
                dve.wait_ge(on_T.sem, on_T.at(t))
                y = zv[:, 0:4, bass.ds(t * P, P)]
                dve.scalar_tensor_tensor(out=y, in0=bank4(6), scalar=gain_b[:, 0:1], in1=y, op0=ALU.mult, op1=ALU.mult)\
                    .then_inc(yb_ready.sem, 1)

            def norm_out(t):
                dve.wait_ge(o_pow.sem, o_pow.at(t))
                dve.tensor_tensor(o_f[:, :], o_r[:, :], o_scale[:, :], ALU.mult).then_inc(on_ready.sem, 1)
                dve.wait_ge(on_ready.sem, on_ready.at(t, 1))
                dve.tensor_tensor(on_b[:, :, :], bank4(6), o_f[:, :].unsqueeze(2).broadcast_to([P, HEADS, P]), ALU.mult)\
                    .then_inc(on_ready.sem, 1)

            def delta_tiles(t, first, last):
                dve.wait_ge(ts_ready.sem, ts_ready.at(t))
                dve.wait_ge(g_b.sem, g_b.at(t, 1))
                dve.wait_ge(o_mm.sem, o_mm.at(t - 1))
                for h in range(HEADS):
                    dve.tensor_scalar(gam[:, h, :], bank4(7)[:, h, :], ts[:, 0, h:h + 1], 0.0, ALU.subtract, ALU.min)\
                        .then_inc(diff_ready.sem, 1)
                if not first:
                    norm_out(t - 1)
                dve.tensor_copy(o_scale[:, :], ts[:, 7, :]).then_inc(o_scale_ready.sem, 1)
                dve.wait_ge(kv_T.sem, kv_T.at(t, 1))
                dve.tensor_tensor(k_tail[:, :, :], bank4(2), wide(4), ALU.mult).then_inc(kv_scaled.sem, 1)
                dve.wait_ge(gam_ready.sem, gam_ready.at(t))
                for h in range(HEADS):
                    dve.scalar_tensor_tensor(out=gm[:, h, :], in0=gam[:, h, :], scalar=ts[:, 1, h:h + 1], in1=tri[:, :],
                                             op0=ALU.mult, op1=ALU.mult).then_inc(gm_ready.sem, 1)
                if not first:
                    write_y(t - 1)
                dve.wait_ge(gm_ready.sem, gm_ready.at(t))
                dve.wait_ge(kk_qk.sem, kk_qk.at(t))
                dve.tensor_tensor(U[:, :, :], bank4(4), gm[:, :, :], ALU.mult).then_inc(u_ready.sem, 1)
                dve.tensor_tensor(gm[:, :, :], bank4(5), gm[:, :, :], ALU.mult).then_inc(at_ready.sem, 1)
                dve.tensor_tensor(k_exp[:, :, :], bank4(2), wide(3), ALU.mult).then_inc(kv_scaled.sem, 1)
                dve.wait_ge(kv_T.sem, kv_T.at(t))
                dve.tensor_tensor(v_beta[:, :, :], bank4(3), wide(2), ALU.mult).then_inc(kv_scaled.sem, 1)
                dve.wait_ge(eg_ready.sem, eg_ready.at(t))
                dve.tensor_tensor(qd[:, :, :], ct[:, 0:4, :], qd[:, :, :], ALU.mult).then_inc(qd_ready.sem, 1)
                dve.wait_ge(u_ready.sem, u_ready.at(t, 1))
                dve.wait_ge(g_b.sem, g_b.at(t))
                dve.tensor_tensor(U[:, :, :], bank4(6), U[:, :, :], ALU.mult).then_inc(u_ready.sem, 1)
                dve.wait_ge(um_ready.sem, um_ready.at(t, 1))
                dve.tensor_tensor(V[:, :, :], ident[:, :].unsqueeze(1).broadcast_to([P, HEADS, P]), um[:, 0, :, :],
                                  ALU.subtract).then_inc(v0_ready.sem, 1)
                for level in range(1, LEVELS):
                    dve.wait_ge(x_mm.sem, x_mm.at(t, level))
                    if level == 1:
                        dve.wait_ge(x0_ready.sem, x0_ready.at(t))
                    else:
                        dve.wait_ge(x_ready.sem, x_ready.at(t, level - 1))
                    X_level = halves(X[:, :, :], level, 0)
                    dve.tensor_tensor(X_level, X_level, blocks(PS[:, 3, 0:HEADS * CHUNK], level), ALU.subtract)\
                        .then_inc(x_ready.sem, 1)
                    if last:
                        continue
                    cols = bass.ds(t * P + P, P)
                    if level == 1:
                        dve.wait_ge(qd_ready.sem, qd_ready.at(t))
                        dve.tensor_copy(ct[:, :, :], conv_out[:, 0:8, cols]).then_inc(tile_in.sem, 1)
                    if level == 2:
                        dve.tensor_copy(vt[:, :, :], conv_out[:, 8:12, cols]).then_inc(tile_in.sem, 1)
                    if level == 3:
                        dve.wait_ge(o_scale_ready.sem, o_scale_ready.at(t))
                        dve.tensor_copy(ts[:, :, :].rearrange("p a h -> p (a h)"), ts_flat[:, bass.ds(t * 32 + 32, 32)])\
                            .then_inc(ts_ready.sem, 1)
                for c in range(2):
                    dve.wait_ge(s_mm.sem, s_mm.at(t, c + 1))
                    dve.wait_ge(sg_ready.sem, sg_ready.at(t, c + 1))
                    dve.tensor_tensor(S[:, :, :], Sg[:, :, :], bank4(3), ALU.add).then_inc(s_ready.sem, 1)
                dve.wait_ge(o_ss_ready.sem, o_ss_ready.at(t))
                dve.tensor_tensor(o_ms[:, :], o_ss[:, :], o_scale[:, :], ALU.mult).then_inc(o_ms_ready.sem, 1)
                dve.wait_ge(o_ms_ready.sem, o_ms_ready.at(t, 1))
                dve.tensor_tensor(o_ms[:, :], o_ms[:, :], o_scale[:, :], ALU.mult).then_inc(o_ms_ready.sem, 1)
                dve.wait_ge(o_ms_ready.sem, o_ms_ready.at(t, 2))
                dve.tensor_scalar(o_ms[:, :], o_ms[:, :], 1.0 / HD, EPS, ALU.mult, ALU.add).then_inc(o_ms_ready.sem, 1)

            delta_tiles(0, True, False)
            with dve.Fori(1, NT - 1) as t:
                delta_tiles(t, False, False)
            delta_tiles(NT - 1, False, True)
            norm_out(NT - 1)
            write_y(NT - 1)

            def head(h):
                dve.wait_ge(proj_out.sem, proj_out.at(h * 4 + (G_C - 4)))
                dve.tensor_copy(q_hi[:, :], qk_raw[:, 0, :]).then_inc(c_q.sem, 1)
                dve.wait_ge(c_q.sem, c_q.at(h, 1))
                dve.tensor_tensor(q_lo[:, :], qk_raw[:, 0, :], q_hi[:, :].bitcast(F32), ALU.subtract).then_inc(c_q.sem, 1)
                dve.tensor_copy(v_st[:, :], zv_flat[:, bass.ds(h * SEQ + 4 * SEQ, SEQ)]).then_inc(c_v.sem, 1)
                for s in (1, 0):
                    dve.wait_ge(c_sq.sem, c_sq.at(h, 2 - s))
                    ms = r_ms[:, s, :, :].rearrange("p t s -> p (t s)")
                    dve.reduce_sum(ms, qk_sq[:, s, :].rearrange("p (n d) -> p n d", d=SUB), AX.X).then_inc(c_ms.sem, 1)
                    dve.wait_ge(c_ms.sem, c_ms.at(h, 3 - 2 * s))
                    dve.tensor_scalar(ms, ms, 1.0 / SUB, EPS, ALU.mult, ALU.add).then_inc(c_ms.sem, 1)
                dve.wait_ge(c_r.sem, c_r.at(h, 1))
                dve.wait_ge(c_kT1.sem, c_kT1.at(h))
                dve.tensor_tensor(k_tok[:, :, :, :], banks(2).rearrange("p (t s d) -> p t s d", s=2, d=SUB),
                                  r_qk[:, 1, :, :].unsqueeze(3).broadcast_to([P, NT, 2, SUB]), ALU.mult)\
                    .then_inc(c_ktok.sem, 1)
                dve.wait_ge(c_zth.sem, c_zth.at(h))
                z = zv_flat[:, bass.ds(h * SEQ + 8 * SEQ, SEQ)]
                dve.scalar_tensor_tensor(out=z, in0=z_th[:, :], scalar=1.0, in1=z, op0=ALU.add, op1=ALU.mult)\
                    .then_inc(c_z.sem, 1)
                dve.wait_ge(c_kT.sem, c_kT.at(h))
                dve.scalar_tensor_tensor(out=k_lo[:, :], in0=banks(2), scalar=gain_qk[:, 0:1], in1=k_hi[:, :].bitcast(F32),
                                         op0=ALU.mult, op1=ALU.subtract).then_inc(c_klo.sem, 1)
                dve.wait_ge(c_r.sem, c_r.at(h))

                def maxima(t):
                    st = h * NT + t
                    n = (t + 1) * P
                    for m in range(2):
                        dve.wait_ge(c_s.sem, c_s.at(st, m + 1))
                        dve.reduce_max(mx[:, m:m + 1], banks(2 + 2 * m)[:, 0:n], AX.X).then_inc(c_mx.sem, 1)
                    dve.wait_ge(c_mx.sem, c_mx.at(st, 2))
                    dve.wait_ge(c_p.sem, c_p.at(st - 1))
                    dve.scalar_tensor_tensor(out=nm[:, :], in0=mx[:, :], scalar=-1.0, in1=r_qk[:, 0, t, :],
                                             op0=ALU.mult, op1=ALU.mult).then_inc(c_mx.sem, 1)

                def combine(t):
                    st = h * NT + t
                    n = (t + 1) * P
                    dve.wait_ge(c_p.sem, c_p.at(st))
                    dve.wait_ge(c_on.sem, c_on.at(st - 1))
                    dve.reciprocal(at_s[:, 5:7], l_sum[:, :]).then_inc(c_coef.sem, 1)
                    dve.wait_ge(c_coef.sem, c_coef.at(st, 1))
                    dve.tensor_tensor(at_s[:, 7:8], at_s[:, 6:7], l_sum[:, 0:1], ALU.mult).then_inc(c_coef.sem, 1)
                    dve.tensor_tensor(at_s[:, 9:10], at_s[:, 5:6], at_s[:, 5:6], ALU.mult).then_inc(c_coef.sem, 1)
                    dve.wait_ge(c_coef.sem, c_coef.at(st, 2))
                    dve.tensor_tensor(at_s[:, 8:9], at_s[:, 7:8], neg_lam[:, :], ALU.mult).then_inc(c_coef.sem, 1)
                    dve.wait_ge(c_coef.sem, c_coef.at(st, 4))
                    dve.wait_ge(c_pT.sem, c_pT.at(st - 1))
                    dve.scalar_tensor_tensor(out=prob_c[:, 0:n], in0=prob[:, 1, 0:n], scalar=at_s[:, 8:9],
                                             in1=prob[:, 0, 0:n], op0=ALU.mult, op1=ALU.add).then_inc(c_pc.sem, 1)

                maxima(0)
                combine(0)
                for t in range(NT):
                    st = h * NT + t
                    if t + 1 < NT:
                        maxima(t + 1)
                    dve.wait_ge(c_oss.sem, c_oss.at(st))
                    dve.tensor_scalar(at_s[:, 2:3], at_s[:, 0:1], at_s[:, 9:10], 1.0 / HD, ALU.mult, ALU.mult)\
                        .then_inc(c_oms.sem, 1)
                    dve.wait_ge(c_oms.sem, c_oms.at(st, 1))
                    dve.tensor_scalar(at_s[:, 3:4], at_s[:, 2:3], EPS, None, ALU.add).then_inc(c_oms.sem, 1)
                    dve.wait_ge(c_opow.sem, c_opow.at(st))
                    dve.tensor_scalar(on_a[:, :], PS[:, 6, 0:P], at_s[:, 4:5], at_s[:, 5:6], ALU.mult, ALU.mult)\
                        .then_inc(c_on.sem, 1)
                    if t + 1 < NT:
                        combine(t + 1)
                    dve.wait_ge(c_oT.sem, c_oT.at(st))
                    y = zv_flat[:, bass.ds(h * SEQ + (8 * SEQ + t * P), P)]
                    if t == 0:
                        dve.wait_ge(c_z.sem, c_z.at(h))
                    dve.scalar_tensor_tensor(out=y, in0=PS[:, 7, 0:P], scalar=gain_a[:, 0:1], in1=y,
                                             op0=ALU.mult, op1=ALU.mult).then_inc(c_y.sem, 1)

            dve.wait_ge(proj_out.sem, proj_out.at(G_QK + 1))
            with dve.Fori(0, HEADS - 1) as h:
                head(h)
            head(HEADS - 1)

            for n, (i, half, k) in enumerate(Y_ORDER):
                toks = slice(half * HALF, (half + 1) * HALF)
                dve.wait_ge(yhi_ready.sem, yhi_ready.at(n))
                dve.tensor_tensor(y_lo[:, 4 * i + k, toks], zv[:, (8, 0)[i] + k, toks],
                                  y_hi[:, 4 * i + k, toks].bitcast(F32), ALU.subtract).then_inc(ylo_ready.sem, 1)
            dve.wait_ge(ylo_ready.sem, ylo_ready.at(len(Y_ORDER) - 1))

            def m_rest(n):
                dve.wait_ge(m_hi_ready.sem, m_hi_ready.at(n))
                m_hi = h_hi_flat[:, bass.ds(n * SEQ, SEQ)].bitcast(F32)
                dve.scalar_tensor_tensor(out=h_lo_flat[:, bass.ds(n * SEQ, SEQ)], in0=zv_flat[:, bass.ds(n * SEQ, SEQ)],
                                         scalar=0.5, in1=m_hi, op0=ALU.mult, op1=ALU.subtract).then_inc(m_lo_ready.sem, 1)

            def merge(n, gates_b):
                gates_a = gate_a[:, n % 2, :] if n < NK - 1 else gate_b[:, HEADS, :]
                g_a = [gates_a[:, half * HALF:(half + 1) * HALF] for half in range(2)]
                g_b = [gates_b[:, n * SEQ + half * HALF:n * SEQ + (half + 1) * HALF] for half in range(2)]
                for i, g in enumerate((g_a, g_b)):
                    if i == 0 and n < NK - 1:
                        dve.wait_ge(gate_loaded[n % 2].sem, gate_loaded[n % 2].at(n // 2))
                    for half in range(2):
                        if half == 0:
                            dve.wait_ge(d_up.sem, d_up.at(n, i + 1))
                        else:
                            dve.wait_ge(w_used.sem, w_used.at(n * 2 + (PAIR_D * 2 + i)))
                        dve.scalar_tensor_tensor(out=g[half], in0=g[half], scalar=1.0, in1=PS[:, 2 + 2 * i + half, :],
                                                 op0=ALU.add, op1=ALU.mult).then_inc(d_gated.sem, 1)
                    if i == 0 and n > 0:
                        m_rest(n - 1)
                for half in range(2):
                    dve.wait_ge(d_gated.sem, d_gated.at(n, 3 + half))
                    dve.tensor_tensor(zv_flat[:, bass.ds(n * SEQ + half * HALF, HALF)], g_a[half], g_b[half], ALU.add)\
                        .then_inc(d_gated.sem, 1)

            for n in range(NK):
                merge(n, gate_b_flat if n < HEADS else zv_flat)
            m_rest(NK - 1)

            dve.wait_ge(x_res_loaded.sem, x_res_loaded.at(0))
            for c in range(2):
                for t in range(NT):
                    if t < NT - 1:
                        dve.wait_ge(out_mm.sem, out_mm.at(c, t + 1))
                    else:
                        dve.wait_ge(w_used.sem, w_used.at(PAIR_E * 2 + (c + 1) * NK - 1))
                    cols = slice(c * HALF, (c + 1) * HALF)
                    dve.tensor_tensor(out_sb[:, t, cols], PS[:, t, :], x_res[:, t, cols], ALU.add).then_inc(out_sum.sem, 1)


_INS = ["x", "norm_w", "w_in", "da_q_gain", "da_k_gain", "da_lambda", "da_out_gain", "gdn_conv_w",
        "gdn_a_log", "gdn_dt_bias", "gdn_norm_w", "w_up_da", "w_up_gdn", "w_out"]


def kernel(**inputs):
    import numpy as _np
    import concourse.bacc as _bacc
    from concourse.bass_utils import run_bass_kernel_spmd as _run

    nc = _bacc.Bacc("TRN2", target_bir_lowering=False, num_devices=1, dynamic_dma_scratch_size=1024)
    arrays, args = {}, []
    for name in _INS:
        a = _np.ascontiguousarray(inputs[name])
        arrays[f"in_{name}"] = a
        args.append(nc.dram_tensor(f"in_{name}", a.shape, F32, kind="ExternalInput").ap())
    args.append(nc.dram_tensor("out_0", (1, SEQ, DM), F32, kind="ExternalOutput").ap())
    hybrid_block(nc, *args)
    r = _run(nc, [arrays], core_ids=[0])
    return r.results[0]["out_0"]
```
